# Optimizing a Trainium2 kernel written in Bass

```python
import jax, jax.numpy as jnp
from jax import lax
import numpy as np

D_MODEL = 1024
BATCH = 1
SEQ = 2048
DEPTH = 1
DEC_BATCH = 8
DEC_SEQ = 16
PAST_LEN = 2048

CHUNK = 64
HEAD_DIM = 64
A_HEADS = 6
A_KV_HEADS = 2
A_GROUP = A_HEADS // A_KV_HEADS
WINDOW = 128
W_CHUNKS = WINDOW // CHUNK
B_HEADS = 6
B_CONV = 4
C_HEADS = 4
SB_BLOCK = 128
A_Q = A_HEADS * HEAD_DIM
A_KV = A_KV_HEADS * HEAD_DIM
B_W = B_HEADS * HEAD_DIM
C_W = C_HEADS * HEAD_DIM
MIX_W = A_Q + B_W + C_W
B_CONV_CH = 3 * B_W
IN_SIZES = (A_Q, A_KV, A_KV, B_CONV_CH, B_W, B_HEADS, B_HEADS, C_W, C_W, C_W)
IN_W = sum(IN_SIZES)
IN_SPLITS = tuple(sum(IN_SIZES[:i + 1]) for i in range(len(IN_SIZES) - 1))
D_FF = 2816
FFN_CONV = 3
N_MOD = 6
ALPHA = (2 * DEPTH) ** 0.25
BETA_INIT = (8 * DEPTH) ** -0.25
LN_EPS = 1e-5
RMS_EPS = 1e-6
NEG = -1e30
F32 = jnp.float32

kernel_name = "hybrid_streaming_encoder_step"

def layer_norm(x, g, b):
    xf = x.astype(F32)
    mu = jnp.mean(xf, -1, keepdims=True)
    var = jnp.mean(jnp.square(xf - mu), -1, keepdims=True)
    return ((xf - mu) * lax.rsqrt(var + LN_EPS) * g.astype(F32) + b.astype(F32)).astype(x.dtype)

def l2norm(x):
    x = x.astype(F32)
    return x * lax.rsqrt(jnp.sum(x * x, -1, keepdims=True) + RMS_EPS)

def causal_dwconv(x, buf, w):
    k, t = w.shape[0], x.shape[1]
    xp = jnp.concatenate([buf.astype(x.dtype), x], axis=1)
    y = xp[:, 0:t] * w[0]
    for i in range(1, k):
        y = y + xp[:, i:i + t] * w[i]
    return y, xp[:, t:]

def sink_softmax(s, sinks):
    sk = jnp.broadcast_to(sinks.astype(F32).reshape(A_KV_HEADS, A_GROUP)[:, :, None, None],
                          s.shape[:-1] + (1,))
    return jax.nn.softmax(jnp.concatenate([s, sk], -1), axis=-1)[..., :-1]

def swa_prompt(q, k, v, sinks):
    b, t = q.shape[:2]
    nc = t // CHUNK
    nk = (W_CHUNKS + 1) * CHUNK
    qc = q.reshape(b, nc, CHUNK, A_KV_HEADS, A_GROUP, HEAD_DIM)
    padw = ((0, 0), (W_CHUNKS * CHUNK, 0), (0, 0), (0, 0))
    kp = jnp.pad(k, padw).reshape(b, nc + W_CHUNKS, CHUNK, A_KV_HEADS, HEAD_DIM)
    vp = jnp.pad(v, padw).reshape(b, nc + W_CHUNKS, CHUNK, A_KV_HEADS, HEAD_DIM)
    kb = jnp.concatenate([kp[:, i:i + nc] for i in range(W_CHUNKS + 1)], axis=2)
    vb = jnp.concatenate([vp[:, i:i + nc] for i in range(W_CHUNKS + 1)], axis=2)
    s = jnp.einsum("bnqhgd,bnkhd->bnhgqk", qc, kb).astype(F32) * HEAD_DIM ** -0.5
    key_chunk = jnp.arange(nc)[:, None] - W_CHUNKS + jnp.arange(nk)[None, :] // CHUNK
    s = jnp.where((key_chunk >= 0)[None, :, None, None, None, :], s, NEG)
    p = sink_softmax(s, sinks)
    o = jnp.einsum("bnhgqk,bnkhd->bnqhgd", p.astype(v.dtype), vb)
    return o.reshape(b, t, A_Q)

def swa_cached(q, k, v, sinks):
    b, t = q.shape[:2]
    s = jnp.einsum("bqhgd,bkhd->bhgqk", q, k).astype(F32) * HEAD_DIM ** -0.5
    p = sink_softmax(s, sinks)
    o = jnp.einsum("bhgqk,bkhd->bqhgd", p.astype(v.dtype), v)
    return o.reshape(b, t, A_Q)

def gated_delta(q, k, v, g, beta, s0, chunk):
    b, t, h, dk = q.shape
    dv = v.shape[-1]
    n = t // chunk

    def to_chunks(a):
        return a.reshape(b, n, chunk, h, -1).transpose(1, 0, 3, 2, 4)

    q = to_chunks(q) * dk ** -0.5
    k = to_chunks(k)
    v = to_chunks(v)
    g = to_chunks(g[..., None])[..., 0]
    beta = to_chunks(beta[..., None])
    gc = jnp.cumsum(g, axis=-1)
    idx = jnp.arange(chunk)
    causal = idx[:, None] >= idx[None, :]
    strict = idx[:, None] > idx[None, :]
    decay = jnp.exp(jnp.where(causal, gc[..., :, None] - gc[..., None, :], NEG))
    kb = k * beta
    lower = jnp.where(strict, jnp.einsum("...id,...jd->...ij", kb, k) * decay, 0.0)
    rhs = jnp.concatenate([v * beta, kb * jnp.exp(gc)[..., None]], -1)
    sol = lax.linalg.triangular_solve(lower + jnp.eye(chunk, dtype=F32), rhs,
                                      left_side=True, lower=True, unit_diagonal=True)
    u, w = sol[..., :dv], sol[..., dv:]
    intra = jnp.where(causal, jnp.einsum("...id,...jd->...ij", q, k) * decay, 0.0)

    def step(s, inp):
        q_i, k_i, u_i, w_i, gc_i, a_i = inp
        v_new = u_i - jnp.einsum("bhck,bhkv->bhcv", w_i, s)
        o = (jnp.einsum("bhck,bhkv->bhcv", q_i * jnp.exp(gc_i)[..., None], s)
             + jnp.einsum("bhcs,bhsv->bhcv", a_i, v_new))
        g_last = gc_i[..., -1:]
        s = (s * jnp.exp(g_last)[..., None]
             + jnp.einsum("bhck,bhcv->bhkv", k_i * jnp.exp(g_last - gc_i)[..., None], v_new))
        return s, o

    s, o = lax.scan(step, s0.astype(F32), (q, k, u, w, gc, intra))
    return o.transpose(1, 0, 3, 2, 4).reshape(b, t, h, dv), s

def sb_attend(q, k, v, qpos):
    z = jnp.einsum("bqhd,bkhd->bhqk", q, k).astype(F32) * HEAD_DIM ** -0.5
    mask = jnp.arange(k.shape[1])[None, :] < qpos[:, None]
    log_keep = jnp.where(mask, -jax.nn.softplus(z), 0.0)
    after = lax.cumsum(log_keep, axis=3, reverse=True) - log_keep
    a = jnp.where(mask, jnp.exp(jax.nn.log_sigmoid(z) + after), 0.0)
    return jnp.einsum("bhqk,bkhd->bqhd", a.astype(v.dtype), v)

def sb_prompt(q, k, v):
    b, t = q.shape[:2]
    nb = t // SB_BLOCK
    qb = q.reshape(b, nb, SB_BLOCK, C_HEADS, HEAD_DIM).swapaxes(0, 1)

    def block(args):
        qi, i = args
        return sb_attend(qi, k, v, i * SB_BLOCK + jnp.arange(SB_BLOCK))

    o = lax.map(block, (qb, jnp.arange(nb)))
    return o.swapaxes(0, 1).reshape(b, t, C_W)

def trunk_layer(x, c, lp, st, prompt):
    (w_ada, b_ada, w_in, a_sinks, b_conv_w, b_a_log, b_dt_bias, b_norm_w, w_out,
     ln1_g, ln1_b, w_gate, w_up, ffn_conv_w, w_down, ln2_g, ln2_b) = lp
    a_k_c, a_v_c, b_conv_c, b_ssm_c, c_k_c, c_v_c, ffn_c = st
    b, t, _ = x.shape
    mod = (jax.nn.silu(c) @ w_ada + b_ada)[:, None, :]
    sh_m, sc_m, g_m, sh_f, sc_f, g_f = jnp.split(mod, N_MOD, axis=-1)
    h = x * (1 + sc_m) + sh_m
    proj = h @ w_in
    aq, ak, av, bqkv, bz, bb, ba, cq, ck, cv = jnp.split(proj, IN_SPLITS, axis=-1)

    aq = aq.reshape(b, t, A_KV_HEADS, A_GROUP, HEAD_DIM)
    ak = ak.reshape(b, t, A_KV_HEADS, HEAD_DIM)
    av = av.reshape(b, t, A_KV_HEADS, HEAD_DIM)
    if prompt:
        oa = swa_prompt(aq, ak, av, a_sinks)
        new_ak, new_av = ak[:, -WINDOW:], av[:, -WINDOW:]
    else:
        kk = jnp.concatenate([a_k_c.astype(ak.dtype), ak], axis=1)
        vv = jnp.concatenate([a_v_c.astype(av.dtype), av], axis=1)
        oa = swa_cached(aq, kk, vv, a_sinks)
        new_ak, new_av = kk[:, -WINDOW:], vv[:, -WINDOW:]

    bconv, new_bconv = causal_dwconv(bqkv, b_conv_c, b_conv_w)
    bq, bk, bv = jnp.split(jax.nn.silu(bconv), 3, axis=-1)
    bq = l2norm(bq.reshape(b, t, B_HEADS, HEAD_DIM))
    bk = l2norm(bk.reshape(b, t, B_HEADS, HEAD_DIM))
    bv = bv.reshape(b, t, B_HEADS, HEAD_DIM).astype(F32)
    beta = jax.nn.sigmoid(bb.astype(F32))
    gdec = -jnp.exp(b_a_log.astype(F32)) * jax.nn.softplus(ba.astype(F32) + b_dt_bias.astype(F32))
    ob, new_ssm = gated_delta(bq, bk, bv, gdec, beta, b_ssm_c, CHUNK if prompt else t)
    ob = ob * lax.rsqrt(jnp.mean(ob * ob, -1, keepdims=True) + RMS_EPS) * b_norm_w.astype(F32)
    ob = (ob * jax.nn.silu(bz.reshape(b, t, B_HEADS, HEAD_DIM).astype(F32))).reshape(b, t, B_W)

    cq = cq.reshape(b, t, C_HEADS, HEAD_DIM)
    ck = ck.reshape(b, t, C_HEADS, HEAD_DIM)
    cv = cv.reshape(b, t, C_HEADS, HEAD_DIM)
    if prompt:
        oc = sb_prompt(cq, ck, cv)
    else:
        kk = jnp.concatenate([c_k_c.astype(ck.dtype), ck], axis=1)
        vv = jnp.concatenate([c_v_c.astype(cv.dtype), cv], axis=1)
        oc = sb_attend(cq, kk, vv, c_k_c.shape[1] + jnp.arange(t)).reshape(b, t, C_W)

    mix = jnp.concatenate([oa, ob.astype(x.dtype), oc], axis=-1) @ w_out
    x = layer_norm(ALPHA * x + g_m * mix, ln1_g, ln1_b)

    h = x * (1 + sc_f) + sh_f
    gconv, new_fbuf = causal_dwconv(h @ w_gate, ffn_c, ffn_conv_w)
    f = (jax.nn.silu(gconv) * (h @ w_up)) @ w_down
    x = layer_norm(ALPHA * x + g_f * f, ln2_g, ln2_b)
    return x, (new_ak, new_av, new_bconv, new_ssm, ck, cv, new_fbuf)

def setup_inputs(seed: int = 0) -> dict:
    key = jax.random.key(seed)
    ks = jax.random.split(key, 32)
    nrm = jax.random.normal
    gate_off = jnp.repeat(jnp.array([0.0, 0.0, 1.0, 0.0, 0.0, 1.0], F32), D_MODEL)
    dt = jnp.exp(jax.random.uniform(ks[17], (DEPTH, B_HEADS), F32, np.log(1e-3), np.log(1e-1)))
    return {
        "x_prompt": nrm(ks[0], (BATCH, SEQ, D_MODEL), F32),
        "x_sample": nrm(ks[1], (DEC_BATCH, DEC_SEQ, D_MODEL), F32),
        "c_prompt": nrm(ks[2], (BATCH, D_MODEL), F32),
        "c_sample": nrm(ks[3], (DEC_BATCH, D_MODEL), F32),
        "cache_a_k": nrm(ks[4], (DEPTH, DEC_BATCH, WINDOW, A_KV_HEADS, HEAD_DIM), F32),
        "cache_a_v": nrm(ks[5], (DEPTH, DEC_BATCH, WINDOW, A_KV_HEADS, HEAD_DIM), F32),
        "state_b_conv": nrm(ks[6], (DEPTH, DEC_BATCH, B_CONV - 1, B_CONV_CH), F32),
        "state_b_ssm": 0.1 * nrm(ks[7], (DEPTH, DEC_BATCH, B_HEADS, HEAD_DIM, HEAD_DIM), F32),
        "cache_c_k": nrm(ks[8], (DEPTH, DEC_BATCH, PAST_LEN, C_HEADS, HEAD_DIM), F32),
        "cache_c_v": nrm(ks[9], (DEPTH, DEC_BATCH, PAST_LEN, C_HEADS, HEAD_DIM), F32),
        "state_ffn_conv": nrm(ks[10], (DEPTH, DEC_BATCH, FFN_CONV - 1, D_FF), F32),
        "ln_in_g": 1.0 + 0.02 * nrm(ks[11], (D_MODEL,), F32),
        "ln_in_b": 0.02 * nrm(ks[12], (D_MODEL,), F32),
        "w_ada": 0.5 * D_MODEL ** -0.5 * nrm(ks[13], (DEPTH, D_MODEL, N_MOD * D_MODEL), F32),
        "b_ada": gate_off + 0.02 * nrm(ks[14], (DEPTH, N_MOD * D_MODEL), F32),
        "w_in": D_MODEL ** -0.5 * nrm(ks[15], (DEPTH, D_MODEL, IN_W), F32),
        "a_sinks": 0.5 * nrm(ks[16], (DEPTH, A_HEADS), F32),
        "b_conv_w": 0.5 * nrm(ks[18], (DEPTH, B_CONV, B_CONV_CH), F32),
        "b_a_log": jnp.log(jax.random.uniform(ks[19], (DEPTH, B_HEADS), F32, 1.0, 16.0)),
        "b_dt_bias": dt + jnp.log(-jnp.expm1(-dt)),
        "b_norm_w": 1.0 + 0.02 * nrm(ks[20], (DEPTH, HEAD_DIM), F32),
        "w_out": BETA_INIT * MIX_W ** -0.5 * nrm(ks[21], (DEPTH, MIX_W, D_MODEL), F32),
        "ln1_g": 1.0 + 0.02 * nrm(ks[22], (DEPTH, D_MODEL), F32),
        "ln1_b": 0.02 * nrm(ks[23], (DEPTH, D_MODEL), F32),
        "w_gate": D_MODEL ** -0.5 * nrm(ks[24], (DEPTH, D_MODEL, D_FF), F32),
        "w_up": D_MODEL ** -0.5 * nrm(ks[25], (DEPTH, D_MODEL, D_FF), F32),
        "ffn_conv_w": 0.5 * nrm(ks[26], (DEPTH, FFN_CONV, D_FF), F32),
        "w_down": BETA_INIT * D_FF ** -0.5 * nrm(ks[27], (DEPTH, D_FF, D_MODEL), F32),
        "ln2_g": 1.0 + 0.02 * nrm(ks[28], (DEPTH, D_MODEL), F32),
        "ln2_b": 0.02 * nrm(ks[29], (DEPTH, D_MODEL), F32),
    }

def reference(x_prompt, x_sample, c_prompt, c_sample, cache_a_k, cache_a_v, state_b_conv,
              state_b_ssm, cache_c_k, cache_c_v, state_ffn_conv, ln_in_g, ln_in_b, w_ada, b_ada,
              w_in, a_sinks, b_conv_w, b_a_log, b_dt_bias, b_norm_w, w_out, ln1_g, ln1_b,
              w_gate, w_up, ffn_conv_w, w_down, ln2_g, ln2_b):
    xp = layer_norm(x_prompt, ln_in_g, ln_in_b)
    xs = layer_norm(x_sample, ln_in_g, ln_in_b)
    bp = x_prompt.shape[0]
    p_lists = [[] for _ in range(7)]
    s_lists = [[] for _ in range(7)]
    for l in range(DEPTH):
        lp = (w_ada[l], b_ada[l], w_in[l], a_sinks[l], b_conv_w[l], b_a_log[l], b_dt_bias[l],
              b_norm_w[l], w_out[l], ln1_g[l], ln1_b[l], w_gate[l], w_up[l], ffn_conv_w[l],
              w_down[l], ln2_g[l], ln2_b[l])
        st_p0 = (None, None,
                 jnp.zeros((bp, B_CONV - 1, B_CONV_CH), x_prompt.dtype),
                 jnp.zeros((bp, B_HEADS, HEAD_DIM, HEAD_DIM), F32),
                 None, None,
                 jnp.zeros((bp, FFN_CONV - 1, D_FF), x_prompt.dtype))
        st_s0 = (cache_a_k[l], cache_a_v[l], state_b_conv[l], state_b_ssm[l],
                 cache_c_k[l], cache_c_v[l], state_ffn_conv[l])
        xp, st_p = trunk_layer(xp, c_prompt, lp, st_p0, True)
        xs, st_s = trunk_layer(xs, c_sample, lp, st_s0, False)
        for j in range(7):
            p_lists[j].append(st_p[j])
            s_lists[j].append(st_s[j])
    p_a_k, p_a_v, p_b_conv, p_b_ssm, p_c_k, p_c_v, p_ffn_conv = [jnp.stack(a) for a in p_lists]
    s_a_k, s_a_v, s_b_conv, s_b_ssm, s_c_k, s_c_v, s_ffn_conv = [jnp.stack(a) for a in s_lists]
    return (xp, xs, p_a_k, p_a_v, p_b_conv, p_b_ssm, p_c_k, p_c_v, p_ffn_conv,
            s_a_k, s_a_v, s_b_conv, s_b_ssm, s_c_k, s_c_v, s_ffn_conv)


_drawn_inputs = setup_inputs


def setup_inputs(seed=0):
    import zlib

    import numpy as np

    out = dict(_drawn_inputs(seed))
    spreads = {}
    factors = {'a_sinks': 130.241,
     'b_norm_w': 23.233,
     'ln1_g': 2.702,
     'ln1_b': 2.766,
     'ln2_g': 20.248,
     'ln2_b': 21.797,
     'cache_c_k': 17.045,
     'cache_c_v': 3.182}
    for name, (base, spread) in spreads.items():
        noise = np.random.default_rng([zlib.crc32(name.encode()), seed]).standard_normal(out[name].shape)
        drawn = base * np.exp(spread * noise) if base else spread * noise
        out[name] = __import__('jax').numpy.asarray(drawn.astype(out[name].dtype))
    for name, factor in factors.items():
        out[name] = (out[name] * factor).astype(out[name].dtype)
    return out
```

```python
from contextlib import ExitStack

import numpy as np
import concourse.bass as bass
from concourse import mybir

F32 = mybir.dt.float32
ALU = mybir.AluOpType
ACT = mybir.ActivationFunctionType
AX = mybir.AxisListType

P = 128
D = 1024
DC = D // P
SEQ = 2048
DEC_B, DEC_T = 8, 16
TOKENS = SEQ + DEC_B * DEC_T
PAST = 2048
HD = 64
A_HEADS, A_KV, A_GROUP = 6, 2, 3
WINDOW = 128
B_HEADS, B_CONV = 6, 4
C_HEADS = 4
B_W = B_HEADS * HD
CONV_CH = 3 * B_W
IN_W = 2956
D_FF = 2816
FC = D_FF // P
FFN_CONV = 3
N_COND = 1 + DEC_B
ALPHA = 2.0 ** 0.25
LN_EPS = 1e-5
RMS_EPS = 1e-6
NEG = -1e30
LOG_EXP_TABLES = "natural_log_exp_and_others"

GROUP = 512
GT = GROUP // P
GROUPS = SEQ // GROUP

AQ0, AK0, AV0 = 0, 384, 512
BQKV0, BZ0 = 640, 1792
CQ0, CK0 = 2188, 2444
ZBA_W = B_W + 2 * B_HEADS
CONV_CHUNKS = CONV_CH // P
QKT_AQ, QKT_AK, QKT_CQ, QKT_CK, QKT_N = 0, 3, 4, 6, 8


def signals(nc, ctx, stage, names):
    handles = {n: nc.alloc_semaphore(f"{stage}_{n}") for n in names.split()}
    ctx.callback(nc.clear_and_free_semaphores, list(handles.values()))
    return handles


def signal(nc, ctx, stage, name):
    return signals(nc, ctx, stage, name)[name]


def row_broadcast(row, n=P):
    return row.to_broadcast([n, row.shape[1]])


def build_constants(nc, K):
    with ExitStack() as ctx:
        ctx.callback(nc.all_engine_barrier)
        s = signals(nc, ctx, "constants", "filled")
        block = ctx.enter_context(nc.Block())

        @block.gpsimd
        def _(pool):
            pool.memset(K["ident"][:], 0.0)
            pool.memset(K["ones"][:], 1.0)
            pool.memset(K["sel"][:], 1.0).then_inc(s["filled"], 1)
            pool.wait_ge(s["filled"], 1)
            pool.affine_select(out=K["ident"][:], in_=K["ident"][:], compare_op=ALU.not_equal, fill=1.0,
                               base=0, pattern=[[-1, P]], channel_multiplier=1)
            pool.affine_select(out=K["later"][:], in_=K["ones"][:], compare_op=ALU.is_gt, fill=0.0,
                               base=0, pattern=[[-1, P]], channel_multiplier=1)
            pool.affine_select(out=K["upto"][:], in_=K["ones"][:], compare_op=ALU.is_ge, fill=0.0,
                               base=0, pattern=[[1, P]], channel_multiplier=-1)
            pool.affine_select(out=K["before"][:], in_=K["ones"][:], compare_op=ALU.is_gt, fill=0.0,
                               base=0, pattern=[[1, P]], channel_multiplier=-1)
            pool.affine_select(out=K["sel"][:, 0, :], in_=K["sel"][:, 0, :], compare_op=ALU.is_equal,
                               fill=0.0, base=0, pattern=[[0, P]], channel_multiplier=1)
            pool.affine_select(out=K["sel"][:, 1, :], in_=K["sel"][:, 1, :], compare_op=ALU.is_equal,
                               fill=0.0, base=-1, pattern=[[-1, DEC_B], [0, DEC_T]],
                               channel_multiplier=1)


def stage_modulation(nc, K, IN):
    COLS, RING = 512, 3
    n_cols = 6 * D // COLS
    with ExitStack() as ctx:
        ctx.callback(nc.all_engine_barrier)
        sb = lambda name, shape: ctx.enter_context(nc.sbuf_tensor(name, shape, F32))
        ps = lambda name, shape: ctx.enter_context(nc.psum_tensor(name, shape, F32))
        cond = sb("cond", [N_COND, D])
        cond_silu = sb("cond_silu", [N_COND, D])
        condT = sb("condT", [P, DC, N_COND])
        bias = sb("bias", [N_COND, 6 * D])
        mod = sb("mod", [N_COND, 6 * D])
        w = sb("w_ada_ring", [P, RING, DC, COLS])
        ps_T = ps("ps_condT", [P, 512])
        ps_mod = ps("ps_mod", [P, RING, COLS])
        ps_gate = ps("ps_gate", [P, 2, COLS])
        s = signals(nc, ctx, "modulation", "cond_loaded bias_loaded silu_done condT_done condT_copied "
                             "mod_done mod_copied modT_done gate_done gate_copied w_free")
        w_loaded = [signal(nc, ctx, "modulation", f"w_ada_loaded{r}") for r in range(RING)]
        w_ada = IN["w_ada"][0].rearrange("(k p) n -> p k n", p=P)
        block = ctx.enter_context(nc.Block())

        @block.sync
        def _(sp):
            sp.dma_start(cond[0:1, :], IN["c_prompt"]).then_inc(s["cond_loaded"], 16)
            sp.dma_start(cond[1:N_COND, :], IN["c_sample"]).then_inc(s["cond_loaded"], 16)
            sp.dma_start(bias[:], IN["b_ada"].to_broadcast([N_COND, 6 * D])).then_inc(s["bias_loaded"], 16)
            with sp.Fori(0, n_cols // RING) as i:
                for r in range(RING):
                    sp.wait_ge(s["w_free"], i * RING + r + 1)
                    sp.dma_start(w[:, r], w_ada[:, :, bass.ds(i * (RING * COLS) + r * COLS, COLS)]
                                 ).then_inc(w_loaded[r], 16)

        @block.scalar
        def _(act):
            act.wait_ge(s["cond_loaded"], 32)
            act.activation(cond_silu[:], cond[:], ACT.Silu).then_inc(s["silu_done"], 1)

        @block.tensor
        def _(pe):
            pe.sem_inc(s["w_free"], RING)
            pe.wait_ge(s["silu_done"], 1)
            for k in range(DC):
                last = pe.transpose(ps_T[:, k * N_COND:(k + 1) * N_COND], cond_silu[:, k * P:(k + 1) * P],
                                    K["ident"][0:N_COND, 0:N_COND])
            last.then_inc(s["condT_done"], 1)
            pe.wait_ge(s["condT_copied"], 1)
            with pe.Fori(0, n_cols // RING) as i:
                for r in range(RING):
                    pe.wait_ge(w_loaded[r], i * 16 + 16)
                    pe.wait_ge(s["mod_copied"], i * RING + r + 1)
                    for k in range(DC):
                        last = pe.matmul(ps_mod[0:N_COND, r], condT[:, k, :], w[:, r, k, :],
                                         start=(k == 0), stop=(k == DC - 1))
                    last.then_inc(s["w_free"], 1)
            pe.wait_ge(s["mod_copied"], RING + n_cols)
            for j, kind in enumerate((0, 1, 3, 4)):
                for k in range(DC):
                    o = (j * DC + k) * N_COND
                    last = pe.transpose(ps_T[:, o:o + N_COND], mod[:, kind * D + k * P:kind * D + (k + 1) * P],
                                        K["ident"][0:N_COND, 0:N_COND])
            last.then_inc(s["modT_done"], 1)
            n = 0
            for g, kind in enumerate((2, 5)):
                for who in range(2):
                    for half in range(2):
                        if n >= 2:
                            pe.wait_ge(s["gate_copied"], n - 1)
                        c0 = kind * D + half * COLS
                        pe.matmul(ps_gate[:, n % 2], K["sel"][:, who, :], mod[:, c0:c0 + COLS],
                                  start=True, stop=True).then_inc(s["gate_done"], 1)
                        n += 1

        @block.vector
        def _(dve):
            dve.sem_inc(s["mod_copied"], RING)
            dve.wait_ge(s["condT_done"], 1)
            dve.tensor_copy(condT[:].rearrange("p k c -> p (k c)"), ps_T[:, 0:DC * N_COND]
                            ).then_inc(s["condT_copied"], 1)
            dve.wait_ge(s["bias_loaded"], 16)
            with dve.Fori(0, n_cols // RING) as i:
                for r in range(RING):
                    dve.wait_ge(s["w_free"], i * RING + (RING + r + 1))
                    at = bass.ds(i * (RING * COLS) + r * COLS, COLS)
                    dve.tensor_tensor(mod[:, at], ps_mod[0:N_COND, r], bias[:, at], ALU.add
                                      ).then_inc(s["mod_copied"], 1)
            dve.wait_ge(s["modT_done"], 1)
            for j in range(4):
                src = ps_T[:, j * DC * N_COND:(j + 1) * DC * N_COND]
                dst = K["modT"][:, j].rearrange("p k c -> p (k c)")
                dve.tensor_scalar(dst, src, float(j % 2), None, ALU.add)
            n = 0
            for g in range(2):
                for who in range(2):
                    for half in range(2):
                        dve.wait_ge(s["gate_done"], n + 1)
                        dve.tensor_copy(K["gates"][:, g, who, half * COLS:(half + 1) * COLS],
                                        ps_gate[:, n % 2]).then_inc(s["gate_copied"], 1)
                        n += 1


def layer_norm_stats(dve, x, stats, mean_var, tiles):
    for t in range(tiles):
        for h in range(2):
            dve.bn_stats(stats[:, t, h, :], x[:, t, h * 512:(h + 1) * 512])
    dve.drain()
    for t in range(tiles):
        last = dve.bn_aggr(mean_var[:, t, :], stats[:, t].rearrange("p a b -> p (a b)"))
    return last


def stage_projection(nc, K, IN, OUT, S):
    with ExitStack() as ctx:
        ctx.callback(nc.all_engine_barrier)
        sb = lambda name, shape: ctx.enter_context(nc.sbuf_tensor(name, shape, F32))
        ps = lambda name, shape: ctx.enter_context(nc.psum_tensor(name, shape, F32))
        HIST = B_CONV - 1
        HR = DEC_B * HIST
        NL = HIST + HR
        w = sb("w_in_all", [P, DC, IN_W])
        x = sb("x_group", [P, GT, D])
        hT = sb("hT", [P, DC, GROUP])
        ln_g, ln_b = sb("ln_in_g_rows", [P, D]), sb("ln_in_b_rows", [P, D])
        stats = sb("ln_stats", [P, GT, 2, 6])
        mean_var = sb("ln_mean_var", [P, GT, 2])
        rstd = sb("ln_rstd", [P, GT])
        minus_half, eps = sb("minus_half", [P, GT]), sb("ln_eps", [P, GT])
        raw = sb("conv_raw", [P, CONV_CHUNKS, HIST + GROUP])
        conv = sb("conv_sum", [P, 3, GROUP])
        conv_act = sb("conv_act", [P, 3, GROUP])
        taps = sb("conv_taps", [P, CONV_CHUNKS, B_CONV])
        histT = sb("conv_hist", [P, CONV_CHUNKS, HR])
        rows = sb("conv_rows", [P, CONV_CH])
        last_raw = sb("conv_last_raw", [P, CONV_CHUNKS, NL])
        qkT = sb("qkT_stage", [P, 2, GROUP])
        tok = sb("token_stage", [P, 2, 3, 512])
        ps_T = ps("ps_hT", [P, DC, P])
        ps_F = ps("ps_feature", [P, 3, GROUP])
        ps_K = ps("ps_token", [P, 3, 512])
        s = signals(nc, ctx, "projection", "w_loaded rows_loaded lnrow_loaded x_loaded x_stored stats_done rstd_done "
                             "x0_ready hT_ps hT_ready feat_done feat_copied hist_ready conv_done "
                             "conv_act_done taps_ps tok_done tok_z tok_v last_kept last_ps last_ready "
                             "rows_stored")
        conv_stored = [signal(nc, ctx, "projection", f"conv_stored{b}") for b in range(3)]
        qkT_stored = [signal(nc, ctx, "projection", f"qkT_stored{b}") for b in range(2)]
        tok_stored = [signal(nc, ctx, "projection", f"tok_stored{b}") for b in range(2)]

        def w_cols(f, k):
            if f < CONV_CHUNKS:
                return w[:, k, BQKV0 + f * P:BQKV0 + (f + 1) * P]
            q = f - CONV_CHUNKS
            if q < QKT_AK:
                return w[:, k, q * P:(q + 1) * P]
            c0 = {QKT_AK: AK0, QKT_CQ: CQ0, QKT_CQ + 1: CQ0 + P, QKT_CK: CK0, QKT_CK + 1: CK0 + P}[q]
            return w[:, k, c0:c0 + P]

        TOK_PIECES = ((AV0, P), (BZ0, ZBA_W), (CK0, 512))
        TOK_DMAS = 5
        FEATS = CONV_CHUNKS + QKT_N

        def groups(engine, body):
            with engine.Fori(0, GROUPS - 1) as i:
                body(i, GT, GROUP, "prompt")
            body(GROUPS - 1, GT, GROUP, "sample")
            body(GROUPS, 1, P, None)

        block = ctx.enter_context(nc.Block())

        @block.gpsimd
        def _(pool):
            pool.memset(minus_half[:], -0.5)
            pool.memset(eps[:], LN_EPS)
            pool.drain()
            pool.dma_start(ln_g[:], row_broadcast(IN["ln_in_g"])).then_inc(s["lnrow_loaded"], 16)
            pool.dma_start(ln_b[:], row_broadcast(IN["ln_in_b"])).then_inc(s["lnrow_loaded"], 16)
            pool.dma_start(rows[0:B_CONV, :], IN["b_conv_w"][0]).then_inc(s["rows_loaded"], 16)
            pool.dma_start(rows[32:32 + HR, :], IN["state_b_conv"].rearrange("l b t c -> (l b t) c")
                           ).then_inc(s["rows_loaded"], 16)

            def load(it, tiles, sample):
                src = (IN["x_sample"].rearrange("b t d -> (b t) d") if sample
                       else IN["x_prompt"][0, bass.ds(it * GROUP, GROUP), :])
                pool.dma_start(x[:, 0:tiles, :], src.rearrange("(t p) d -> p t d", p=P)
                               ).then_inc(s["x_loaded"], 16)

            def body(it, tiles, tokens, follows):
                pool.wait_ge(s["stats_done"], it + 1)
                pool.tensor_tensor(rstd[:, 0:tiles], mean_var[:, 0:tiles, 1], eps[:, 0:tiles], ALU.add)
                pool.drain()
                pool.tensor_tensor(rstd[:, 0:tiles], rstd[:, 0:tiles], minus_half[:, 0:tiles], ALU.pow
                                   ).then_inc(s["rstd_done"], 1)
                pool.wait_ge(s["x0_ready"], it + 1)
                pool.dma_start(S["x0"][bass.ds(it * GROUP, tokens), :].rearrange("(t p) d -> p t d", p=P),
                               x[:, 0:tiles, :]).then_inc(s["x_stored"], 16)
                pool.wait_ge(s["x_stored"], it * 16 + 16)
                if follows is not None:
                    pool.wait_ge(s["hT_ps"], (it + 1) * GT)
                    load(it + 1, GT if follows == "prompt" else 1, follows == "sample")

            load(0, GT, False)
            groups(pool, body)

        @block.tensor
        def _(pe):
            pe.wait_ge(s["rows_loaded"], 32)
            for f in range(CONV_CHUNKS):
                pe.transpose(ps_F[:, 0, f * B_CONV:(f + 1) * B_CONV], rows[0:B_CONV, f * P:(f + 1) * P],
                             K["ident"][0:B_CONV, 0:B_CONV])
                last = pe.transpose(ps_F[:, 1, f * HR:(f + 1) * HR], rows[32:32 + HR, f * P:(f + 1) * P],
                                    K["ident"][32:32 + HR, 32:32 + HR])
            last.then_inc(s["taps_ps"], 1)
            pe.wait_ge(s["hist_ready"], 1)
            pe.wait_ge(s["w_loaded"], 16 * 3 * DC)

            def body(it, tiles, tokens, follows):
                tile0, chunk0 = it * GT, it * FEATS
                pe.wait_ge(s["x0_ready"], it + 1)
                for t in range(tiles):
                    pe.wait_ge(s["hT_ready"], tile0 + t + 1)
                    for k in range(DC):
                        last = pe.transpose(ps_T[:, k, :], x[:, t, k * P:(k + 1) * P], K["ident"][:])
                    last.then_inc(s["hT_ps"], 1)
                pe.wait_ge(s["hT_ready"], tile0 + (tiles + 1))
                for f in range(FEATS):
                    pe.wait_ge(s["feat_copied"], chunk0 + (f + 2 if f < 2 else f + 1))
                    for k in range(DC):
                        last = pe.matmul(ps_F[:, f % 3, 0:tokens], w_cols(f, k), hT[:, k, 0:tokens],
                                         start=(k == 0), stop=(k == DC - 1))
                    last.then_inc(s["feat_done"], 1)
                for t in range(tiles):
                    for j, (c0, width) in enumerate(TOK_PIECES):
                        n2 = (tile0 + t) * 2
                        pe.wait_ge(s["tok_z"] if j == 1 else s["tok_v"], n2 + (1 if j == 0 else 2))
                        for k in range(DC):
                            last = pe.matmul(ps_K[:, j, 0:width], hT[:, k, t * P:(t + 1) * P],
                                             w[:, k, c0:c0 + width], start=(k == 0), stop=(k == DC - 1))
                        last.then_inc(s["tok_done"], 1)
            groups(pe, body)
            pe.wait_ge(s["last_kept"], 2)
            pe.wait_ge(s["feat_copied"], 3 + FEATS * (GROUPS + 1))
            for f in range(CONV_CHUNKS):
                last = pe.transpose(ps_F[0:NL, f // 4, (f % 4) * P:(f % 4 + 1) * P], last_raw[:, f, :],
                                    K["ident"][:])
            last.then_inc(s["last_ps"], 1)

        @block.scalar
        def _(act):
            act.sem_inc(s["hT_ready"], 1)
            act.sem_inc(s["feat_copied"], 3)
            act.sem_inc(s["tok_z"], 2)
            act.sem_inc(s["conv_act_done"], 3)

            def body(it, tiles, tokens, follows):
                tile0, chunk0, conv0 = it * GT, it * FEATS, it * CONV_CHUNKS
                if follows is not None:
                    for t in range(tiles):
                        act.wait_ge(s["hT_ps"], tile0 + (t + 1))
                        for k in range(DC):
                            last = act.activation(hT[:, k, t * P:(t + 1) * P], ps_T[:, k, :], ACT.Identity,
                                                  bias=K["modT"][:, 0, k, 0:1], scale=K["modT"][:, 1, k, 0:1])
                        last.then_inc(s["hT_ready"], 1)

                def silu_conv(f):
                    act.wait_ge(s["conv_done"], conv0 + (f + 1))
                    act.wait_ge(conv_stored[f % 3], it * 48 + (f // 3 * 16 + 16))
                    act.activation(conv_act[:, f % 3, 0:tokens], conv[:, f % 3, 0:tokens], ACT.Silu
                                   ).then_inc(s["conv_act_done"], 1)

                for f in range(FEATS):
                    act.wait_ge(s["feat_done"], chunk0 + (f + 1))
                    src = ps_F[:, f % 3, 0:tokens]
                    if f < CONV_CHUNKS:
                        if f == 0:
                            act.wait_ge(s["hist_ready"], it + 1)
                        dst = raw[:, f, HIST:]
                        if follows is None:
                            dst = raw[:, f, 0:DEC_B * (HIST + DEC_T)].rearrange(
                                "p (b t) -> p b t", b=DEC_B)[:, :, HIST:]
                            src = src.rearrange("p (b t) -> p b t", b=DEC_B)
                    else:
                        q = f - CONV_CHUNKS
                        act.wait_ge(qkT_stored[q % 2], it * (QKT_N // 2 * 16) + (q // 2 * 16 + 16))
                        dst = qkT[:, q % 2, 0:tokens]
                    act.activation(dst, src, ACT.Identity).then_inc(s["feat_copied"], 1)
                    if 1 <= f <= CONV_CHUNKS:
                        silu_conv(f - 1)
                for t in range(tiles):
                    act.wait_ge(s["tok_done"], (tile0 + t) * 3 + 2)
                    act.wait_ge(tok_stored[t % 2], it * (GT // 2 * TOK_DMAS * 16)
                                + ((t // 2 + 1) * TOK_DMAS * 16))
                    act.activation(tok[:, t % 2, 1, 0:B_W], ps_K[:, 1, 0:B_W], ACT.Silu
                                   ).then_inc(s["tok_z"], 1)
                    act.activation(tok[:, t % 2, 1, B_W:ZBA_W], ps_K[:, 1, B_W:ZBA_W], ACT.Identity
                                   ).then_inc(s["tok_z"], 1)
            groups(act, body)

        @block.sync
        def _(sp):
            for b in range(3):
                sp.sem_inc(conv_stored[b], 16)
            for b in range(2):
                sp.sem_inc(qkT_stored[b], 16)
                sp.sem_inc(tok_stored[b], TOK_DMAS * 16)
            for k in range(DC):
                w_rows = IN["w_in"][0, k * P:(k + 1) * P, :]
                sp.dma_start(w[:, k, AK0:], w_rows[:, AK0:]).then_inc(s["w_loaded"], 16)
                for v in range(A_KV):
                    sp.dma_start(w[:, k, 0:AK0].rearrange("p (g v d) -> p g v d", g=A_GROUP, v=A_KV)[:, :, v],
                                 w_rows[:, 0:AK0].rearrange("p (v g d) -> p v g d", v=A_KV, g=A_GROUP)[:, v]
                                 ).then_inc(s["w_loaded"], 16)

            def body(it, tiles, tokens, follows):
                tile0, chunk0, conv0 = it * GT, it * FEATS, it * CONV_CHUNKS
                at = bass.ds(it * GROUP, tokens)
                for f in range(CONV_CHUNKS):
                    sp.wait_ge(s["conv_act_done"], conv0 + (f + 4))
                    sp.dma_start(S["convT"][f, :, at], conv_act[:, f % 3, 0:tokens]
                                 ).then_inc(conv_stored[f % 3], 16)
                for q in range(QKT_N):
                    sp.wait_ge(s["feat_copied"], chunk0 + (CONV_CHUNKS + q + 4))
                    sp.dma_start(S["qkT"][q, :, at], qkT[:, q % 2, 0:tokens]).then_inc(qkT_stored[q % 2], 16)
                for t in range(tiles):
                    n = tile0 + t
                    rows_at = bass.ds(it * GROUP + t * P, P)
                    stage = tok[:, t % 2]
                    sp.wait_ge(s["tok_v"], n * 2 + 4)
                    sp.wait_ge(s["tok_z"], n * 2 + 4)
                    who = "s" if follows is None else "p"
                    ck, cv = (OUT[f"{who}_c_{a}"].rearrange("l b t h d -> (l b t) (h d)") for a in "kv")
                    out_at = slice(0, P) if follows is None else rows_at
                    for dst, src in ((S["av"][rows_at, :], stage[:, 0, 0:P]),
                                     (S["zba"][rows_at, :], stage[:, 1, 0:ZBA_W]),
                                     (S["cv"][rows_at, :], stage[:, 2, 256:512]),
                                     (ck[out_at, :], stage[:, 2, 0:256]),
                                     (cv[out_at, :], stage[:, 2, 256:512])):
                        sp.dma_start(dst, src).then_inc(tok_stored[t % 2], 16)
            groups(sp, body)
            sp.wait_ge(s["last_ready"], 1)
            sp.dma_start(OUT["p_b_conv"].rearrange("l b t c -> (l b t) c"), rows[0:HIST, :]
                         ).then_inc(s["rows_stored"], 16)
            sp.dma_start(OUT["s_b_conv"].rearrange("l b t c -> (l b t) c"), rows[HIST:NL, :]
                         ).then_inc(s["rows_stored"], 16)
            sp.wait_ge(s["rows_stored"], 32)
            for b in range(3):
                sp.wait_ge(conv_stored[b], 16 * (3 * (GROUPS + 1) + 1))
            for b in range(2):
                sp.wait_ge(qkT_stored[b], 16 * (QKT_N // 2 * (GROUPS + 1) + 1))
                sp.wait_ge(tok_stored[b], 16 * TOK_DMAS * (GROUPS * GT // 2 + (2 if b == 0 else 1)))

        @block.vector
        def _(dve):
            dve.sem_inc(s["tok_v"], 2)
            dve.wait_ge(s["taps_ps"], 1)
            dve.tensor_copy(taps[:].rearrange("p f t -> p (f t)"), ps_F[:, 0, 0:CONV_CHUNKS * B_CONV])
            dve.tensor_copy(histT[:].rearrange("p f t -> p (f t)"), ps_F[:, 1, 0:CONV_CHUNKS * HR])
            dve.memset(raw[:, :, 0:HIST], 0.0).then_inc(s["hist_ready"], 1)
            dve.wait_ge(s["lnrow_loaded"], 32)

            def norm(it, tiles):
                dve.wait_ge(s["x_loaded"], it * 16 + 16)
                layer_norm_stats(dve, x, stats, mean_var, tiles).then_inc(s["stats_done"], 1)
                dve.wait_ge(s["rstd_done"], it + 1)
                for t in range(tiles):
                    dve.tensor_scalar(x[:, t], x[:, t], mean_var[:, t, 0:1], rstd[:, t:t + 1],
                                      ALU.subtract, ALU.mult)
                dve.drain()
                for t in range(tiles):
                    dve.tensor_tensor(x[:, t], x[:, t], ln_g[:], ALU.mult)
                dve.drain()
                for t in range(tiles):
                    last = dve.tensor_tensor(x[:, t], x[:, t], ln_b[:], ALU.add)
                last.then_inc(s["x0_ready"], 1)

            def body(it, tiles, tokens, follows):
                tile0, chunk0, conv0 = it * GT, it * FEATS, it * CONV_CHUNKS
                if follows is None:
                    dve.wait_ge(s["hT_ps"], tile0 + 1)
                    for k in range(DC):
                        h = hT[:, k, 0:P].rearrange("p (b t) -> p b t", b=DEC_B)
                        by_seq = lambda j: K["modT"][:, j, k, 1:].unsqueeze(2).to_broadcast([P, DEC_B, DEC_T])
                        dve.tensor_tensor(h, ps_T[:, k, :].rearrange("p (b t) -> p b t", b=DEC_B),
                                          by_seq(1), ALU.mult)
                    dve.drain()
                    for k in range(DC):
                        h = hT[:, k, 0:P].rearrange("p (b t) -> p b t", b=DEC_B)
                        by_seq = lambda j: K["modT"][:, j, k, 1:].unsqueeze(2).to_broadcast([P, DEC_B, DEC_T])
                        last = dve.tensor_tensor(h, h, by_seq(0), ALU.add)
                    last.then_inc(s["hT_ready"], 1)
                for f in range(CONV_CHUNKS):
                    dve.wait_ge(s["feat_copied"], chunk0 + (f + 4))
                    dve.wait_ge(s["conv_act_done"], conv0 + (f + 1))
                    for i in range(B_CONV):
                        if follows is None:
                            src = raw[:, f, 0:DEC_B * (HIST + DEC_T)].rearrange(
                                "p (b t) -> p b t", b=DEC_B)[:, :, i:i + DEC_T]
                            dst = conv[:, f % 3, 0:tokens].rearrange("p (b t) -> p b t", b=DEC_B)
                        else:
                            src, dst = raw[:, f, i:i + GROUP], conv[:, f % 3, :]
                        if i == 0:
                            last = dve.tensor_scalar(dst, src, taps[:, f, 0:1], None, ALU.mult)
                        else:
                            dve.drain()
                            last = dve.scalar_tensor_tensor(dst, src, taps[:, f, i:i + 1], dst,
                                                            ALU.mult, ALU.add)
                    last.then_inc(s["conv_done"], 1)
                if follows == "prompt":
                    dve.tensor_copy(raw[:, :, 0:HIST], raw[:, :, GROUP:GROUP + HIST]
                                    ).then_inc(s["hist_ready"], 1)
                elif follows == "sample":
                    dve.tensor_copy(last_raw[:, :, 0:HIST], raw[:, :, GROUP:GROUP + HIST]
                                    ).then_inc(s["last_kept"], 1)
                    dve.drain()
                    for b in range(DEC_B):
                        o = b * (HIST + DEC_T)
                        last = dve.tensor_copy(raw[:, :, o:o + HIST], histT[:, :, b * HIST:(b + 1) * HIST])
                    last.then_inc(s["hist_ready"], 1)
                else:
                    for b in range(DEC_B):
                        o = (b + 1) * (HIST + DEC_T)
                        last = dve.tensor_copy(last_raw[:, :, HIST + b * HIST:HIST + (b + 1) * HIST],
                                               raw[:, :, o - HIST:o])
                    last.then_inc(s["last_kept"], 1)
                if follows is not None:
                    norm(it + 1, GT if follows == "prompt" else 1)
                for t in range(tiles):
                    dve.wait_ge(tok_stored[t % 2], it * (GT // 2 * TOK_DMAS * 16)
                                + ((t // 2 + 1) * TOK_DMAS * 16))
                    for j in (0, 2):
                        dve.wait_ge(s["tok_done"], (tile0 + t) * 3 + (j + 1))
                        width = TOK_PIECES[j][1]
                        dve.tensor_copy(tok[:, t % 2, j, 0:width], ps_K[:, j, 0:width]
                                        ).then_inc(s["tok_v"], 1)

            norm(0, GT)
            groups(dve, body)
            dve.wait_ge(s["last_ps"], 1)
            last = dve.tensor_copy(rows[0:NL, 0:1024], ps_F[0:NL, 0:2, :].rearrange("p a b -> p (a b)"))
            last = dve.tensor_copy(rows[0:NL, 1024:CONV_CH], ps_F[0:NL, 2, 0:CONV_CH - 1024])
            last.then_inc(s["last_ready"], 1)


def rstd_of(pool, rstd, variance, eps, minus_half):
    pool.tensor_tensor(rstd, variance, eps, ALU.add)
    pool.drain()
    return pool.tensor_tensor(rstd, rstd, minus_half, ALU.pow)


def stage_mix_out(nc, K, IN, S):
    TILES = TOKENS // P
    with ExitStack() as ctx:
        ctx.callback(nc.all_engine_barrier)
        sb = lambda name, shape: ctx.enter_context(nc.sbuf_tensor(name, shape, F32))
        ps = lambda name, shape: ctx.enter_context(nc.psum_tensor(name, shape, F32))
        w = sb("w_out_all", [P, DC, D])
        mixT = sb("mixT_tile", [P, 2, DC, P])
        x = sb("x_tile", [P, 2, D])
        y = sb("gated_mix", [P, 2, D])
        hT = sb("h2T_tile", [P, 2, DC, P])
        ln_g, ln_b = sb("ln1_g_rows", [P, D]), sb("ln1_b_rows", [P, D])
        stats = sb("ln1_stats", [P, 1, 2, 6])
        mean_var = sb("ln1_mean_var", [P, 1, 2])
        rstd = sb("ln1_rstd", [P, 1])
        minus_half, eps = sb("ln1_minus_half", [P, 1]), sb("ln1_eps", [P, 1])
        ps_O = ps("ps_mix_out", [P, 2, D])
        ps_T = ps("ps_h2T", [P, 2, DC, P])
        s = signals(nc, ctx, "mix_out", "w_loaded lnrow_loaded out_done out_copied stats_done rstd_done x1_ready "
                             "hT_ps hT_ready hT_sample_ready x_free x1_stored")
        mix_loaded, x_loaded, hT_stored = (
            [signal(nc, ctx, "mix_out", f"{n}{b}") for b in range(2)]
            for n in ("mix_loaded", "x0_loaded", "h2T_stored"))
        block = ctx.enter_context(nc.Block())

        def tiles(engine, body):
            with engine.Fori(0, TILES // 2) as i:
                for b in range(2):
                    body(i * 2 + b, b, i, False)
            body(TILES - 1, 0, TILES // 2, True)

        @block.sync
        def _(sp):
            for k in range(DC):
                if k < A_GROUP:
                    for v in range(A_KV):
                        r0 = (v * A_GROUP + k) * HD
                        sp.dma_start(w[v * HD:(v + 1) * HD, k, :], IN["w_out"][0, r0:r0 + HD, :]
                                     ).then_inc(s["w_loaded"], 16)
                else:
                    sp.dma_start(w[:, k, :], IN["w_out"][0, k * P:(k + 1) * P, :]).then_inc(s["w_loaded"], 16)

            def body(n, slot, uses, sample):
                at = bass.ds(n * P, P)
                sp.wait_ge(s["out_done"], n + 1)
                sp.dma_start(mixT[:, slot], S["mixT"][:, :, at].rearrange("k p t -> p k t")
                             ).then_inc(mix_loaded[slot], 16)
                sp.wait_ge(s["hT_ps"], n + 1)
                sp.wait_ge(s["x_free"], n + 1)
                sp.dma_start(x[:, slot], S["x0"][at, :]).then_inc(x_loaded[slot], 16)
            tiles(sp, body)

        @block.gpsimd
        def _(pool):
            pool.memset(minus_half[:], -0.5)
            pool.memset(eps[:], LN_EPS)
            pool.drain()
            pool.dma_start(ln_g[:], row_broadcast(IN["ln1_g"])).then_inc(s["lnrow_loaded"], 16)
            pool.dma_start(ln_b[:], row_broadcast(IN["ln1_b"])).then_inc(s["lnrow_loaded"], 16)

            def body(n, slot, uses, sample):
                pool.wait_ge(s["stats_done"], n + 1)
                rstd_of(pool, rstd[:], mean_var[:, :, 1], eps[:], minus_half[:]).then_inc(s["rstd_done"], 1)
                pool.wait_ge(s["x1_ready"], n + 1)
                pool.dma_start(S["x1"][bass.ds(n * P, P), :], x[:, slot]).then_inc(s["x1_stored"], 16)
                pool.wait_ge(s["x1_stored"], n * 16 + 16)
                pool.sem_inc(s["x_free"], 1)
            pool.sem_inc(s["x_free"], 2)
            tiles(pool, body)

        @block.tensor
        def _(pe):
            pe.sem_inc(s["out_done"], 2)
            pe.sem_inc(s["hT_ps"], 2)
            pe.wait_ge(s["w_loaded"], 16 * (DC + A_GROUP))

            def project(n, slot, uses):
                pe.wait_ge(mix_loaded[slot], uses * 16 + 16)
                pe.wait_ge(s["out_copied"], n + 1)
                for half in range(2):
                    cols = slice(half * 512, half * 512 + 512)
                    for k in range(DC):
                        last = pe.matmul(ps_O[:, slot, cols], mixT[:, slot, k, :], w[:, k, cols],
                                         start=(k == 0), stop=(k == DC - 1))
                last.then_inc(s["out_done"], 1)

            def turn(n, slot):
                pe.wait_ge(s["x1_ready"], n + 1)
                pe.wait_ge(s["hT_ready"], n + 1)
                for k in range(DC):
                    last = pe.transpose(ps_T[:, slot, k, :], x[:, slot, k * P:(k + 1) * P], K["ident"][:])
                last.then_inc(s["hT_ps"], 1)

            project(0, 0, 0)
            with pe.Fori(0, TILES // 2) as i:
                project(i * 2 + 1, 1, i)
                turn(i * 2, 0)
                project(i * 2 + 2, 0, i + 1)
                turn(i * 2 + 1, 1)
            turn(TILES - 1, 0)

        @block.scalar
        def _(act):
            act.sem_inc(s["hT_ready"], 2)
            for b in range(2):
                act.sem_inc(hT_stored[b], 16)

            def body(n, slot, uses, sample):
                if not sample:
                    act.wait_ge(s["hT_ps"], n + 3)
                    act.wait_ge(hT_stored[slot], uses * 16 + 16)
                    for k in range(DC):
                        last = act.activation(hT[:, slot, k, :], ps_T[:, slot, k, :], ACT.Identity,
                                              bias=K["modT"][:, 2, k, 0:1], scale=K["modT"][:, 3, k, 0:1])
                    last.then_inc(s["hT_ready"], 1)
                if sample:
                    act.wait_ge(s["hT_sample_ready"], 1)
                else:
                    act.wait_ge(s["hT_ready"], n + 3)
                act.dma_start(S["h2T"][:, :, bass.ds(n * P, P)].rearrange("k p t -> p k t"), hT[:, slot]
                              ).then_inc(hT_stored[slot], 16)
            tiles(act, body)
            act.wait_ge(hT_stored[0], 16 * (TILES // 2 + 2))
            act.wait_ge(hT_stored[1], 16 * (TILES // 2 + 1))

        @block.vector
        def _(dve):
            dve.sem_inc(s["out_copied"], 2)
            dve.wait_ge(s["lnrow_loaded"], 32)

            def body(n, slot, uses, sample):
                dve.wait_ge(s["out_done"], n + 3)
                dve.tensor_tensor(y[:, slot], ps_O[:, slot], K["gates"][:, 0, int(sample)], ALU.mult
                                  ).then_inc(s["out_copied"], 1)
                dve.drain()
                dve.wait_ge(x_loaded[slot], uses * 16 + 16)
                dve.scalar_tensor_tensor(x[:, slot], x[:, slot], ALPHA, y[:, slot], ALU.mult, ALU.add)
                dve.drain()
                layer_norm_stats(dve, x[:, slot:slot + 1, :], stats, mean_var, 1).then_inc(s["stats_done"], 1)
                dve.wait_ge(s["rstd_done"], n + 1)
                dve.tensor_scalar(x[:, slot], x[:, slot], mean_var[:, 0, 0:1], rstd[:, 0:1],
                                  ALU.subtract, ALU.mult)
                dve.drain()
                dve.tensor_tensor(x[:, slot], x[:, slot], ln_g[:], ALU.mult)
                dve.drain()
                dve.tensor_tensor(x[:, slot], x[:, slot], ln_b[:], ALU.add).then_inc(s["x1_ready"], 1)
                if sample:
                    dve.wait_ge(s["hT_ps"], n + 3)
                    dve.wait_ge(hT_stored[slot], uses * 16 + 16)
                    modulate_samples(dve, hT[:, slot], ps_T[:, slot], K["modT"], 2
                                     ).then_inc(s["hT_sample_ready"], 1)
            tiles(dve, body)


def modulate_samples(dve, hT, ps_T, modT, kind):
    split = lambda a, k: a[:, k, 0:P].rearrange("p (b t) -> p b t", b=DEC_B)
    by_sequence = lambda j, k: modT[:, j, k, 1:].unsqueeze(2).to_broadcast([P, DEC_B, DEC_T])
    for k in range(DC):
        dve.tensor_tensor(split(hT, k), split(ps_T, k), by_sequence(kind + 1, k), ALU.mult)
    dve.drain()
    for k in range(DC):
        last = dve.tensor_tensor(split(hT, k), split(hT, k), by_sequence(kind, k), ALU.add)
    return last


def stage_ffn(nc, K, IN, OUT, S):
    HIST = FFN_CONV - 1
    HR = DEC_B * HIST
    NL = HIST + HR
    WD = 4
    with ExitStack() as ctx:
        ctx.callback(nc.all_engine_barrier)
        sb = lambda name, shape: ctx.enter_context(nc.sbuf_tensor(name, shape, F32))
        ps = lambda name, shape: ctx.enter_context(nc.psum_tensor(name, shape, F32))
        wgu = sb("w_gate_up", [P, 2, 2, DC, P])
        wd = sb("w_down_ring", [P, WD, 512])
        hT = sb("h2T_group", [P, DC, GROUP])
        act_T = sb("hidden_T", [P, FC, GROUP])
        x = sb("x1_group", [P, GT, D])
        y = sb("gated_ffn", [P, 2, 512])
        raw = sb("gate_raw", [P, 2, HIST + GROUP])
        conv = sb("gate_conv", [P, 2, GROUP])
        taps = sb("ffn_taps", [P, FC, FFN_CONV])
        hist = sb("ffn_hist", [P, FC, HIST])
        hist_s = sb("ffn_hist_samples", [P, FC, HR])
        last_raw = sb("ffn_last_raw", [P, FC, NL])
        rows = sb("ffn_rows", [P, D_FF])
        ln_g, ln_b = sb("ln2_g_rows", [P, D]), sb("ln2_b_rows", [P, D])
        stats = sb("ln2_stats", [P, GT, 2, 6])
        mean_var = sb("ln2_mean_var", [P, GT, 2])
        rstd = sb("ln2_rstd", [P, GT])
        minus_half, eps = sb("ln2_minus_half", [P, GT]), sb("ln2_eps", [P, GT])
        ps_gu = ps("ps_gate_up", [P, 2, 2, 512])
        ps_D = ps("ps_down", [P, GT, 512])
        s = signals(nc, ctx, "ffn", "rows_loaded lnrow_loaded hT_loaded x_loaded y_stored gu_done raw_ready "
                             "conv_done silu_done hidden_ready wd_used down_done down_copied "
                             "stats_done rstd_done y_ready taps_ps taps_ready last_kept last_ps "
                             "last_copied rows_stored")
        gu_loaded = [signal(nc, ctx, "ffn", f"gu_loaded{b}") for b in range(2)]
        wd_loaded = [signal(nc, ctx, "ffn", f"wd_loaded{b}") for b in range(WD)]

        def groups(engine, body):
            with engine.Fori(0, GROUPS - 1) as i:
                body(i, GT, GROUP, "prompt")
            body(GROUPS - 1, GT, GROUP, "sample")
            body(GROUPS, 1, P, None)

        block = ctx.enter_context(nc.Block())

        @block.sync
        def _(sp):
            w_gu = [IN[n][0].rearrange("(k p) f -> p k f", p=P) for n in ("w_gate", "w_up")]

            def body(it, tiles, tokens, follows):
                for c in range(FC):
                    sp.wait_ge(s["gu_done"], it * FC + (c + 1))
                    for j in range(2):
                        sp.dma_start(wgu[:, c % 2, j], w_gu[j][:, :, c * P:(c + 1) * P]
                                     ).then_inc(gu_loaded[c % 2], 16)
                for j in range(2 * FC):
                    half, c = j // FC, j % FC
                    sp.wait_ge(s["wd_used"], it * (2 * FC) + (j + 1))
                    sp.dma_start(wd[:, j % WD], IN["w_down"][0, c * P:(c + 1) * P, half * 512:half * 512 + 512]
                                 ).then_inc(wd_loaded[j % WD], 16)
            groups(sp, body)
            sp.wait_ge(s["last_copied"], 2)
            sp.dma_start(OUT["p_ffn_conv"].rearrange("l b t c -> (l b t) c"), rows[0:HIST, :]
                         ).then_inc(s["rows_stored"], 16)
            sp.dma_start(OUT["s_ffn_conv"].rearrange("l b t c -> (l b t) c"), rows[HIST:NL, :]
                         ).then_inc(s["rows_stored"], 16)
            sp.wait_ge(s["rows_stored"], 32)

        @block.gpsimd
        def _(pool):
            pool.memset(minus_half[:], -0.5)
            pool.memset(eps[:], LN_EPS)
            pool.drain()
            pool.dma_start(rows[0:FFN_CONV, :], IN["ffn_conv_w"][0]).then_inc(s["rows_loaded"], 16)
            pool.dma_start(rows[32:32 + HR, :], IN["state_ffn_conv"].rearrange("l b t c -> (l b t) c")
                           ).then_inc(s["rows_loaded"], 16)
            pool.dma_start(ln_g[:], row_broadcast(IN["ln2_g"])).then_inc(s["lnrow_loaded"], 16)
            pool.dma_start(ln_b[:], row_broadcast(IN["ln2_b"])).then_inc(s["lnrow_loaded"], 16)

            def load_hT(it, tokens):
                pool.dma_start(hT[:, :, 0:tokens], S["h2T"][:, :, bass.ds(it * GROUP, tokens)].rearrange(
                    "k p t -> p k t")).then_inc(s["hT_loaded"], 16)

            def load_x(it, tiles):
                pool.dma_start(x[:, 0:tiles], S["x1"][bass.ds(it * GROUP, tiles * P), :].rearrange(
                    "(t p) d -> p t d", p=P)).then_inc(s["x_loaded"], 16)

            def body(it, tiles, tokens, follows):
                next_tiles = GT if follows == "prompt" else 1
                if follows is not None:
                    pool.wait_ge(s["gu_done"], it * FC + (FC + 2))
                    load_hT(it + 1, next_tiles * P)
                pool.wait_ge(s["stats_done"], it + 1)
                rstd_of(pool, rstd[:, 0:tiles], mean_var[:, 0:tiles, 1], eps[:, 0:tiles],
                        minus_half[:, 0:tiles]).then_inc(s["rstd_done"], 1)
                pool.wait_ge(s["y_ready"], it + 1)
                dst = (OUT["y_sample"].rearrange("b t d -> (b t) d") if follows is None
                       else OUT["y_prompt"][0, bass.ds(it * GROUP, GROUP), :])
                pool.dma_start(dst.rearrange("(t p) d -> p t d", p=P), x[:, 0:tiles]).then_inc(s["y_stored"], 16)
                pool.wait_ge(s["y_stored"], it * 16 + 16)
                if follows is not None:
                    load_x(it + 1, next_tiles)

            load_hT(0, GROUP)
            load_x(0, GT)
            groups(pool, body)

        @block.tensor
        def _(pe):
            pe.sem_inc(s["gu_done"], 2)
            pe.sem_inc(s["wd_used"], WD)
            pe.wait_ge(s["rows_loaded"], 32)
            for c in range(FC):
                pe.transpose(ps_gu[:, 0, 0, c * FFN_CONV:(c + 1) * FFN_CONV], rows[0:FFN_CONV, c * P:(c + 1) * P],
                             K["ident"][0:FFN_CONV, 0:FFN_CONV])
                last = pe.transpose(ps_gu[:, 0, 1, c * HR:(c + 1) * HR], rows[32:32 + HR, c * P:(c + 1) * P],
                                    K["ident"][32:32 + HR, 32:32 + HR])
            last.then_inc(s["taps_ps"], 1)
            pe.wait_ge(s["taps_ready"], 1)

            def body(it, tiles, tokens, follows):
                pe.wait_ge(s["hT_loaded"], it * 16 + 16)
                for c in range(FC):
                    b = c % 2
                    pe.wait_ge(gu_loaded[b], it * (FC * 16) + (c // 2 * 32 + 32))
                    pe.wait_ge(s["hidden_ready"], it * FC + (c + 1))
                    for j in range(2):
                        for k in range(DC):
                            last = pe.matmul(ps_gu[:, b, j, 0:tokens], wgu[:, b, j, k, :], hT[:, k, 0:tokens],
                                             start=(k == 0), stop=(k == DC - 1))
                    last.then_inc(s["gu_done"], 1)
                for j in range(2 * FC):
                    half, c = j // FC, j % FC
                    pe.wait_ge(wd_loaded[j % WD], it * (2 * FC // WD * 16) + (j // WD * 16 + 16))
                    pe.wait_ge(s["hidden_ready"], it * FC + (c + 3))
                    for t in range(tiles):
                        if c == 0:
                            pe.wait_ge(s["down_copied"], it * (2 * GT) + (half * GT + t + 1))
                        last = pe.matmul(ps_D[:, t], act_T[:, c, t * P:(t + 1) * P], wd[:, j % WD],
                                         start=(c == 0), stop=(c == FC - 1))
                        if c == FC - 1 and t < tiles - 1:
                            last.then_inc(s["down_done"], 1)
                    last.then_inc(s["wd_used"], 1)
            groups(pe, body)
            pe.wait_ge(s["last_kept"], 2)
            for part in range(2):
                pe.wait_ge(s["down_copied"], GT + 2 * (GROUPS * GT + 1))
                for c in range(part * 16, min(FC, part * 16 + 16)):
                    q = c - part * 16
                    dst = (ps_D[0:NL, q // 4] if part == 0 else ps_gu[0:NL, 0, q // 4])
                    last = pe.transpose(dst[:, (q % 4) * P:(q % 4 + 1) * P], last_raw[:, c, :], K["ident"][:])
                last.then_inc(s["last_ps"], 1)

        @block.scalar
        def _(act):
            def body(it, tiles, tokens, follows):
                for c in range(FC):
                    b = c % 2
                    act.wait_ge(s["gu_done"], it * FC + (c + 3))
                    if follows is None:
                        dst = raw[:, b, 0:DEC_B * (HIST + DEC_T)].rearrange("p (b t) -> p b t", b=DEC_B)[:, :, HIST:]
                        src = ps_gu[:, b, 0, 0:P].rearrange("p (b t) -> p b t", b=DEC_B)
                    else:
                        dst, src = raw[:, b, HIST:], ps_gu[:, b, 0, :]
                    act.activation(dst, src, ACT.Identity).then_inc(s["raw_ready"], 1)
                    act.wait_ge(s["conv_done"], it * FC + (c + 1))
                    act.activation(conv[:, b, 0:tokens], conv[:, b, 0:tokens], ACT.Silu
                                   ).then_inc(s["silu_done"], 1)
            groups(act, body)

        @block.vector
        def _(dve):
            dve.sem_inc(s["hidden_ready"], 2)
            dve.sem_inc(s["down_copied"], GT)
            dve.wait_ge(s["taps_ps"], 1)
            dve.tensor_copy(taps[:].rearrange("p c t -> p (c t)"), ps_gu[:, 0, 0, 0:FC * FFN_CONV])
            dve.tensor_copy(hist_s[:].rearrange("p c t -> p (c t)"), ps_gu[:, 0, 1, 0:FC * HR])
            dve.memset(hist[:], 0.0).then_inc(s["taps_ready"], 1)
            dve.drain()
            dve.wait_ge(s["lnrow_loaded"], 32)

            def body(it, tiles, tokens, follows):
                sample = follows is None
                for c in range(FC):
                    b = c % 2
                    by_seq = raw[:, b, 0:DEC_B * (HIST + DEC_T)].rearrange("p (b t) -> p b t", b=DEC_B)
                    dst = conv[:, b, 0:tokens]
                    if sample:
                        dve.tensor_copy(by_seq[:, :, 0:HIST], hist_s[:, c].rearrange("p (b t) -> p b t", b=DEC_B))
                        dst = dst.rearrange("p (b t) -> p b t", b=DEC_B)
                    else:
                        dve.tensor_copy(raw[:, b, 0:HIST], hist[:, c])
                    dve.drain()
                    dve.wait_ge(s["raw_ready"], it * FC + (c + 1))
                    for i in range(FFN_CONV):
                        src = by_seq[:, :, i:i + DEC_T] if sample else raw[:, b, i:i + GROUP]
                        if i == 0:
                            last = dve.tensor_scalar(dst, src, taps[:, c, 0:1], None, ALU.mult)
                        else:
                            dve.drain()
                            last = dve.scalar_tensor_tensor(dst, src, taps[:, c, i:i + 1], dst, ALU.mult, ALU.add)
                    last.then_inc(s["conv_done"], 1)
                    if follows == "prompt":
                        dve.tensor_copy(hist[:, c], raw[:, b, GROUP:GROUP + HIST])
                    elif follows == "sample":
                        dve.tensor_copy(last_raw[:, c, 0:HIST], raw[:, b, GROUP:GROUP + HIST])
                    else:
                        dve.tensor_copy(last_raw[:, c, HIST:NL].rearrange("p (b t) -> p b t", b=DEC_B),
                                        by_seq[:, :, DEC_T:DEC_T + HIST])
                    dve.wait_ge(s["silu_done"], it * FC + (c + 1))
                    last = dve.tensor_tensor(act_T[:, c, 0:tokens], conv[:, b, 0:tokens], ps_gu[:, b, 1, 0:tokens],
                                             ALU.mult)
                    last.then_inc(s["hidden_ready"], 1)
                if follows != "prompt":
                    dve.drain()
                    dve.sem_inc(s["last_kept"], 1)
                dve.wait_ge(s["x_loaded"], it * 16 + 16)
                for half in range(2):
                    cols = slice(half * 512, half * 512 + 512)
                    for t in range(tiles):
                        if t < tiles - 1:
                            dve.wait_ge(s["down_done"], it * (2 * GT - 2) + (half * (GT - 1) + t + 1))
                        else:
                            dve.wait_ge(s["wd_used"], it * (2 * FC) + ((half + 1) * FC + WD))
                        dve.tensor_tensor(y[:, (half * tiles + t) % 2], ps_D[:, t], K["gates"][:, 1, int(sample), cols], ALU.mult
                                          ).then_inc(s["down_copied"], 1)
                        dve.drain()
                        dve.scalar_tensor_tensor(x[:, t, cols], x[:, t, cols], ALPHA, y[:, (half * tiles + t) % 2],
                                                 ALU.mult, ALU.add)
                dve.drain()
                layer_norm_stats(dve, x, stats, mean_var, tiles).then_inc(s["stats_done"], 1)
                dve.wait_ge(s["rstd_done"], it + 1)
                for t in range(tiles):
                    dve.tensor_scalar(x[:, t], x[:, t], mean_var[:, t, 0:1], rstd[:, t:t + 1],
                                      ALU.subtract, ALU.mult)
                dve.drain()
                for t in range(tiles):
                    dve.tensor_tensor(x[:, t], x[:, t], ln_g[:], ALU.mult)
                dve.drain()
                for t in range(tiles):
                    last = dve.tensor_tensor(x[:, t], x[:, t], ln_b[:], ALU.add)
                last.then_inc(s["y_ready"], 1)
            groups(dve, body)
            dve.wait_ge(s["last_ps"], 1)
            dve.tensor_copy(rows[0:NL, 0:2048], ps_D[0:NL].rearrange("p a b -> p (a b)")
                            ).then_inc(s["last_copied"], 1)
            dve.wait_ge(s["last_ps"], 2)
            dve.tensor_copy(rows[0:NL, 2048:D_FF], ps_gu[0:NL, 0].rearrange("p a b -> p (a b)")[:, 0:D_FF - 2048]
                            ).then_inc(s["last_copied"], 1)


def stage_window(nc, K, IN, OUT, S):
    TILES = SEQ // P
    H, KEYS, SKEYS = A_HEADS, 2 * P, WINDOW + DEC_T
    SC = HD ** -0.5
    with ExitStack() as ctx:
        ctx.callback(nc.all_engine_barrier)
        sb = lambda name, shape: ctx.enter_context(nc.sbuf_tensor(name, shape, F32))
        ps = lambda name, shape: ctx.enter_context(nc.psum_tensor(name, shape, F32))
        qT = sb("aqT", [P, 4, A_GROUP, P])
        kT = sb("akT", [P, 4, P])
        v_rows = sb("av_rows", [P, 4, P])
        mask = sb("window_mask", [P, 2, KEYS])
        sc = sb("scores", [P, 2, H, KEYS])
        pT = sb("probsT", [P, A_KV, A_GROUP, 2, P])
        mix = sb("mixA", [P, 2, A_GROUP, P])
        sink = sb("sink_rows", [P, H])
        top, neg_top, sink_less = sb("top", [P, 2, H]), sb("neg_top", [P, 2, H]), sb("sink_less", [P, 2, H])
        sink_exp, den = sb("sink_exp", [P, 2, H]), sb("den", [P, 2, H])
        s_cache_k = sb("s_cache_k", [P, DEC_B, P])
        s_cache_v = sb("s_cache_v", [P, DEC_B, P])
        s_new_v = sb("s_new_v", [DEC_T, DEC_B, P])
        s_kT = sb("s_kT", [P, DEC_B, SKEYS])
        s_qT = sb("s_qT_masked", [P, A_GROUP, DEC_B, P])
        ak_rows = sb("ak_rows", [P, 2, P])
        ps_S = ps("ps_scores", [P, A_KV, 1024])
        ps_T = ps("ps_probsT", [P, 1024])
        ps_O = ps("ps_window_out", [P, A_KV, 512])
        s = signals(nc, ctx, "window", "sink_loaded blank_ready masks_ready scores_done scores_read bias_ready "
                             "exp_done p_ready pT_ps pT_copied_act pT_copied_dve out_done mix_copied "
                             "cache_loaded s_kT_ps s_kT_ready rows_ps rows_ready q_masked moved "
                             "s_tail_ps s_tail_copied s_vnew_loaded")
        loaded = [signal(nc, ctx, "window", f"qkv_loaded{j}") for j in range(4)]
        mix_stored = [signal(nc, ctx, "window", f"mixA_stored{b}") for b in range(2)]
        block = ctx.enter_context(nc.Block())

        def quads(engine, body):
            with engine.Fori(0, TILES // 4 - 1) as i:
                for j in range(4):
                    body(i * 4 + j, j, i, False)
            for j in range(4):
                body(TILES - 4 + j, j, TILES // 4 - 1, j == 3)

        def copy_probs(engine, pT, ps_T, v, width):
            copy = (lambda o, i: engine.activation(o, i, ACT.Identity)) if v == 0 else engine.tensor_copy
            split = ps_T[:, 0:A_GROUP * 2 * P].rearrange("p (g w t) -> p g w t", g=A_GROUP, w=2)
            if width == KEYS:
                return copy(pT[:, v].rearrange("p g w t -> p (g w t)"), ps_T[:, 0:A_GROUP * 2 * P])
            copy(pT[:, v, :, 0], split[:, :, 0])
            return copy(pT[0:width - P, v, :, 1], split[0:width - P, :, 1])

        @block.sync
        def _(sp):
            def load(n, j):
                at = bass.ds(n * P, P)
                sp.dma_start(qT[:, j], S["qkT"][QKT_AQ:QKT_AK, :, at].rearrange("g p t -> p g t")
                             ).then_inc(loaded[j], 16)
                sp.dma_start(kT[:, j], S["qkT"][QKT_AK, :, at]).then_inc(loaded[j], 16)
                sp.dma_start(v_rows[:, j], S["av"][at, :]).then_inc(loaded[j], 16)

            for j in range(3):
                load(j, j)

            def body(n, j, i, last):
                sp.wait_ge(s["out_done"], n + 1)
                load(n + 3, (j + 3) % 4)
            with sp.Fori(0, TILES // 4 - 1) as i:
                for j in range(4):
                    body(i * 4 + j, j, i, False)
            body(TILES - 4, 0, 0, False)
            sp.wait_ge(s["out_done"], TILES - 2)
            load(TILES, 0)
            sp.dma_start(s_new_v[:], S["av"][SEQ:TOKENS, :].rearrange("(b t) d -> t b d", b=DEC_B)
                         ).then_inc(s["s_vnew_loaded"], 16)
            for c, (name, dst) in enumerate((("cache_a_k", s_cache_k), ("cache_a_v", s_cache_v))):
                sp.dma_start(dst[:], IN[name][0].rearrange("b w h d -> w b (h d)")).then_inc(s["cache_loaded"], 16)
            rows = lambda a: a.rearrange("l b w h d -> (l b) w (h d)")
            keep = WINDOW - DEC_T
            sp.dma_start(rows(OUT["p_a_v"])[0], S["av"][SEQ - WINDOW:SEQ, :]).then_inc(s["moved"], 16)
            sp.dma_start(rows(OUT["s_a_v"])[:, keep:, :], S["av"][SEQ:TOKENS, :].rearrange(
                "(b t) d -> b t d", b=DEC_B)).then_inc(s["moved"], 16)
            for a in ("k", "v"):
                sp.dma_start(rows(OUT[f"s_a_{a}"])[:, 0:keep, :], rows(IN[f"cache_a_{a}"])[:, DEC_T:, :]
                             ).then_inc(s["moved"], 16)
            sp.wait_ge(s["rows_ready"], 1)
            sp.dma_start(rows(OUT["p_a_k"])[0], ak_rows[:, 0]).then_inc(s["moved"], 16)
            for b in range(DEC_B):
                sp.dma_start(rows(OUT["s_a_k"])[b, keep:, :], ak_rows[b * DEC_T:(b + 1) * DEC_T, 1]
                             ).then_inc(s["moved"], 16)
            sp.wait_ge(s["moved"], 16 * (5 + DEC_B))

        @block.gpsimd
        def _(pool):
            pool.dma_start(sink[:], row_broadcast(IN["a_sinks"])).then_inc(s["sink_loaded"], 16)
            pool.memset(kT[:, 3], 0.0)
            pool.memset(v_rows[:, 3], 0.0).then_inc(s["blank_ready"], 1)
            pool.memset(mask[:], 0.0)
            pool.memset(s_qT[:], 0.0)
            pool.drain()
            pool.memset(mask[64:P, 1, 0:64], NEG)
            pool.drain()
            pool.memset(mask[0:64, 1, P + 64:], NEG)
            pool.drain()
            pool.memset(mask[:, 0, 0:P], NEG)
            pool.drain()
            pool.memset(mask[0:64, 0, P + 64:], NEG).then_inc(s["masks_ready"], 1)

        @block.tensor
        def _(pe):
            pe.wait_ge(s["blank_ready"], 1)

            def scores(n, j, uses):
                pe.wait_ge(loaded[j], uses * 48 + 48)
                pe.wait_ge(s["scores_read"], n + 1)
                for v in range(A_KV):
                    rows = slice(v * HD, (v + 1) * HD)
                    for g in range(A_GROUP):
                        for w, slot in ((0, (j + 3) % 4), (1, j)):
                            c0 = g * KEYS + w * P
                            last = pe.matmul(ps_S[:, v, c0:c0 + P], qT[rows, j, g, :], kT[rows, slot, :],
                                             start=True, stop=True)
                last.then_inc(s["scores_done"], 1)

            def probs_turned(n, b, width):
                for v in range(A_KV):
                    pe.wait_ge(s["p_ready"], n * 2 + (v + 1))
                    if v == 0:
                        pe.wait_ge(s["pT_copied_dve"], n + 1)
                    else:
                        pe.wait_ge(s["pT_copied_act"], n + 1)
                    for g in range(A_GROUP):
                        for w in range(2):
                            keys = min(P, width - w * P)
                            o = (g * 2 + w) * P
                            last = pe.transpose(ps_T[0:keys, o:o + P],
                                                sc[:, b, v * A_GROUP + g, w * P:w * P + keys], K["ident"][:])
                    last.then_inc(s["pT_ps"], 1)

            def out(n, j):
                pe.wait_ge(s["pT_copied_dve"], n + 2)
                pe.wait_ge(s["mix_copied"], n * 2 + 2)
                for v in range(A_KV):
                    for g in range(A_GROUP):
                        for w, slot in ((0, (j + 3) % 4), (1, j)):
                            last = pe.matmul(ps_O[:, v, g * P:(g + 1) * P], v_rows[:, slot, :],
                                             pT[:, v, g, w, :], start=(w == 0), stop=(w == 1))
                last.then_inc(s["out_done"], 1)

            scores(0, 0, 0)

            def body(n, j, i, last):
                if not last:
                    scores(n + 1, (j + 1) % 4, i + (1 if j == 3 else 0))
                probs_turned(n, j % 2, KEYS)
                out(n, j)
            quads(pe, body)

            pe.wait_ge(loaded[0], 48 * (TILES // 4 + 1))
            pe.wait_ge(s["pT_copied_dve"], TILES + 1)
            for a, slot in enumerate((3, 0)):
                last = pe.transpose(ps_T[:, a * P:(a + 1) * P], kT[:, slot, :], K["ident"][:])
            last.then_inc(s["rows_ps"], 1)
            pe.wait_ge(s["cache_loaded"], 32)
            pe.wait_ge(s["rows_ready"], 1)
            for b in range(DEC_B):
                last = pe.transpose(ps_T[:, b * P:(b + 1) * P], s_cache_k[:, b, :], K["ident"][:])
            last.then_inc(s["s_kT_ps"], 1)
            pe.wait_ge(s["s_kT_ready"], 1)
            pe.wait_ge(s["q_masked"], 1)
            pe.wait_ge(s["scores_read"], TILES + 1)
            for v in range(A_KV):
                rows = slice(v * HD, (v + 1) * HD)
                for g in range(A_GROUP):
                    for b in range(DEC_B):
                        last = pe.matmul(ps_S[:, v, g * KEYS:g * KEYS + SKEYS], s_qT[rows, g, b, :], s_kT[rows, b, :],
                                         start=(b == 0), stop=(b == DEC_B - 1))
            last.then_inc(s["scores_done"], 1)
            probs_turned(TILES, 0, SKEYS)
            pe.wait_ge(s["pT_copied_dve"], TILES + 2)
            pe.wait_ge(s["mix_copied"], TILES * 2 + 2)
            pe.wait_ge(s["s_vnew_loaded"], 16)
            for v in range(A_KV):
                for g in range(A_GROUP):
                    for b in range(DEC_B):
                        q = slice(b * DEC_T, (b + 1) * DEC_T)
                        o = ps_O[:, v, g * P + b * DEC_T:g * P + (b + 1) * DEC_T]
                        pe.matmul(o, s_cache_v[:, b, :], pT[:, v, g, 0, q], start=True, stop=False)
                        last = pe.matmul(o, s_new_v[:, b, :], pT[0:DEC_T, v, g, 1, q], start=False, stop=True)
            last.then_inc(s["out_done"], 1)

        @block.scalar
        def _(act):
            for b in range(2):
                act.sem_inc(mix_stored[b], 16)

            def body(n, b, uses, width):
                act.wait_ge(s["bias_ready"], n + 1)
                for h in range(H):
                    act.activation(sc[:, b, h, 0:width], sc[:, b, h, 0:width], ACT.Exp, bias=neg_top[:, b, h:h + 1],
                                   scale=SC, accum_out=den[:, b, h:h + 1])
                act.activation(sink_exp[:, b], sink_less[:, b], ACT.Exp).then_inc(s["exp_done"], 1)
                act.wait_ge(s["pT_ps"], n * 2 + 1)
                copy_probs(act, pT, ps_T, 0, width).then_inc(s["pT_copied_act"], 1)
                act.wait_ge(s["out_done"], n + 1)
                act.wait_ge(mix_stored[b], uses * 16 + 16)
                act.activation(mix[0:HD, b].rearrange("p g t -> p (g t)"), ps_O[0:HD, 0, 0:A_GROUP * P],
                               ACT.Identity).then_inc(s["mix_copied"], 1)
                act.wait_ge(s["mix_copied"], n * 2 + 4)
                act.dma_start(S["mixT"][0:A_GROUP, :, bass.ds(n * P, P)].rearrange("g p t -> p g t"), mix[:, b]
                              ).then_inc(mix_stored[b], 16)
            quads(act, lambda n, j, i, last: body(n, j % 2, i * 2 + j // 2, KEYS))
            body(TILES, 0, TILES // 2, SKEYS)
            act.wait_ge(mix_stored[0], 16 * (TILES // 2 + 2))
            act.wait_ge(mix_stored[1], 16 * (TILES // 2 + 1))

        @block.vector
        def _(dve):
            dve.sem_inc(s["scores_read"], 1)
            dve.sem_inc(s["pT_copied_dve"], 1)
            dve.sem_inc(s["mix_copied"], 2)
            dve.wait_ge(s["sink_loaded"], 16)
            dve.wait_ge(s["masks_ready"], 1)

            def shifted(n, b, width, which):
                dve.wait_ge(s["scores_done"], n + 1)
                for v in range(A_KV):
                    src = ps_S[:, v, 0:A_GROUP * KEYS].rearrange("p (g k) -> p g k", g=A_GROUP)[:, :, 0:width]
                    dst = sc[:, b, v * A_GROUP:(v + 1) * A_GROUP, 0:width]
                    if which is None:
                        last = dve.tensor_copy(dst, src)
                    else:
                        last = dve.tensor_tensor(dst, src, mask[:, which].unsqueeze(1).to_broadcast(
                            [P, A_GROUP, KEYS]), ALU.add)
                last.then_inc(s["scores_read"], 1)
                dve.drain()
                dve.tensor_reduce(top[:, b], sc[:, b, :, 0:width], AX.X, ALU.max)
                dve.drain()
                dve.scalar_tensor_tensor(top[:, b], top[:, b], SC, sink[:], ALU.mult, ALU.max)
                dve.drain()
                dve.tensor_scalar(neg_top[:, b], top[:, b], -1.0, None, ALU.mult)
                dve.tensor_tensor(sink_less[:, b], sink[:], top[:, b], ALU.subtract).then_inc(s["bias_ready"], 1)

            def normalised(n, b, width):
                dve.wait_ge(s["exp_done"], n + 1)
                dve.tensor_tensor(den[:, b], den[:, b], sink_exp[:, b], ALU.add)
                dve.drain()
                dve.reciprocal(den[:, b], den[:, b])
                dve.drain()
                for v in range(A_KV):
                    for g in range(A_GROUP):
                        h = v * A_GROUP + g
                        last = dve.tensor_scalar(sc[:, b, h, 0:width], sc[:, b, h, 0:width], den[:, b, h:h + 1], None,
                                                 ALU.mult)
                    last.then_inc(s["p_ready"], 1)

            def copied(n, b, uses, width):
                dve.wait_ge(s["pT_ps"], n * 2 + 2)
                copy_probs(dve, pT, ps_T, 1, width).then_inc(s["pT_copied_dve"], 1)
                dve.wait_ge(s["out_done"], n + 1)
                dve.wait_ge(mix_stored[b], uses * 16 + 16)
                dve.tensor_copy(mix[HD:P, b].rearrange("p g t -> p (g t)"), ps_O[HD:P, 1, 0:A_GROUP * P]
                                ).then_inc(s["mix_copied"], 1)

            shifted(0, 0, KEYS, 0)

            def body(n, j, i, last):
                normalised(n, j % 2, KEYS)
                if not last:
                    shifted(n + 1, (j + 1) % 2, KEYS, 1)
                copied(n, j % 2, i * 2 + j // 2, KEYS)
            quads(dve, body)
            dve.wait_ge(s["rows_ps"], 1)
            dve.tensor_copy(ak_rows[:].rearrange("p a t -> p (a t)"), ps_T[:, 0:2 * P]).then_inc(s["rows_ready"], 1)
            dve.wait_ge(loaded[0], 48 * (TILES // 4 + 1))
            for b in range(DEC_B):
                q = slice(b * DEC_T, (b + 1) * DEC_T)
                last = dve.tensor_copy(s_qT[:, :, b, q], qT[:, 0, :, q])
            last.then_inc(s["q_masked"], 1)
            dve.tensor_copy(s_kT[:, :, WINDOW:], kT[:, 0, :].rearrange("p (b t) -> p b t", b=DEC_B))
            dve.wait_ge(s["s_kT_ps"], 1)
            dve.tensor_copy(s_kT[:, :, 0:WINDOW], ps_T[:].rearrange("p (b k) -> p b k", b=DEC_B)
                            ).then_inc(s["s_kT_ready"], 1)
            shifted(TILES, 0, SKEYS, None)
            normalised(TILES, 0, SKEYS)
            copied(TILES, 0, TILES // 2, SKEYS)


def softplus_part(act, z, e):
    act.activation(e, z, ACT.Abs)
    act.drain()
    act.activation(e, e, ACT.Exp, scale=-1.0)
    act.drain()
    return act.activation(e, e, ACT.Ln, bias=1.0)


def stage_stick(nc, K, IN, S):
    H = C_HEADS
    with ExitStack() as ctx:
        ctx.callback(nc.all_engine_barrier)
        sb = lambda name, shape: ctx.enter_context(nc.sbuf_tensor(name, shape, F32))
        ps = lambda name, shape: ctx.enter_context(nc.psum_tensor(name, shape, F32))
        qT = sb("cqT", [P, 2, 2, GROUP])
        kT = sb("ckT_block", [P, 2, 2, P])
        v_rows = sb("cv_block", [P, 2, H * HD])
        e = sb("stick_e", [P, H, GROUP])
        sp_ = sb("stick_softplus", [P, H, GROUP])
        a = sb("stick_weight", [P, H, GROUP])
        mix = sb("mixC", [P, 2, GROUP])
        ps_z = ps("ps_z", [P, 2, GROUP])
        ps_C = ps("ps_later", [P, H, GROUP])
        ps_O = ps("ps_stick_out", [P, 2, GROUP])
        s = signals(nc, ctx, "stick", "q_loaded q_ready z_done chain_done sp_done T_done u_done exp_done "
                             "a_masked item_done o_done o_copied mix_stored")
        loaded = [signal(nc, ctx, "stick", f"ckv_loaded{b}") for b in range(2)]
        block = ctx.enter_context(nc.Block())

        first_beta = [sum(4 * q + 4 for q in range(Q)) for Q in range(GROUPS + 1)]

        def blocks(engine, body):
            for Q in range(GROUPS):
                b0 = first_beta[Q]
                for j in (3, 2, 1, 0):
                    nxt = ((4 - j) % 2, max(j - 1, 0) * P)
                    if Q == 0 and j == 0:
                        nxt = None
                    body(Q, b0 + 3 - j, (3 - j) % 2, 4 * Q + j, j * P, True, nxt, j == 3)
                pairs = 2 * Q
                if pairs > 1:
                    with engine.Fori(0, pairs - 1) as i:
                        for r in range(2):
                            body(Q, i * 2 + (b0 + 4 + r), r, i * -2 + (4 * Q - 1 - r), 0, False, (1 - r, 0), False)
                if pairs:
                    i = pairs - 1
                    for r in range(2):
                        body(Q, b0 + 4 + 2 * i + r, r, 1 - r, 0, False, (1, 0) if r == 0 else None, False)

        @block.sync
        def _(sp):
            def body(Q, beta, slot, kb, c0, diag, follows, first):
                if first:
                    if Q >= 2:
                        sp.wait_ge(s["o_done"], Q - 1)
                    sp.dma_start(qT[:, Q % 2], S["qkT"][QKT_CQ:QKT_CK, :, Q * GROUP:(Q + 1) * GROUP].rearrange(
                        "a p t -> p a t")).then_inc(s["q_loaded"], 16)
                sp.wait_ge(s["item_done"], beta * H + H)
                at = bass.ds(kb * P, P)
                sp.dma_start(kT[:, slot], S["qkT"][QKT_CK:QKT_N, :, at].rearrange("a p t -> p a t")
                             ).then_inc(loaded[slot], 16)
                sp.dma_start(v_rows[:, slot], S["cv"][at, :]).then_inc(loaded[slot], 16)
            blocks(sp, body)

        @block.tensor
        def _(pe):
            pe.sem_inc(s["item_done"], 2 * H)

            def z(Q, beta, slot, c0, h):
                rows = slice(h % 2 * HD, h % 2 * HD + HD)
                if h == 0:
                    pe.wait_ge(loaded[slot], (beta - slot) * 16 + 32)
                pe.wait_ge(s["sp_done"], beta * H + (h + 1))
                pe.matmul(ps_z[:, h % 2, c0:], kT[rows, slot, h // 2, :], qT[rows, Q % 2, h // 2, c0:],
                          start=True, stop=True).then_inc(s["z_done"], 1)

            def rest_and_pv(Q, beta, slot, c0, h, diag, first, last):
                if not last:
                    pe.wait_ge(s["u_done"], beta * H + (h + 1))
                    pe.matmul(ps_C[:, h, c0:], K["upto"][:], sp_[:, h, c0:], start=False, stop=True,
                              skip_group_check=True)
                if diag:
                    pe.wait_ge(s["a_masked"], Q * 4 * H + (beta - first_beta[Q]) * H + h + 1)
                else:
                    pe.wait_ge(s["exp_done"], beta * H + (h + 1))
                    pe.wait_ge(s["a_masked"], (Q + 1) * 4 * H)
                if first and Q:
                    pe.wait_ge(s["o_copied"], Q)
                rows = slice(h % 2 * HD, h % 2 * HD + HD)
                pe.matmul(ps_O[rows, h // 2, c0:], v_rows[:, slot, h * HD:(h + 1) * HD], a[:, h, c0:],
                          start=first, stop=last, skip_group_check=True).then_inc(s["item_done"], 1)

            def body(Q, beta, slot, kb, c0, diag, follows, first):
                if first:
                    pe.wait_ge(s["q_ready"], Q + 1)
                    z(Q, beta, slot, c0, 0)
                    z(Q, beta, slot, c0, 1)
                for h in range(H):
                    pe.wait_ge(s["sp_done"], beta * H + (h + 3))
                    pe.matmul(ps_C[:, h, c0:], K["later"][:], sp_[:, h, c0:], start=first, stop=True,
                              skip_group_check=True).then_inc(s["T_done"], 1)
                    if h + 2 < H:
                        z(Q, beta, slot, c0, h + 2)
                    elif follows is not None:
                        z(Q, beta + 1, follows[0], follows[1], h - 2)
                    if h > 0:
                        rest_and_pv(Q, beta, slot, c0, h - 1, diag, first, follows is None)
                    elif not first:
                        was_diag = diag or (isinstance(beta, int) and beta == first_beta[Q] + 4)
                        rest_and_pv(Q, beta - 1, 1 - slot, c0 + P if diag else 0, H - 1,
                                    was_diag, diag and beta == first_beta[Q] + 1, False)
                if follows is None:
                    rest_and_pv(Q, beta, slot, c0, H - 1, diag, first, True)
                    pe.drain()
                    pe.sem_inc(s["o_done"], 1)
            blocks(pe, body)

        @block.scalar
        def _(act):
            act.preload_act_table_set(LOG_EXP_TABLES)
            act.sem_inc(s["mix_stored"], 16)

            def chain(beta, c0, h):
                act.wait_ge(s["z_done"], beta * H + (h + 1))
                softplus_part(act, ps_z[:, h % 2, c0:], e[:, h, c0:]).then_inc(s["chain_done"], 1)

            def body(Q, beta, slot, kb, c0, diag, follows, first):
                if first:
                    chain(beta, c0, 0)
                    chain(beta, c0, 1)
                for h in range(H):
                    if h + 2 < H:
                        chain(beta, c0, h + 2)
                    elif follows is not None:
                        chain(beta + 1, follows[1], h - 2)
                    act.wait_ge(s["u_done"], beta * H + (h + 1))
                    act.activation(a[:, h, c0:], a[:, h, c0:], ACT.Exp).then_inc(s["exp_done"], 1)
                if follows is None:
                    act.wait_ge(s["o_done"], Q + 1)
                    act.wait_ge(s["mix_stored"], 16 * (Q + 1))
                    act.activation(mix[:].rearrange("p a t -> p (a t)"), ps_O[:].rearrange("p a t -> p (a t)"),
                                   ACT.Identity).then_inc(s["o_copied"], 1)
                    act.wait_ge(s["o_copied"], Q + 1)
                    act.dma_start(S["mixT"][6:8, :, Q * GROUP:(Q + 1) * GROUP].rearrange("a p t -> p a t"), mix[:]
                                  ).then_inc(s["mix_stored"], 16)
            blocks(act, body)
            act.wait_ge(s["mix_stored"], 16 * (GROUPS + 1))

        @block.gpsimd
        def _(pool):
            def body(Q, beta, slot, kb, c0, diag, follows, first):
                if diag:
                    for h in range(H):
                        pool.wait_ge(s["exp_done"], beta * H + (h + 1))
                        pool.tensor_tensor(a[:, h, c0:c0 + P], a[:, h, c0:c0 + P], K["before"][:], ALU.mult
                                           ).then_inc(s["a_masked"], 1)
            for Q in range(GROUPS):
                for j in (3, 2, 1, 0):
                    body(Q, first_beta[Q] + 3 - j, 0, 0, j * P, True, None, False)

        @block.vector
        def _(dve):
            dve.sem_inc(s["sp_done"], 2)

            def softplus_and_sigmoid(beta, c0, h, diag):
                dve.wait_ge(s["chain_done"], beta * H + (h + 1))
                last = dve.scalar_tensor_tensor(sp_[:, h, c0:], ps_z[:, h % 2, c0:], 0.0, e[:, h, c0:],
                                                ALU.max, ALU.add)
                if diag:
                    dve.drain()
                    dve.tensor_tensor(sp_[:, h, c0:c0 + P], sp_[:, h, c0:c0 + P], K["before"][:], ALU.mult)
                dve.scalar_tensor_tensor(a[:, h, c0:], ps_z[:, h % 2, c0:], 0.0, e[:, h, c0:],
                                         ALU.min, ALU.subtract).then_inc(s["sp_done"], 1)

            def body(Q, beta, slot, kb, c0, diag, follows, first):
                if first:
                    dve.wait_ge(s["q_loaded"], 16 * (Q + 1))
                    q = qT[:, Q % 2].rearrange("p a t -> p (a t)")
                    dve.tensor_scalar(q, q, HD ** -0.5, None, ALU.mult).then_inc(s["q_ready"], 1)
                    softplus_and_sigmoid(beta, c0, 0, True)
                    softplus_and_sigmoid(beta, c0, 1, True)
                for h in range(H):
                    dve.wait_ge(s["T_done"], beta * H + (h + 1))
                    dve.tensor_tensor(a[:, h, c0:], a[:, h, c0:], ps_C[:, h, c0:], ALU.subtract
                                      ).then_inc(s["u_done"], 1)
                    if h + 2 < H:
                        softplus_and_sigmoid(beta, c0, h + 2, diag)
                    elif follows is not None:
                        softplus_and_sigmoid(beta + 1, follows[1], h - 2, diag and c0 > 0)
            blocks(dve, body)


def stage_stick_samples(nc, K, IN, S):
    H, PAIRS = C_HEADS, 2
    BLOCKS = PAST // P
    COLS = DEC_B * H * DEC_T
    with ExitStack() as ctx:
        ctx.callback(nc.all_engine_barrier)
        sb = lambda name, shape: ctx.enter_context(nc.sbuf_tensor(name, shape, F32))
        ps = lambda name, shape: ctx.enter_context(nc.psum_tensor(name, shape, F32))
        q_new = sb("s_cqT", [P, PAIRS, P])
        k_new = sb("s_ckT", [P, PAIRS, P])
        v_new = sb("s_cv_new", [DEC_T, DEC_B, H * HD])
        q_diag = sb("s_cq_diag", [P, DEC_B, PAIRS, 2 * DEC_T])
        k_rows = sb("s_ck_block", [P, 2, DEC_B, H * HD])
        v_rows = sb("s_cv_block", [P, 2, DEC_B, H * HD])
        kT = sb("s_ckT_block", [P, 2, DEC_B, PAIRS, P])
        e = sb("s_stick_e", [P, COLS])
        sp_ = sb("s_stick_softplus", [P, COLS])
        a = sb("s_stick_weight", [P, COLS])
        mix = sb("s_mixC", [P, PAIRS, P])
        ps_K = ps("ps_s_kT", [P, DEC_B, PAIRS, P])
        ps_z = ps("ps_s_z", [P, COLS])
        ps_C = ps("ps_s_later", [P, COLS])
        ps_O = ps("ps_s_stick_out", [P, COLS])
        s = signals(nc, ctx, "stick_samples", "new_loaded q_ready zeroed kT_ps kT_ready_act kT_ready_dve z_done chain_done "
                             "sp_done T_done u_done exp_done a_masked pv_done o_copied mix_stored")
        k_loaded = [signal(nc, ctx, "stick_samples", f"s_ck_loaded{b}") for b in range(2)]
        v_loaded = [signal(nc, ctx, "stick_samples", f"s_cv_loaded{b}") for b in range(2)]
        block = ctx.enter_context(nc.Block())

        def cached(engine, body):
            with engine.Fori(0, BLOCKS // 2 - 1) as i:
                for r in range(2):
                    body(i * 2 + (1 + r), r, i, False)
            for r in range(2):
                body(BLOCKS - 1 + r, r, BLOCKS // 2 - 1, r == 1)

        @block.sync
        def _(sp):
            for dst, src in ((q_new, S["qkT"][QKT_CQ:QKT_CK, :, SEQ:TOKENS].rearrange("a p t -> p a t")),
                             (k_new, S["qkT"][QKT_CK:QKT_N, :, SEQ:TOKENS].rearrange("a p t -> p a t")),
                             (v_new, S["cv"][SEQ:TOKENS, :].rearrange("(b t) d -> t b d", b=DEC_B))):
                sp.dma_start(dst[:], src).then_inc(s["new_loaded"], 16)

            def body(n, slot, uses, last):
                at = bass.ds(n * -P + PAST, P)
                src = lambda name: IN[name][0][:, at].rearrange("b k h d -> k b (h d)")
                sp.wait_ge(s["kT_ps"], n)
                sp.dma_start(k_rows[:, slot], src("cache_c_k")).then_inc(k_loaded[slot], 16)
                sp.wait_ge(s["pv_done"], n)
                sp.dma_start(v_rows[:, slot], src("cache_c_v")).then_inc(v_loaded[slot], 16)
            cached(sp, body)
            sp.wait_ge(s["o_copied"], 1)
            sp.dma_start(S["mixT"][6:8, :, SEQ:TOKENS].rearrange("a p t -> p a t"), mix[:]
                         ).then_inc(s["mix_stored"], 16)
            sp.wait_ge(s["mix_stored"], 16)

        @block.tensor
        def _(pe):
            pe.sem_inc(s["kT_ps"], 2)
            pe.sem_inc(s["pv_done"], 1)

            def turn(n, slot, uses):
                pe.wait_ge(k_loaded[slot], uses * 16 + 16)
                pe.wait_ge(s["kT_ready_act"], n)
                pe.wait_ge(s["kT_ready_dve"], n)
                for b in range(DEC_B):
                    for p in range(PAIRS):
                        last = pe.transpose(ps_K[:, b, p, :], k_rows[:, slot, b, p * P:(p + 1) * P], K["ident"][:])
                last.then_inc(s["kT_ps"], 1)

            def z(n, slot):
                pe.wait_ge(s["kT_ready_act"], n + 1)
                pe.wait_ge(s["kT_ready_dve"], n + 1)
                pe.wait_ge(s["sp_done"], n)
                for b in range(DEC_B):
                    for p in range(PAIRS):
                        c0 = (b * PAIRS + p) * 2 * DEC_T
                        last = pe.matmul(ps_z[:, c0:c0 + 2 * DEC_T], kT[:, slot, b, p, :], q_diag[:, b, p, :],
                                         start=True, stop=True)
                last.then_inc(s["z_done"], 1)

            def pv(n, slot, first, last_block):
                for b in range(DEC_B):
                    for p in range(PAIRS):
                        c0 = (b * PAIRS + p) * 2 * DEC_T
                        v = (v_new[:, b, p * P:(p + 1) * P] if first else v_rows[:, slot, b, p * P:(p + 1) * P])
                        w = a[0:DEC_T if first else P, c0:c0 + 2 * DEC_T]
                        last = pe.matmul(ps_O[:, c0:c0 + 2 * DEC_T], v, w, start=(first and c0 == 0),
                                         stop=last_block, skip_group_check=True)
                last.then_inc(s["pv_done"], 1)

            pe.wait_ge(s["new_loaded"], 48)
            pe.wait_ge(s["q_ready"], 1)
            for b in range(DEC_B):
                for p in range(PAIRS):
                    c0 = (b * PAIRS + p) * 2 * DEC_T
                    last = pe.matmul(ps_z[0:DEC_T, c0:c0 + 2 * DEC_T], k_new[:, p, b * DEC_T:(b + 1) * DEC_T],
                                     q_diag[:, b, p, :], start=True, stop=True)
            last.then_inc(s["z_done"], 1)
            turn(1, 0, 0)
            pe.wait_ge(s["sp_done"], 1)
            pe.matmul(ps_C[:], K["later"][:], sp_[:], start=True, stop=True, skip_group_check=True
                      ).then_inc(s["T_done"], 1)
            z(1, 0)
            turn(2, 1, 0)
            pe.wait_ge(s["u_done"], 1)
            pe.matmul(ps_C[:], K["upto"][:], sp_[:], start=False, stop=True, skip_group_check=True)
            pe.wait_ge(s["a_masked"], 1)
            pv(0, 0, True, False)

            def body(n, slot, uses, last):
                pe.wait_ge(s["sp_done"], n + 1)
                pe.matmul(ps_C[:], K["later"][:], sp_[:], start=False, stop=True, skip_group_check=True
                          ).then_inc(s["T_done"], 1)
                if not last:
                    z(n + 1, 1 - slot)
                    if not (isinstance(n, int) and n == BLOCKS - 1):
                        turn(n + 2, slot, uses + 1)
                    pe.wait_ge(s["u_done"], n + 1)
                    pe.matmul(ps_C[:], K["upto"][:], sp_[:], start=False, stop=True, skip_group_check=True)
                pe.wait_ge(s["exp_done"], n + 1)
                pe.wait_ge(v_loaded[slot], uses * 16 + 16)
                pv(n, slot, False, last)
            cached(pe, body)

        halves = {"act": slice(0, DEC_B // 2), "dve": slice(DEC_B // 2, DEC_B)}

        @block.scalar
        def _(act):
            act.preload_act_table_set(LOG_EXP_TABLES)
            act.sem_inc(s["kT_ready_act"], 1)

            def copy_kT(n, slot):
                act.wait_ge(s["kT_ps"], n + 2)
                act.activation(kT[:, slot, halves["act"]].rearrange("p b a k -> p (b a k)"),
                               ps_K[:, halves["act"]].rearrange("p b a k -> p (b a k)"), ACT.Identity
                               ).then_inc(s["kT_ready_act"], 1)

            def chain(n, rows):
                act.wait_ge(s["z_done"], n + 1)
                softplus_part(act, ps_z[0:rows], e[0:rows]).then_inc(s["chain_done"], 1)

            chain(0, DEC_T)
            copy_kT(1, 0)
            chain(1, P)
            act.wait_ge(s["u_done"], 1)
            act.activation(a[0:DEC_T], a[0:DEC_T], ACT.Exp).then_inc(s["exp_done"], 1)
            copy_kT(2, 1)

            def body(n, slot, uses, last):
                if not last:
                    chain(n + 1, P)
                act.wait_ge(s["u_done"], n + 1)
                act.activation(a[:], a[:], ACT.Exp).then_inc(s["exp_done"], 1)
                if not last and not (isinstance(n, int) and n == BLOCKS - 1):
                    copy_kT(n + 2, slot)
            cached(act, body)

        @block.gpsimd
        def _(pool):
            pool.memset(q_diag[:], 0.0)
            pool.memset(sp_[:], 0.0).then_inc(s["zeroed"], 1)
            pool.wait_ge(s["exp_done"], 1)
            cols = lambda t: t[0:DEC_T].rearrange("p (c i) -> p c i", i=DEC_T)
            pool.tensor_tensor(cols(a), cols(a), K["before"][0:DEC_T, 0:DEC_T].unsqueeze(1).to_broadcast(
                [DEC_T, COLS // DEC_T, DEC_T]), ALU.mult).then_inc(s["a_masked"], 1)

        @block.vector
        def _(dve):
            dve.sem_inc(s["kT_ready_dve"], 1)
            dve.wait_ge(s["new_loaded"], 48)
            dve.wait_ge(s["zeroed"], 1)
            for h2 in range(2):
                rows = slice(h2 * HD, (h2 + 1) * HD)
                for p in range(PAIRS):
                    last = dve.tensor_scalar(q_diag[rows, :, p, h2 * DEC_T:(h2 + 1) * DEC_T],
                                             q_new[rows, p, :].rearrange("p (b t) -> p b t", b=DEC_B),
                                             HD ** -0.5, None, ALU.mult)
            last.then_inc(s["q_ready"], 1)

            def copy_kT(n, slot):
                dve.wait_ge(s["kT_ps"], n + 2)
                dve.tensor_copy(kT[:, slot, halves["dve"]].rearrange("p b a k -> p (b a k)"),
                                ps_K[:, halves["dve"]].rearrange("p b a k -> p (b a k)")
                                ).then_inc(s["kT_ready_dve"], 1)

            def softplus_and_sigmoid(n, rows, masked):
                dve.wait_ge(s["chain_done"], n + 1)
                if not masked:
                    dve.wait_ge(s["pv_done"], n + 1)
                dve.scalar_tensor_tensor(sp_[0:rows], ps_z[0:rows], 0.0, e[0:rows], ALU.max, ALU.add)
                if masked:
                    dve.drain()
                    cols = sp_[0:rows].rearrange("p (c i) -> p c i", i=DEC_T)
                    dve.tensor_tensor(cols, cols, K["before"][0:DEC_T, 0:DEC_T].unsqueeze(1).to_broadcast(
                        [DEC_T, COLS // DEC_T, DEC_T]), ALU.mult)
                dve.scalar_tensor_tensor(a[0:rows], ps_z[0:rows], 0.0, e[0:rows], ALU.min, ALU.subtract
                                         ).then_inc(s["sp_done"], 1)

            def less_later(n, rows):
                dve.wait_ge(s["T_done"], n + 1)
                dve.tensor_tensor(a[0:rows], a[0:rows], ps_C[0:rows], ALU.subtract).then_inc(s["u_done"], 1)

            softplus_and_sigmoid(0, DEC_T, True)
            copy_kT(1, 0)
            less_later(0, DEC_T)
            copy_kT(2, 1)
            softplus_and_sigmoid(1, P, False)

            def body(n, slot, uses, last):
                less_later(n, P)
                if not last:
                    if not (isinstance(n, int) and n == BLOCKS - 1):
                        copy_kT(n + 2, slot)
                    softplus_and_sigmoid(n + 1, P, False)
            cached(dve, body)
            dve.wait_ge(s["pv_done"], BLOCKS + 2)
            for h2 in range(2):
                rows = slice(h2 * HD, (h2 + 1) * HD)
                src = ps_O[rows].rearrange("p (b a h t) -> p a b h t", b=DEC_B, a=PAIRS, h=2)
                for p in range(PAIRS):
                    last = dve.tensor_copy(mix[rows, p, :].rearrange("p (b t) -> p b t", b=DEC_B),
                                           src[:, p, :, h2, :])
            last.then_inc(s["o_copied"], 1)


def same_block(pool, view, first, size, fill):
    n, inner = view.shape[1], view.shape[2]
    pool.affine_select(out=view, in_=view, compare_op=ALU.is_ge, fill=fill, base=-first,
                       pattern=[[-size, n], [0, inner]], channel_multiplier=1)
    pool.drain()
    pool.affine_select(out=view, in_=view, compare_op=ALU.is_ge, fill=fill, base=first + size - 1,
                       pattern=[[size, n], [0, inner]], channel_multiplier=-1)
    pool.drain()


def stage_delta(nc, K, IN, OUT, S):
    TILES = SEQ // P
    H, J, C = B_HEADS, B_HEADS // 2, HD
    HH = H // 2
    W = H * HD
    LEVELS = 6
    S_LEVELS = 4
    GATE = {0: slice(0, H), 1: slice(H, 2 * H)}
    BETA, KBE, KD, QG = range(4)
    with ExitStack() as ctx:
        ctx.callback(nc.all_engine_barrier)
        sb = lambda name, shape: ctx.enter_context(nc.sbuf_tensor(name, shape, F32))
        ps = lambda name, shape: ctx.enter_context(nc.psum_tensor(name, shape, F32))
        chT = sb("d_convT", [P, 2, CONV_CHUNKS, P])
        zba = sb("d_zba", [P, 2, ZBA_W])
        squares = sb("d_squares", [P, H, P])
        soft_in, soft_e, soft = (sb(f"d_soft_{n}", [P, 2 * H]) for n in ("in", "e", "out"))
        logs = sb("d_norm_logs", [P, 2 * H])
        g, g_seq = sb("d_g", [P, H]), sb("d_g_by_seq", [P, 2, DEC_B, J])
        sums = sb("d_sums", [P, 2 * H + DEC_B * J])
        minus_gc = sb("d_minus_gc", [P, H])
        fac_log, fac = sb("d_factor_logs", [P, 4, H]), sb("d_factors", [P, 2, 4, H])
        decay = sb("d_decay", [P, 2, DEC_B, J])
        diag = sb("d_log_diag", [P, H, 2, C])
        wgt = sb("d_weights", [P, H, 2, C])
        mats = sb("d_matrices", [P, 2, H, 2, C])
        X = sb("d_inverse", [P, H, 2, C])
        Y = sb("d_LX", [P, H, C])
        v_beta, k_beta, k_decay = (sb(f"d_{n}", [P, 2, W]) for n in ("v_beta", "k_beta", "k_decay"))
        wT = sb("d_wT", [P, J, P])
        v_new = sb("d_v_new", [P, W])
        state, faded = sb("d_state", [P, J, P]), sb("d_state_faded", [P, J, P])
        out, out_sq = sb("d_out", [P, W]), sb("d_out_sq", [P, W])
        out_ss, out_r = sb("d_out_ss", [P, H]), sb("d_out_r", [P, H])
        gate = sb("d_gate", [P, 2, W])
        qT = sb("d_qT", [P, 2, J, P])
        zero = sb("d_zero", [P, H])
        mix = sb("d_mix", [P, J, P])
        s_state, s_faded = sb("d_s_state", [P, DEC_B, J, P]), sb("d_s_faded", [P, DEC_B, J, P])
        s_wT, s_qT = sb("d_s_wT", [P, DEC_B, J, P]), sb("d_s_qT", [P, DEC_B, J, P])
        s_k_decay = sb("d_s_k_decay", [P, DEC_B, W])
        ident = sb("d_ident", [P, C])
        expo_mask = sb("d_exponent_mask", [P, 2, 2, C])
        level = sb("d_level_masks", [P, LEVELS, C])
        level_1T = sb("d_level_1T", [P, C])
        run_sum, seq_sum = sb("d_run_sum", [P, 2, P]), sb("d_seq_sum", [P, 2, P])
        in_seq = sb("d_in_seq", [P, 2, DEC_B])
        eps = sb("d_eps", [P, 1])
        a_log, dt_bias, norm_w = sb("d_a_log", [P, H]), sb("d_dt_bias", [P, H]), sb("d_norm_w", [P, HD])
        ps_kv = ps("ps_d_kv", [P, 2, 512])
        ps_A = ps("ps_d_qk", [P, 2, 512])
        ps_Z = ps("ps_d_Z", [P, 2, 512])
        ps_Y = ps("ps_d_Y", [P, 2, 512])
        ps_s = ps_A[:, 1, HH * 2 * C:]
        SS, GC, SEQ_SUM = 0, 12, 24
        s = signals(nc, ctx, "delta", "masks_ready pe_passed rows_loaded a_log_exp squares_ready soft_in_ready soft_ready "
                             "kv_done qk_done ss_done logs_ready g_ready sums_done fac_log_ready fac_ready "
                             "diag_ready G_done0 G_done1 expo_ready0 expo_ready1 wgt_ready0 wgt_ready1 "
                             "mats_ready0 mats_ready1 X_ready0 X_ready1 Y_done0 Y_done1 "
                             "Y_ready0 Y_ready1 Z_done0 Z_done1 kv_ready wT_done wT_ready v_done "
                             "v_ready state_done state_ready out_done out_ss_ready out_r_ready gate_ready "
                             "out_ready outT_done qT_ready mix_ready s_state_loaded s_operands s_k_decay_ready "
                             "state_stored")
        loaded = [signal(nc, ctx, "delta", f"d_loaded{b}") for b in range(2)]
        mix_stored = signal(nc, ctx, "delta", "d_mix_stored")
        block = ctx.enter_context(nc.Block())
        halves = [slice(0, HH), slice(HH, H)]
        by_head = lambda t: t.rearrange("p (h d) -> p h d", d=HD)

        def tiles(engine, body):
            body(0, 0, 0, "prompt")
            with engine.Fori(0, TILES // 2 - 1) as i:
                body(i * 2 + 1, 1, i, "prompt")
                body(i * 2 + 2, 0, i + 1, "prompt")
            body(TILES - 1, 1, TILES // 2 - 1, "sample")
            body(TILES, 0, TILES // 2, None)

        def ahead(prepare, n, slot, uses, follows):
            if follows is not None:
                prepare(n + 1, 1 - slot, uses + slot, follows == "sample")

        def flat(t):
            return t.rearrange("p h a c -> p (h a c)")

        def at(h):
            return h % 2 * J + h // 2

        @block.gpsimd
        def _(pool):
            for row, src in ((a_log, "b_a_log"), (dt_bias, "b_dt_bias"), (norm_w, "b_norm_w")):
                pool.dma_start(row[:], row_broadcast(IN[src])).then_inc(s["rows_loaded"], 16)
            for t in (ident, level, in_seq, run_sum, seq_sum):
                pool.memset(t[:], 1.0)
            for t in (zero, expo_mask, level_1T, state, s_state, s_wT, s_qT):
                pool.memset(t[:], 0.0)
            pool.memset(eps[:], RMS_EPS)
            pool.drain()
            for c in range(2):
                r = slice(c * C, (c + 1) * C)
                pool.affine_select(out=ident[r], in_=ident[r], compare_op=ALU.is_equal, fill=0.0, base=0,
                                   pattern=[[-1, C]], channel_multiplier=1)
                pool.drain()
                for sample in range(2):
                    for kind in range(2):
                        m = expo_mask[r, sample, kind, :]
                        pool.affine_select(out=m, in_=m, compare_op=ALU.is_ge, fill=NEG, base=-kind,
                                           pattern=[[1, C]], channel_multiplier=-1)
                        pool.drain()
                        if sample:
                            same_block(pool, m.rearrange("p (b t) -> p b t", t=DEC_T), 0, DEC_T, NEG)
                for l in range(LEVELS):
                    b = 1 << l
                    m = level[r, l, :].rearrange("p (n a t) -> p n a t", a=2, t=b)
                    pool.memset(m[:, :, 1, :], 0.0)
                    same_block(pool, m[:, :, 0, :], 0, 2 * b, 0.0)
                    pool.affine_select(out=m[:, :, 0, :], in_=m[:, :, 0, :], compare_op=ALU.is_ge, fill=0.0,
                                       base=-b, pattern=[[-2 * b, C // (2 * b)], [0, b]], channel_multiplier=1)
                    pool.drain()
                m = level_1T[r].rearrange("p (n a) -> p n a", a=2)[:, :, 1]
                pool.affine_select(out=m, in_=m, compare_op=ALU.not_equal, fill=1.0, base=0,
                                   pattern=[[-2, C // 2]], channel_multiplier=1)
                pool.drain()
            for sample, size in ((0, C), (1, DEC_T)):
                m = in_seq[:, sample, 0:P // size].unsqueeze(2)
                same_block(pool, m, 0, size, 0.0)
                for t in (run_sum, seq_sum):
                    same_block(pool, t[:, sample].rearrange("p (b t) -> p b t", t=size), 0, size, 0.0)
                pool.affine_select(out=run_sum[:, sample], in_=run_sum[:, sample], compare_op=ALU.is_ge,
                                   fill=0.0, base=0, pattern=[[1, P]], channel_multiplier=-1)
            pool.drain()
            pool.sem_inc(s["masks_ready"], 1)
            pool.wait_ge(s["rows_loaded"], 48)

            def prepare(n, slot, uses, sample):
                pool.wait_ge(loaded[slot], uses * 32 + 32)
                pool.wait_ge(s["ss_done"], n + 1)
                pool.tensor_tensor(squares[:].rearrange("p f t -> p (f t)"),
                                   chT[:, slot, 0:H].rearrange("p f t -> p (f t)"),
                                   chT[:, slot, 0:H].rearrange("p f t -> p (f t)"), ALU.mult
                                   ).then_inc(s["squares_ready"], 1)
                pool.wait_ge(s["g_ready"], n + 1)
                pool.tensor_tensor(soft_in[:, GATE[0]], zero[:], zba[:, slot, W:W + H], ALU.subtract)
                pool.tensor_tensor(soft_in[:, GATE[1]], zba[:, slot, W + H:], dt_bias[:], ALU.add
                                   ).then_inc(s["soft_in_ready"], 1)
                pool.wait_ge(s["out_ready"], n + 1)
                pool.wait_ge(s["out_done"], n + 1)
                pool.tensor_tensor(by_head(gate[:, slot]), by_head(zba[:, slot, 0:W]),
                                   norm_w[:].unsqueeze(1).to_broadcast([P, H, HD]), ALU.mult
                                   ).then_inc(s["gate_ready"], 1)
                if not sample:
                    pool.tensor_copy(qT[:, slot].rearrange("p j t -> p (j t)"),
                                     chT[:, slot, 0:J].rearrange("p j t -> p (j t)")).then_inc(s["qT_ready"], 1)
                else:
                    for b in range(DEC_B):
                        t = slice(b * DEC_T, (b + 1) * DEC_T)
                        pool.tensor_copy(s_qT[:, b, :, t], chT[:, slot, 0:J, t])
                    pool.drain()
                    pool.sem_inc(s["qT_ready"], 1)
            pool.sem_inc(s["ss_done"], 1)
            pool.sem_inc(s["g_ready"], 1)
            pool.sem_inc(s["out_done"], 2)
            pool.sem_inc(s["out_ready"], 2)
            prepare(0, 0, 0, False)
            tiles(pool, lambda *tile: ahead(prepare, *tile))

        @block.sync
        def _(sp):
            sp.wait_ge(s["masks_ready"], 1)
            for hh in range(2):
                r = slice(hh * HD, (hh + 1) * HD)
                src = IN["state_b_ssm"][0].rearrange("b (j a) k v -> a k (b j) v", a=2)[hh]
                sp.dma_start(s_state[r].rearrange("p b j v -> p (b j) v")[:, :, r], src
                             ).then_inc(s["s_state_loaded"], 16)

            def load(n, slot):
                rows = bass.ds(n * P, P)
                sp.dma_start(chT[:, slot], S["convT"][:, :, rows].rearrange("f p t -> p f t")
                             ).then_inc(loaded[slot], 16)
                sp.dma_start(zba[:, slot], S["zba"][rows, :]).then_inc(loaded[slot], 16)

            sp.sem_inc(mix_stored, 16)
            load(0, 0)
            load(1, 1)

            def body(n, slot, uses, follows):
                if follows is not None and not (isinstance(n, int) and n == TILES - 1):
                    sp.wait_ge(s["qk_done"], n + 1)
                    sp.wait_ge(s["qT_ready"], n + 1)
                    load(n + 2, slot)
                sp.wait_ge(s["mix_ready"], n + 3)
                sp.dma_start(S["mixT"][A_GROUP:A_GROUP + J, :, bass.ds(n * P, P)].rearrange("j p t -> p j t"),
                             mix[:]).then_inc(mix_stored, 16)
            tiles(sp, body)
            sp.wait_ge(s["state_ready"], 1 + 2 * TILES + DEC_B)
            for hh in range(2):
                r = slice(hh * HD, (hh + 1) * HD)
                dst = OUT["p_b_ssm"][0, 0].rearrange("(j a) k v -> a k j v", a=2)[hh]
                sp.dma_start(dst, state[r, :, r]).then_inc(s["state_stored"], 16)
                dst = OUT["s_b_ssm"][0].rearrange("b (j a) k v -> a k (b j) v", a=2)[hh]
                sp.dma_start(dst, s_state[r].rearrange("p b j v -> p (b j) v")[:, :, r]
                             ).then_inc(s["state_stored"], 16)
            sp.wait_ge(s["state_stored"], 64)
            sp.wait_ge(mix_stored, 16 * (TILES + 2))

        @block.tensor
        def _(pe):
            def wait(name, value):
                pe.wait_ge(s[name], value)
                pe.sem_inc(s["pe_passed"], 1)

            def quadrants(outs, lhs, rhs, half):
                for j in range(J):
                    for c in range(2):
                        r = slice(c * C, (c + 1) * C)
                        i = half * J + j
                        last = pe.matmul(outs(r, j), lhs(r, i), rhs(r, i), start=True, stop=True)
                return last

            def norms(n, slot, uses, sample):
                pe.wait_ge(s["squares_ready"], n + 1)
                for f in range(H):
                    last = pe.matmul(ps_s[:, SS + 2 * f:SS + 2 * f + 2], squares[:, f, :], in_seq[:, 0, 0:2],
                                     start=True, stop=True)
                last.then_inc(s["ss_done"], 1)

            def sums_and_kv(n, slot, uses, sample):
                pe.wait_ge(loaded[slot], uses * 32 + 32)
                pe.wait_ge(s["out_ss_ready"], n + 1)
                for f in range(2):
                    for j in range(J):
                        last = pe.transpose(ps_kv[:, f, j * P:(j + 1) * P], chT[:, slot, (f + 1) * J + j, :],
                                            K["ident"][:])
                last.then_inc(s["kv_done"], 1)
                kind, seqs = int(sample), DEC_B if sample else 2
                pe.wait_ge(s["g_ready"], n + 2)
                pe.wait_ge(s["logs_ready"], n + 1)
                pe.matmul(ps_s[:, GC:GC + H], run_sum[:, kind, :], g[:], start=True, stop=True)
                pe.matmul(ps_s[:, GC + H:GC + 2 * H], seq_sum[:, kind, :], g[:], start=True, stop=True)
                for hh in range(2):
                    r = slice(hh * HD, (hh + 1) * HD)
                    last = pe.matmul(ps_s[r, SEQ_SUM:SEQ_SUM + seqs * J], K["ones"][:, r],
                                     g_seq[:, hh, 0:seqs].rearrange("p b j -> p (b j)"), start=True, stop=True)
                last.then_inc(s["sums_done"], 1)

            def products(n, slot, uses, sample):
                pe.wait_ge(s["mix_ready"], n + 1)
                wait("fac_log_ready", n + 1)
                for h in range(H):
                    r = slice(h % 2 * HD, h % 2 * HD + HD)
                    for c in range(2):
                        cols = slice(c * C, (c + 1) * C)
                        o = h // 2 * 2 * C
                        last = pe.matmul(ps_A[cols, h % 2, o:o + 2 * C].rearrange("p (a t) -> p a t", a=2),
                                         chT[r, slot, J + h // 2, cols], chT[r, slot, h // 2:2 * J:J, cols],
                                         start=True, stop=True)
                last.then_inc(s["qk_done"], 1)
                pe.wait_ge(s["diag_ready"], n + 1)
                pe.wait_ge(s["kv_ready"], n + 1)
                for half in range(2):
                    pe.matmul(ps_kv[:, half, 0:HH * 2 * C], seq_sum[:, 0, :], flat(diag[:, halves[half]]),
                              start=True, stop=True).then_inc(s[f"G_done{half}"], 1)

            def turn_L(n, slot, uses, sample):
                for half in range(2):
                    wait(f"mats_ready{half}", n + 1)
                    if half == 0:
                        wait("mats_ready1", n + 1)
                    quadrants(lambda r, j: ps_A[r, half, j * C:(j + 1) * C],
                              lambda r, i: mats[r, slot, i, 1, :], lambda r, i: K["ident"][r, r], half
                              ).then_inc(s[f"Y_done{half}"], 1)

            def turn_out(n):
                pe.wait_ge(s["out_ready"], n + 3)
                for j in range(J):
                    last = pe.transpose(ps_A[:, 0, j * P:(j + 1) * P], out[:, j * P:(j + 1) * P], K["ident"][:])
                last.then_inc(s["outT_done"], 1)

            def body(n, slot, uses, follows):
                sample = follows is None
                tile = (n, slot, uses, follows)
                levels = S_LEVELS if sample else LEVELS
                X_at, Y_at = n * LEVELS, n * (LEVELS - 1)
                for l in range(1, levels):
                    for half in range(2):
                        wait(f"X_ready{half}", X_at + l)
                        quadrants(lambda r, j: ps_Y[r, half, j * C:(j + 1) * C],
                                  lambda r, i: mats[r, slot, i, 1, :], lambda r, i: X[r, i, 0, :], half
                                  ).then_inc(s[f"Y_done{half}"], 1)
                    for half in range(2):
                        wait(f"Y_ready{half}", Y_at + l)
                        if l < levels - 1:
                            quadrants(lambda r, j: ps_Z[r, half, j * 2 * C:j * 2 * C + C],
                                      lambda r, i: X[r, i, 1, :], lambda r, i: Y[r, i, :], half)
                        quadrants(lambda r, j: ps_Z[r, half, j * 2 * C + C:(j + 1) * 2 * C],
                                  lambda r, i: Y[r, i, :], lambda r, i: X[r, i, 1, :], half
                                  ).then_inc(s[f"Z_done{half}"], 1)
                    if l == 1:
                        ahead(norms, *tile)
                    if l == 2:
                        ahead(sums_and_kv, *tile)
                    if l == 3 and not (isinstance(n, int) and n == 0):
                        turn_out(n - 1)
                    if l == 4:
                        ahead(products, *tile)
                for half in range(2):
                    wait(f"X_ready{half}", X_at + levels)
                wait("kv_ready", n + 1)
                for h in range(H):
                    rows = slice(h % 2 * HD, h % 2 * HD + HD)
                    for c in range(2):
                        r = slice(c * C, (c + 1) * C)
                        last = pe.matmul(ps_Y[rows, c, h // 2 * C:(h // 2 + 1) * C],
                                         k_beta[r, slot, h * HD:(h + 1) * HD], X[r, at(h), 1, :],
                                         start=True, stop=True)
                last.then_inc(s["wT_done"], 1)
                for h in range(H):
                    for c in range(2):
                        r = slice(c * C, (c + 1) * C)
                        pe.matmul(ps_Z[r, 0, h * HD:(h + 1) * HD], X[r, at(h), 1, :],
                                  v_beta[r, slot, h * HD:(h + 1) * HD],
                                  start=(h == 0), stop=False, skip_group_check=True)
                if follows is not None:
                    for half in range(2):
                        wait(f"expo_ready{half}", n + 2)

                def intra(c):
                    r = slice(c * C, (c + 1) * C)
                    for h in range(H):
                        last = pe.matmul(ps_kv[r, 1, h * HD:(h + 1) * HD], mats[r, slot, at(h), 0, :],
                                         v_new[r, h * HD:(h + 1) * HD], start=True, stop=True)
                    return last

                pe.wait_ge(s["wT_ready"], n + 1)
                pe.wait_ge(s["qT_ready"], n + 1)
                if not sample:
                    for c in range(2):
                        r = slice(c * C, (c + 1) * C)
                        pe.wait_ge(s["state_ready"], n * 2 + (c + 1))
                        for j in range(J):
                            last = pe.matmul(ps_Z[r, 0, j * P:(j + 1) * P], wT[:, j, r], state[:, j, :],
                                             start=False, stop=True, skip_group_check=True)
                        last.then_inc(s["v_done"], 1)
                        for j in range(J):
                            pe.matmul(ps_kv[r, 0, j * P:(j + 1) * P], qT[:, slot, j, r], state[:, j, :],
                                      start=True, stop=True)
                        wait("v_ready", n * 2 + (c + 1))
                        for j in range(J):
                            last = pe.matmul(ps_Z[:, 1, j * P:(j + 1) * P], k_decay[r, slot, j * P:(j + 1) * P],
                                             v_new[r, j * P:(j + 1) * P], start=True, stop=True)
                        last.then_inc(s["state_done"], 1)
                        if c == 1:
                            ahead(turn_L, *tile)
                        last = intra(c)
                    last.then_inc(s["out_done"], 1)
                else:
                    pe.wait_ge(s["s_state_loaded"], 32)
                    for b in range(DEC_B):
                        for j in range(J):
                            last = pe.matmul(ps_Z[:, 0, j * P:(j + 1) * P], s_wT[:, b, j, :], s_state[:, b, j, :],
                                             start=False, stop=(b == DEC_B - 1), skip_group_check=True)
                    last.then_inc(s["v_done"], 2)
                    for j in range(J):
                        for b in range(DEC_B):
                            pe.matmul(ps_kv[:, 0, j * P:(j + 1) * P], s_qT[:, b, j, :], s_state[:, b, j, :],
                                      start=(b == 0), stop=(b == DEC_B - 1))
                    pe.wait_ge(s["v_ready"], n * 2 + 2)
                    intra(0)
                    intra(1).then_inc(s["out_done"], 1)
                    pe.wait_ge(s["s_k_decay_ready"], 1)
                    for b in range(DEC_B):
                        if b >= 2:
                            pe.wait_ge(s["state_ready"], 1 + 2 * TILES + b - 1)
                        for j in range(J):
                            last = pe.matmul((ps_Z[:, 1] if b % 2 else ps_Y[:, 0])[:, j * P:(j + 1) * P],
                                             s_k_decay[:, b, j * P:(j + 1) * P], v_new[:, j * P:(j + 1) * P],
                                             start=True, stop=True)
                        last.then_inc(s["state_done"], 1)
                    turn_out(n)

            first = (0, 0, 0, False)
            norms(*first)
            sums_and_kv(*first)
            products(*first)
            turn_L(*first)
            tiles(pe, body)

        @block.scalar
        def _(act):
            act.preload_act_table_set(LOG_EXP_TABLES)
            act.sem_inc(s["out_ss_ready"], 2)
            act.sem_inc(s["mix_ready"], 2)

            def softplus(n, slot, uses, sample):
                act.wait_ge(s["soft_in_ready"], n + 1)
                softplus_part(act, soft_in[:], soft_e[:]).then_inc(s["soft_ready"], 1)

            def norm_logs(n, slot, uses, sample):
                act.wait_ge(s["ss_done"], n + 2)
                act.activation(logs[:], ps_s[:, SS:SS + 2 * H], ACT.Ln, bias=eps[:, 0:1]).then_inc(s["logs_ready"], 1)

            def factors(n, slot, uses, sample):
                act.wait_ge(s["fac_log_ready"], n + 1)
                act.activation(decay[:, slot].rearrange("p b j -> p (b j)"), sums[:, 2 * H:], ACT.Exp)
                act.activation(fac[:, slot].rearrange("p k h -> p (k h)"), fac_log[:].rearrange("p k h -> p (k h)"),
                               ACT.Exp).then_inc(s["fac_ready"], 1)

            def weights(n, half):
                act.wait_ge(s[f"expo_ready{half}"], n + 1)
                for j in range(J):
                    w = wgt[:, half * J + j].rearrange("p a c -> p (a c)")
                    h = 2 * j + half
                    last = act.activation(w, w, ACT.Exp, bias=minus_gc[:, h:h + 1])
                last.then_inc(s[f"wgt_ready{half}"], 1)

            def norm_out(n):
                act.wait_ge(s["out_ss_ready"], n + 3)
                act.activation(out_r[:], out_ss[:], ACT.Ln, bias=eps[:, 0:1], scale=1.0 / HD)
                act.drain()
                act.activation(out_r[:], out_r[:], ACT.Exp, scale=-0.5).then_inc(s["out_r_ready"], 1)

            def copy_mix(n):
                act.wait_ge(s["outT_done"], n + 1)
                act.wait_ge(mix_stored, n * 16 + 16)
                act.activation(mix[:].rearrange("p j t -> p (j t)"), ps_A[:, 0, 0:W], ACT.Identity
                               ).then_inc(s["mix_ready"], 1)

            def body(n, slot, uses, follows):
                tile = (n, slot, uses, follows)
                first = isinstance(n, int) and n == 0
                ahead(softplus, *tile)
                ahead(norm_logs, *tile)
                if not first:
                    norm_out(n - 1)
                ahead(factors, *tile)
                if not first:
                    copy_mix(n - 1)
                act.wait_ge(s["wT_done"], n + 1)
                if follows is None:
                    for b in range(DEC_B):
                        t = slice(b * DEC_T, (b + 1) * DEC_T)
                        c, b_t = b // 4, slice(b % 4 * DEC_T, (b % 4 + 1) * DEC_T)
                        last = act.activation(s_wT[:, b, :, t], ps_Y[:, c, 0:J * C].rearrange(
                            "p (j t) -> p j t", j=J)[:, :, b_t], ACT.Identity)
                else:
                    last = act.activation(wT[:].rearrange("p j (c t) -> p c j t", c=2),
                                          ps_Y[:, :, 0:J * C].rearrange("p c (j t) -> p c j t", j=J), ACT.Identity)
                last.then_inc(s["wT_ready"], 1)
                for c in range(2):
                    r = slice(c * C, (c + 1) * C)
                    if follows is not None:
                        weights(n + 1, c)
                    act.wait_ge(s["v_done"], n * 2 + (c + 1))
                    act.activation(v_new[r], ps_Z[r, 0, 0:W], ACT.Identity).then_inc(s["v_ready"], 1)
            act.wait_ge(s["masks_ready"], 1)
            act.wait_ge(s["rows_loaded"], 48)
            act.activation(a_log[:], a_log[:], ACT.Exp).then_inc(s["a_log_exp"], 1)
            first = (0, 0, 0, False)
            softplus(*first)
            norm_logs(*first)
            factors(*first)
            weights(0, 0)
            weights(0, 1)
            tiles(act, body)
            norm_out(TILES)
            copy_mix(TILES)

        @block.vector
        def _(dve):
            dve.wait_ge(s["rows_loaded"], 48)
            dve.wait_ge(s["masks_ready"], 1)
            dve.memset(sums[:], 0.0).then_inc(s["state_ready"], 1)

            def wide(col, d=C):
                return col.unsqueeze(2).to_broadcast([P, col.shape[1], d])

            def decays(n, slot, uses, sample):
                kind, seqs = int(sample), DEC_B if sample else 2
                dve.wait_ge(s["soft_ready"], n + 1)
                dve.scalar_tensor_tensor(soft[:], soft_in[:], 0.0, soft_e[:], ALU.max, ALU.add)
                dve.drain()
                dve.tensor_tensor(g[:], soft[:, GATE[1]], a_log[:], ALU.mult)
                dve.drain()
                for hh in range(2):
                    last = dve.tensor_tensor(g_seq[:, hh, 0:seqs],
                                             g[:].rearrange("p (j a) -> p a j", a=2)[:, hh].unsqueeze(1).to_broadcast(
                                                 [P, seqs, J]),
                                             in_seq[:, kind, 0:seqs].unsqueeze(2).to_broadcast([P, seqs, J]), ALU.mult)
                last.then_inc(s["g_ready"], 1)

            def factor_logs(n, slot, uses, sample):
                seqs = DEC_B if sample else 2
                dve.wait_ge(s["logs_ready"], n + 1)
                dve.tensor_scalar(logs[:, GATE[0]], logs[:, GATE[0]], -0.5, float(-0.5 * np.log(HD)), ALU.mult, ALU.add)
                dve.tensor_scalar(logs[:, GATE[1]], logs[:, GATE[1]], -0.5, None, ALU.mult)
                dve.tensor_scalar(fac_log[:, BETA], soft[:, GATE[0]], -1.0, None, ALU.mult)
                dve.wait_ge(s["sums_done"], n + 1)
                dve.tensor_copy(sums[:, 0:2 * H + seqs * J], ps_s[:, GC:GC + 2 * H + seqs * J])
                dve.drain()
                gc, whole = sums[:, GATE[0]], sums[:, GATE[1]]
                dve.tensor_tensor(fac_log[:, QG], gc, logs[:, GATE[0]], ALU.add)
                dve.tensor_tensor(fac_log[:, KBE], gc, logs[:, GATE[1]], ALU.add)
                dve.tensor_tensor(minus_gc[:], logs[:, GATE[1]], gc, ALU.subtract)
                dve.drain()
                dve.tensor_tensor(fac_log[:, KBE], fac_log[:, KBE], fac_log[:, BETA], ALU.add)
                dve.tensor_tensor(fac_log[:, KD], minus_gc[:], whole, ALU.add).then_inc(s["fac_log_ready"], 1)
                dve.drain()
                for half in range(2):
                    for a, f in enumerate((QG, KBE)):
                        row = fac_log[:, f].rearrange("p (j a) -> p a j", a=2)[:, half]
                        last = dve.tensor_tensor(diag[:, halves[half], a, :],
                                                 ident[:].unsqueeze(1).to_broadcast([P, HH, C]), wide(row), ALU.mult)
                last.then_inc(s["diag_ready"], 1)

            def scale_kv(n, slot, uses, sample):
                dve.wait_ge(s["fac_ready"], n + 1)
                dve.wait_ge(s["kv_done"], n + 1)
                k_rows, v_rows = (by_head(ps_kv[:, f, 0:W]) for f in range(2))
                factor = lambda f: wide(fac[:, slot, f], HD)
                dve.tensor_tensor(by_head(v_beta[:, slot]), v_rows, factor(BETA), ALU.mult)
                dve.scalar_tensor_tensor(by_head(k_beta[:, slot]), k_rows, -1.0, factor(KBE), ALU.mult, ALU.mult)
                dve.tensor_tensor(by_head(k_decay[:, slot]), k_rows, factor(KD), ALU.mult
                                  ).then_inc(s["kv_ready"], 1)
                if sample:
                    dve.drain()
                    for b in range(DEC_B):
                        last = dve.tensor_scalar(s_k_decay[:, b], k_decay[:, slot], in_seq[:, 1, b:b + 1], None, ALU.mult)
                    last.then_inc(s["s_k_decay_ready"], 1)

            def exponents(n, slot, uses, sample):
                for half in range(2):
                    dve.wait_ge(s[f"G_done{half}"], n + 1)
                    dve.tensor_tensor(wgt[:, halves[half]].rearrange("p h a c -> p h (a c)"),
                                      ps_kv[:, half, 0:HH * 2 * C].rearrange("p (h x) -> p h x", h=HH),
                                      expo_mask[:, int(sample)].rearrange("p a c -> p (a c)").unsqueeze(1).to_broadcast(
                                          [P, HH, 2 * C]), ALU.add).then_inc(s[f"expo_ready{half}"], 1)

            def matrices(n, slot, uses, sample):
                for half in range(2):
                    dve.wait_ge(s[f"wgt_ready{half}"], n + 1)
                    dve.wait_ge(s["qk_done"], n + 1)
                    dve.tensor_tensor(flat(mats[:, slot, halves[half]]), flat(wgt[:, halves[half]]),
                                      ps_A[:, half, 0:HH * 2 * C], ALU.mult).then_inc(s[f"mats_ready{half}"], 1)

            def first_inverse(n, slot, uses, sample):
                for half in range(2):
                    hs = halves[half]
                    rows_h = lambda m: m.unsqueeze(1).to_broadcast([P, HH, C])
                    dve.wait_ge(s[f"Y_done{half}"], n * LEVELS + 1)
                    dve.scalar_tensor_tensor(X[:, hs, 1, :], mats[:, slot, hs, 1, :], -1.0, rows_h(level_1T[:]),
                                             ALU.mult, ALU.mult)
                    dve.scalar_tensor_tensor(X[:, hs, 0, :], ps_A[:, half, 0:HH * C].rearrange("p (h c) -> p h c", h=HH),
                                             -1.0, rows_h(level[:, 0]), ALU.mult, ALU.mult)
                    dve.drain()
                    x = X[:, hs].rearrange("p h a c -> p (h a) c")
                    dve.tensor_tensor(x, x, ident[:].unsqueeze(1).to_broadcast([P, 2 * HH, C]), ALU.add
                                      ).then_inc(s[f"X_ready{half}"], 1)

            def output(n, slot):
                dve.wait_ge(s["out_done"], n + 3)
                dve.tensor_tensor(by_head(out[:]), by_head(ps_kv[:, 0, 0:W]), wide(fac[:, slot, QG], HD), ALU.mult)
                dve.drain()
                dve.tensor_tensor(out[:], out[:], ps_kv[:, 1, 0:W], ALU.add)
                dve.drain()
                dve.tensor_tensor(out_sq[:], out[:], out[:], ALU.mult)
                dve.drain()
                dve.tensor_reduce(out_ss[:], by_head(out_sq[:]), AX.X, ALU.add).then_inc(s["out_ss_ready"], 1)

            def gated_output(n, slot):
                dve.wait_ge(s["gate_ready"], n + 1)
                dve.tensor_tensor(out[:], out[:], gate[:, slot], ALU.mult)
                dve.drain()
                dve.wait_ge(s["out_r_ready"], n + 1)
                dve.tensor_tensor(by_head(out[:]), by_head(out[:]), wide(out_r[:], HD), ALU.mult
                                  ).then_inc(s["out_ready"], 1)

            def fade(s_new, s_old, factor):
                dve.tensor_tensor(s_new.rearrange("p b j v -> p (b j) v"), s_old.rearrange("p b j v -> p (b j) v"),
                                  factor.unsqueeze(2).to_broadcast([P, factor.shape[1], P]), ALU.mult)

            def body(n, slot, uses, follows):
                tile = (n, slot, uses, follows)
                sample = follows is None
                first = isinstance(n, int) and n == 0
                levels = S_LEVELS if sample else LEVELS
                for l in range(1, levels):
                    for half in range(2):
                        dve.wait_ge(s[f"Y_done{half}"], n * LEVELS + (l + 1))
                        dve.tensor_tensor(Y[:, halves[half]], ps_Y[:, half, 0:HH * C].rearrange("p (h c) -> p h c", h=HH),
                                          level[:, l].unsqueeze(1).to_broadcast([P, HH, C]), ALU.mult
                                          ).then_inc(s[f"Y_ready{half}"], 1)
                    for half in range(2):
                        dve.wait_ge(s[f"Z_done{half}"], n * (LEVELS - 1) + l)
                        if l < levels - 1:
                            x = flat(X[:, halves[half]])
                            z = ps_Z[:, half, 0:HH * 2 * C]
                        else:
                            x = X[:, halves[half], 1, :]
                            z = ps_Z[:, half, 0:HH * 2 * C].rearrange("p (h a c) -> p h a c", h=HH, a=2)[:, :, 1, :]
                        dve.tensor_tensor(x, x, z, ALU.subtract).then_inc(s[f"X_ready{half}"], 1)
                    if l == 1:
                        ahead(decays, *tile)
                        if not first:
                            output(n - 1, 1 - slot)
                    if l == 2:
                        ahead(factor_logs, *tile)
                        if not first:
                            gated_output(n - 1, 1 - slot)
                    if l == 3:
                        ahead(scale_kv, *tile)
                if not sample:
                    ahead(exponents, *tile)
                    for c in range(2):
                        fade(faded[:].unsqueeze(1), state[:].unsqueeze(1), decay[:, slot, c])
                        dve.drain()
                        dve.wait_ge(s["state_done"], n * 2 + (c + 1))
                        for hh in range(2):
                            r = slice(hh * HD, (hh + 1) * HD)
                            last = dve.tensor_tensor(state[r, :, r], faded[r, :, r],
                                                     ps_Z[r, 1, 0:W].rearrange("p (j v) -> p j v", j=J)[:, :, r], ALU.add)
                        last.then_inc(s["state_ready"], 1)
                        if c == 0:
                            ahead(matrices, *tile)
                        dve.drain()
                    ahead(first_inverse, *tile)
                else:
                    dve.wait_ge(s["s_state_loaded"], 32)
                    fade(s_faded[:], s_state[:], decay[:, slot].rearrange("p b j -> p (b j)"))
                    dve.drain()
                    output(n, slot)
                    gated_output(n, slot)
                    for b in range(DEC_B):
                        dve.wait_ge(s["state_done"], 2 * TILES + b + 1)
                        for hh in range(2):
                            r = slice(hh * HD, (hh + 1) * HD)
                            last = dve.tensor_tensor(s_state[r, b, :, r], s_faded[r, b, :, r],
                                                     (ps_Z[r, 1] if b % 2 else ps_Y[r, 0])[:, 0:W].rearrange(
                                                         "p (j v) -> p j v", j=J)[:, :, r], ALU.add)
                        last.then_inc(s["state_ready"], 1)
            dve.wait_ge(s["a_log_exp"], 1)
            dve.tensor_scalar(a_log[:], a_log[:], -1.0, None, ALU.mult)
            dve.drain()
            start = (0, 0, 0, False)
            decays(*start)
            factor_logs(*start)
            scale_kv(*start)
            exponents(*start)
            matrices(*start)
            first_inverse(*start)
            tiles(dve, body)


def scratch(nc, kind="Internal"):
    shapes = {"x0": [TOKENS, D], "convT": [CONV_CHUNKS, P, TOKENS], "qkT": [QKT_N, P, TOKENS],
              "av": [TOKENS, P], "zba": [TOKENS, ZBA_W], "cv": [TOKENS, C_HEADS * HD],
              "mixT": [DC, P, TOKENS], "x1": [TOKENS, D], "h2T": [DC, P, TOKENS]}
    return {n: nc.dram_tensor(f"scratch_{n}", s, F32, kind=kind).ap() for n, s in shapes.items()}


def constants(nc, ctx):
    shapes = {"ident": [P, P], "ones": [P, P], "later": [P, P], "upto": [P, P], "before": [P, P],
              "sel": [N_COND, 2, P], "modT": [P, 4, DC, N_COND], "gates": [P, 2, 2, D]}
    return {n: ctx.enter_context(nc.sbuf_tensor(f"const_{n}", s, F32)) for n, s in shapes.items()}


def program(nc, IN, OUT, S):
    with ExitStack() as ctx:
        K = constants(nc, ctx)
        build_constants(nc, K)
        stage_modulation(nc, K, IN)
        stage_projection(nc, K, IN, OUT, S)
        stage_window(nc, K, IN, OUT, S)
        stage_delta(nc, K, IN, OUT, S)
        stage_stick(nc, K, IN, S)
        stage_stick_samples(nc, K, IN, S)
        stage_mix_out(nc, K, IN, S)
        stage_ffn(nc, K, IN, OUT, S)


def output_shapes():
    shapes = {"y_prompt": (1, SEQ, D), "y_sample": (DEC_B, DEC_T, D)}
    for who, b, t in (("p", 1, SEQ), ("s", DEC_B, DEC_T)):
        shapes |= {f"{who}_a_k": (1, b, WINDOW, A_KV, HD), f"{who}_a_v": (1, b, WINDOW, A_KV, HD),
                   f"{who}_b_conv": (1, b, B_CONV - 1, CONV_CH), f"{who}_b_ssm": (1, b, B_HEADS, HD, HD),
                   f"{who}_c_k": (1, b, t, C_HEADS, HD), f"{who}_c_v": (1, b, t, C_HEADS, HD),
                   f"{who}_ffn_conv": (1, b, FFN_CONV - 1, D_FF)}
    return shapes


def kernel(**inputs):
    import concourse.bacc as bacc
    from concourse.bass_utils import run_bass_kernel_spmd

    nc = bacc.Bacc("TRN2", target_bir_lowering=False, num_devices=1)
    arrays, ins = {}, {}
    for name, value in inputs.items():
        a = np.ascontiguousarray(value)
        if a.ndim == 1:
            a = a.reshape(1, -1)
        arrays[f"in_{name}"] = a
        ins[name] = nc.dram_tensor(f"in_{name}", a.shape, F32, kind="ExternalInput").ap()
    outs = {name: nc.dram_tensor(f"out_{name}", shape, F32, kind="ExternalOutput").ap()
            for name, shape in output_shapes().items()}
    program(nc, ins, outs, scratch(nc))
    r = run_bass_kernel_spmd(nc, [arrays], core_ids=[0])
    return tuple(r.results[0][f"out_{name}"] for name in outs)
```

```python
from contextlib import ExitStack

import numpy as np
import concourse.bass as bass
from concourse import mybir

F32 = mybir.dt.float32
F32R = mybir.dt.float32r
ALU = mybir.AluOpType
ACT = mybir.ActivationFunctionType
AX = mybir.AxisListType

P = 128
D = 1024
DC = D // P
SEQ = 2048
DEC_B, DEC_T = 8, 16
TOKENS = SEQ + DEC_B * DEC_T
PAST = 2048
HD = 64
A_HEADS, A_KV, A_GROUP = 6, 2, 3
WINDOW = 128
B_HEADS, B_CONV = 6, 4
C_HEADS = 4
B_W = B_HEADS * HD
CONV_CH = 3 * B_W
IN_W = 2956
D_FF = 2816
FC = D_FF // P
FFN_CONV = 3
N_COND = 1 + DEC_B
ALPHA = 2.0 ** 0.25
LN_EPS = 1e-5
RMS_EPS = 1e-6
NEG = -1e30
LOG_EXP_TABLES = "natural_log_exp_and_others"

GROUP = 512
GT = GROUP // P
GROUPS = SEQ // GROUP

AQ0, AK0, AV0 = 0, 384, 512
BQKV0, BZ0 = 640, 1792
CQ0, CK0 = 2188, 2444
ZBA_W = B_W + 2 * B_HEADS
CONV_CHUNKS = CONV_CH // P
QKT_AQ, QKT_AK, QKT_CQ, QKT_CK, QKT_N = 0, 3, 4, 6, 8


def signals(nc, ctx, stage, names):
    handles = {n: nc.alloc_semaphore(f"{stage}_{n}") for n in names.split()}
    ctx.callback(nc.clear_and_free_semaphores, list(handles.values()))
    return handles


def signal(nc, ctx, stage, name):
    return signals(nc, ctx, stage, name)[name]


def row_broadcast(row, n=P):
    return row.to_broadcast([n, row.shape[1]])


def build_constants(nc, K):
    with ExitStack() as ctx:
        ctx.callback(nc.all_engine_barrier)
        s = signals(nc, ctx, "constants", "filled")
        block = ctx.enter_context(nc.Block())

        @block.gpsimd
        def _(pool):
            pool.memset(K["ident"][:], 0.0)
            pool.memset(K["ones"][:], 1.0)
            pool.memset(K["sel"][:], 1.0).then_inc(s["filled"], 1)
            pool.wait_ge(s["filled"], 1)
            pool.affine_select(out=K["ident"][:], in_=K["ident"][:], compare_op=ALU.not_equal, fill=1.0,
                               base=0, pattern=[[-1, P]], channel_multiplier=1)
            pool.affine_select(out=K["later"][:], in_=K["ones"][:], compare_op=ALU.is_gt, fill=0.0,
                               base=0, pattern=[[-1, P]], channel_multiplier=1)
            pool.affine_select(out=K["upto"][:], in_=K["ones"][:], compare_op=ALU.is_ge, fill=0.0,
                               base=0, pattern=[[1, P]], channel_multiplier=-1)
            pool.affine_select(out=K["before"][:], in_=K["ones"][:], compare_op=ALU.is_gt, fill=0.0,
                               base=0, pattern=[[1, P]], channel_multiplier=-1)
            pool.affine_select(out=K["sel"][:, 0, :], in_=K["sel"][:, 0, :], compare_op=ALU.is_equal,
                               fill=0.0, base=0, pattern=[[0, P]], channel_multiplier=1)
            pool.affine_select(out=K["sel"][:, 1, :], in_=K["sel"][:, 1, :], compare_op=ALU.is_equal,
                               fill=0.0, base=-1, pattern=[[-1, DEC_B], [0, DEC_T]],
                               channel_multiplier=1)


def stage_modulation(nc, K, IN):
    COLS, RING = 512, 3
    n_cols = 6 * D // COLS
    with ExitStack() as ctx:
        ctx.callback(nc.all_engine_barrier)
        sb = lambda name, shape: ctx.enter_context(nc.sbuf_tensor(name, shape, F32))
        ps = lambda name, shape: ctx.enter_context(nc.psum_tensor(name, shape, F32))
        cond = sb("cond", [N_COND, D])
        cond_silu = sb("cond_silu", [N_COND, D])
        condT = sb("condT", [P, DC, N_COND])
        bias = sb("bias", [N_COND, 6 * D])
        mod = sb("mod", [N_COND, 6 * D])
        w = sb("w_ada_ring", [P, RING, DC, COLS])
        ps_T = ps("ps_condT", [P, 512])
        ps_mod = ps("ps_mod", [P, RING, COLS])
        ps_gate = ps("ps_gate", [P, 2, COLS])
        s = signals(nc, ctx, "modulation", "cond_loaded bias_loaded silu_done condT_done condT_copied "
                             "mod_done mod_copied modT_done gate_done gate_copied w_free")
        w_loaded = [signal(nc, ctx, "modulation", f"w_ada_loaded{r}") for r in range(RING)]
        w_ada = IN["w_ada"][0].rearrange("(k p) n -> p k n", p=P)
        block = ctx.enter_context(nc.Block())

        @block.sync
        def _(sp):
            sp.dma_start(cond[0:1, :], IN["c_prompt"]).then_inc(s["cond_loaded"], 16)
            sp.dma_start(cond[1:N_COND, :], IN["c_sample"]).then_inc(s["cond_loaded"], 16)
            sp.dma_start(bias[:], IN["b_ada"].to_broadcast([N_COND, 6 * D])).then_inc(s["bias_loaded"], 16)
            with sp.Fori(0, n_cols // RING) as i:
                for r in range(RING):
                    sp.wait_ge(s["w_free"], i * RING + r + 1)
                    sp.dma_start(w[:, r], w_ada[:, :, bass.ds(i * (RING * COLS) + r * COLS, COLS)]
                                 ).then_inc(w_loaded[r], 16)

        @block.scalar
        def _(act):
            act.wait_ge(s["cond_loaded"], 32)
            act.activation(cond_silu[:], cond[:], ACT.Silu).then_inc(s["silu_done"], 1)

        @block.tensor
        def _(pe):
            pe.sem_inc(s["w_free"], RING)
            pe.wait_ge(s["silu_done"], 1)
            for k in range(DC):
                last = pe.transpose(ps_T[:, k * N_COND:(k + 1) * N_COND], cond_silu[:, k * P:(k + 1) * P],
                                    K["ident"][0:N_COND, 0:N_COND])
            last.then_inc(s["condT_done"], 1)
            pe.wait_ge(s["condT_copied"], 1)
            with pe.Fori(0, n_cols // RING) as i:
                for r in range(RING):
                    pe.wait_ge(w_loaded[r], i * 16 + 16)
                    pe.wait_ge(s["mod_copied"], i * RING + r + 1)
                    for k in range(DC):
                        last = pe.matmul(ps_mod[0:N_COND, r], condT[:, k, :], w[:, r, k, :],
                                         start=(k == 0), stop=(k == DC - 1))
                    last.then_inc(s["w_free"], 1)
            pe.wait_ge(s["mod_copied"], RING + n_cols)
            for j, kind in enumerate((0, 1, 3, 4)):
                for k in range(DC):
                    o = (j * DC + k) * N_COND
                    last = pe.transpose(ps_T[:, o:o + N_COND], mod[:, kind * D + k * P:kind * D + (k + 1) * P],
                                        K["ident"][0:N_COND, 0:N_COND])
            last.then_inc(s["modT_done"], 1)
            n = 0
            for g, kind in enumerate((2, 5)):
                for who in range(2):
                    for half in range(2):
                        if n >= 2:
                            pe.wait_ge(s["gate_copied"], n - 1)
                        c0 = kind * D + half * COLS
                        pe.matmul(ps_gate[:, n % 2], K["sel"][:, who, :], mod[:, c0:c0 + COLS],
                                  start=True, stop=True).then_inc(s["gate_done"], 1)
                        n += 1

        @block.vector
        def _(dve):
            dve.sem_inc(s["mod_copied"], RING)
            dve.wait_ge(s["condT_done"], 1)
            dve.tensor_copy(condT[:].rearrange("p k c -> p (k c)"), ps_T[:, 0:DC * N_COND]
                            ).then_inc(s["condT_copied"], 1)
            dve.wait_ge(s["bias_loaded"], 16)
            with dve.Fori(0, n_cols // RING) as i:
                for r in range(RING):
                    dve.wait_ge(s["w_free"], i * RING + (RING + r + 1))
                    at = bass.ds(i * (RING * COLS) + r * COLS, COLS)
                    dve.tensor_tensor(mod[:, at], ps_mod[0:N_COND, r], bias[:, at], ALU.add
                                      ).then_inc(s["mod_copied"], 1)
            dve.wait_ge(s["modT_done"], 1)
            for j in range(4):
                src = ps_T[:, j * DC * N_COND:(j + 1) * DC * N_COND]
                dst = K["modT"][:, j].rearrange("p k c -> p (k c)")
                dve.tensor_scalar(dst, src, float(j % 2), None, ALU.add)
            n = 0
            for g in range(2):
                for who in range(2):
                    for half in range(2):
                        dve.wait_ge(s["gate_done"], n + 1)
                        dve.tensor_copy(K["gates"][:, g, who, half * COLS:(half + 1) * COLS],
                                        ps_gate[:, n % 2]).then_inc(s["gate_copied"], 1)
                        n += 1


def layer_norm_stats(dve, x, stats, mean_var, tiles):
    for t in range(tiles):
        for h in range(2):
            dve.bn_stats(stats[:, t, h, :], x[:, t, h * 512:(h + 1) * 512])
    dve.drain()
    for t in range(tiles):
        last = dve.bn_aggr(mean_var[:, t, :], stats[:, t].rearrange("p a b -> p (a b)"))
    return last


def stage_projection(nc, K, IN, OUT, S):
    with ExitStack() as ctx:
        ctx.callback(nc.all_engine_barrier)
        sb = lambda name, shape: ctx.enter_context(nc.sbuf_tensor(name, shape, F32))
        ps = lambda name, shape: ctx.enter_context(nc.psum_tensor(name, shape, F32))
        HIST = B_CONV - 1
        HR = DEC_B * HIST
        NL = HIST + HR
        w = sb("w_in_all", [P, DC, IN_W])
        x = sb("x_group", [P, GT, D])
        hT = sb("hT", [P, DC, GROUP])
        ln_g, ln_b = sb("ln_in_g_rows", [P, D]), sb("ln_in_b_rows", [P, D])
        stats = sb("ln_stats", [P, GT, 2, 6])
        mean_var = sb("ln_mean_var", [P, GT, 2])
        rstd = sb("ln_rstd", [P, GT])
        minus_half, eps = sb("minus_half", [P, GT]), sb("ln_eps", [P, GT])
        raw = sb("conv_raw", [P, CONV_CHUNKS, HIST + GROUP])
        conv = sb("conv_sum", [P, 3, GROUP])
        conv_act = sb("conv_act", [P, 3, GROUP])
        taps = sb("conv_taps", [P, CONV_CHUNKS, B_CONV])
        histT = sb("conv_hist", [P, CONV_CHUNKS, HR])
        rows = sb("conv_rows", [P, CONV_CH])
        last_raw = sb("conv_last_raw", [P, CONV_CHUNKS, NL])
        qkT = sb("qkT_stage", [P, 2, GROUP])
        tok = sb("token_stage", [P, 2, 3, 512])
        ps_T = ps("ps_hT", [P, DC, P])
        ps_F = ps("ps_feature", [P, 3, GROUP])
        ps_K = ps("ps_token", [P, 3, 512])
        s = signals(nc, ctx, "projection", "w_loaded rows_loaded lnrow_loaded x_loaded x_stored stats_done rstd_done "
                             "x0_ready hT_ps hT_ready feat_done feat_copied hist_ready conv_done "
                             "conv_act_done taps_ps tok_done tok_z tok_v last_kept last_ps last_ready "
                             "rows_stored")
        conv_stored = [signal(nc, ctx, "projection", f"conv_stored{b}") for b in range(3)]
        qkT_stored = [signal(nc, ctx, "projection", f"qkT_stored{b}") for b in range(2)]
        tok_stored = [signal(nc, ctx, "projection", f"tok_stored{b}") for b in range(2)]

        def w_cols(f, k):
            if f < CONV_CHUNKS:
                return w[:, k, BQKV0 + f * P:BQKV0 + (f + 1) * P]
            q = f - CONV_CHUNKS
            if q < QKT_AK:
                return w[:, k, q * P:(q + 1) * P]
            c0 = {QKT_AK: AK0, QKT_CQ: CQ0, QKT_CQ + 1: CQ0 + P, QKT_CK: CK0, QKT_CK + 1: CK0 + P}[q]
            return w[:, k, c0:c0 + P]

        TOK_PIECES = ((AV0, P), (BZ0, ZBA_W), (CK0, 512))
        TOK_DMAS = 5
        FEATS = CONV_CHUNKS + QKT_N

        def groups(engine, body):
            with engine.Fori(0, GROUPS - 1) as i:
                body(i, GT, GROUP, "prompt")
            body(GROUPS - 1, GT, GROUP, "sample")
            body(GROUPS, 1, P, None)

        block = ctx.enter_context(nc.Block())

        @block.gpsimd
        def _(pool):
            pool.memset(minus_half[:], -0.5)
            pool.memset(eps[:], LN_EPS)
            pool.drain()
            pool.dma_start(ln_g[:], row_broadcast(IN["ln_in_g"])).then_inc(s["lnrow_loaded"], 16)
            pool.dma_start(ln_b[:], row_broadcast(IN["ln_in_b"])).then_inc(s["lnrow_loaded"], 16)
            pool.dma_start(rows[0:B_CONV, :], IN["b_conv_w"][0]).then_inc(s["rows_loaded"], 16)
            pool.dma_start(rows[32:32 + HR, :], IN["state_b_conv"].rearrange("l b t c -> (l b t) c")
                           ).then_inc(s["rows_loaded"], 16)

            def load(it, tiles, sample):
                src = (IN["x_sample"].rearrange("b t d -> (b t) d") if sample
                       else IN["x_prompt"][0, bass.ds(it * GROUP, GROUP), :])
                pool.dma_start(x[:, 0:tiles, :], src.rearrange("(t p) d -> p t d", p=P)
                               ).then_inc(s["x_loaded"], 16)

            def body(it, tiles, tokens, follows):
                pool.wait_ge(s["stats_done"], it + 1)
                pool.tensor_tensor(rstd[:, 0:tiles], mean_var[:, 0:tiles, 1], eps[:, 0:tiles], ALU.add)
                pool.drain()
                pool.tensor_tensor(rstd[:, 0:tiles], rstd[:, 0:tiles], minus_half[:, 0:tiles], ALU.pow
                                   ).then_inc(s["rstd_done"], 1)
                pool.wait_ge(s["x0_ready"], it + 1)
                pool.dma_start(S["x0"][bass.ds(it * GROUP, tokens), :].rearrange("(t p) d -> p t d", p=P),
                               x[:, 0:tiles, :]).then_inc(s["x_stored"], 16)
                pool.wait_ge(s["x_stored"], it * 16 + 16)
                if follows is not None:
                    pool.wait_ge(s["hT_ps"], (it + 1) * GT)
                    load(it + 1, GT if follows == "prompt" else 1, follows == "sample")

            load(0, GT, False)
            groups(pool, body)

        @block.tensor
        def _(pe):
            pe.wait_ge(s["rows_loaded"], 32)
            for f in range(CONV_CHUNKS):
                pe.transpose(ps_F[:, 0, f * B_CONV:(f + 1) * B_CONV], rows[0:B_CONV, f * P:(f + 1) * P],
                             K["ident"][0:B_CONV, 0:B_CONV])
                last = pe.transpose(ps_F[:, 1, f * HR:(f + 1) * HR], rows[32:32 + HR, f * P:(f + 1) * P],
                                    K["ident"][32:32 + HR, 32:32 + HR])
            last.then_inc(s["taps_ps"], 1)
            pe.wait_ge(s["hist_ready"], 1)
            pe.wait_ge(s["w_loaded"], 16 * 3 * DC)

            def turn(it, t):
                if t == 0:
                    pe.wait_ge(s["x0_ready"], it + 1)
                pe.wait_ge(s["hT_ready"], it * GT + (t + 1))
                for k in range(DC):
                    last = pe.transpose(ps_T[:, k, :], x[:, t, k * P:(k + 1) * P], K["ident"][:])
                last.then_inc(s["hT_ps"], 1)

            def body(it, tiles, tokens, follows):
                tile0, chunk0 = it * GT, it * FEATS
                pe.wait_ge(s["hT_ready"], tile0 + (tiles + 1))
                for f in range(FEATS):
                    pe.wait_ge(s["feat_copied"], chunk0 + (f + 2 if f < 2 else f + 1))
                    for k in range(DC):
                        last = pe.matmul(ps_F[:, f % 3, 0:tokens], w_cols(f, k), hT[:, k, 0:tokens],
                                         start=(k == 0), stop=(k == DC - 1))
                    last.then_inc(s["feat_done"], 1)
                for t in range(tiles):
                    for j, (c0, width) in enumerate(TOK_PIECES):
                        n2 = (tile0 + t) * 2
                        pe.wait_ge(s["tok_z"] if j == 1 else s["tok_v"], n2 + (1 if j == 0 else 2))
                        for k in range(DC):
                            last = pe.matmul(ps_K[:, j, 0:width], hT[:, k, t * P:(t + 1) * P],
                                             w[:, k, c0:c0 + width], start=(k == 0), stop=(k == DC - 1))
                        last.then_inc(s["tok_done"], 1)
                    if follows == "prompt" or follows == "sample" and t == 0:
                        turn(it + 1, t)
            for t in range(GT):
                turn(0, t)
            groups(pe, body)
            pe.wait_ge(s["last_kept"], 2)
            pe.wait_ge(s["feat_copied"], 3 + FEATS * (GROUPS + 1))
            for f in range(CONV_CHUNKS):
                last = pe.transpose(ps_F[0:NL, f // 4, (f % 4) * P:(f % 4 + 1) * P], last_raw[:, f, :],
                                    K["ident"][:])
            last.then_inc(s["last_ps"], 1)

        @block.scalar
        def _(act):
            act.sem_inc(s["hT_ready"], 1)
            act.sem_inc(s["feat_copied"], 3)
            act.sem_inc(s["tok_z"], 2)
            act.sem_inc(s["conv_act_done"], 3)

            def modulate(it, t):
                act.wait_ge(s["hT_ps"], it * GT + (t + 1))
                for k in range(DC):
                    last = act.activation(hT[:, k, t * P:(t + 1) * P], ps_T[:, k, :], ACT.Identity,
                                          bias=K["modT"][:, 0, k, 0:1], scale=K["modT"][:, 1, k, 0:1])
                last.then_inc(s["hT_ready"], 1)

            def body(it, tiles, tokens, follows):
                tile0, chunk0, conv0 = it * GT, it * FEATS, it * CONV_CHUNKS

                def silu_conv(f):
                    act.wait_ge(s["conv_done"], conv0 + (f + 1))
                    act.wait_ge(conv_stored[f % 3], it * 48 + (f // 3 * 16 + 16))
                    act.activation(conv_act[:, f % 3, 0:tokens], conv[:, f % 3, 0:tokens], ACT.Silu
                                   ).then_inc(s["conv_act_done"], 1)

                for f in range(FEATS):
                    act.wait_ge(s["feat_done"], chunk0 + (f + 1))
                    src = ps_F[:, f % 3, 0:tokens]
                    if f < CONV_CHUNKS:
                        if f == 0:
                            act.wait_ge(s["hist_ready"], it + 1)
                        dst = raw[:, f, HIST:]
                        if follows is None:
                            dst = raw[:, f, 0:DEC_B * (HIST + DEC_T)].rearrange(
                                "p (b t) -> p b t", b=DEC_B)[:, :, HIST:]
                            src = src.rearrange("p (b t) -> p b t", b=DEC_B)
                    else:
                        q = f - CONV_CHUNKS
                        act.wait_ge(qkT_stored[q % 2], it * (QKT_N // 2 * 16) + (q // 2 * 16 + 16))
                        dst = qkT[:, q % 2, 0:tokens]
                    act.activation(dst, src, ACT.Identity).then_inc(s["feat_copied"], 1)
                    if 1 <= f <= CONV_CHUNKS:
                        silu_conv(f - 1)
                for t in range(tiles):
                    act.wait_ge(s["tok_done"], (tile0 + t) * 3 + 2)
                    act.wait_ge(tok_stored[t % 2], it * (GT // 2 * TOK_DMAS * 16)
                                + ((t // 2 + 1) * TOK_DMAS * 16))
                    act.activation(tok[:, t % 2, 1, 0:B_W], ps_K[:, 1, 0:B_W], ACT.Silu
                                   ).then_inc(s["tok_z"], 1)
                    act.activation(tok[:, t % 2, 1, B_W:ZBA_W], ps_K[:, 1, B_W:ZBA_W], ACT.Identity
                                   ).then_inc(s["tok_z"], 1)
                    if follows == "prompt":
                        modulate(it + 1, t)
            for t in range(GT):
                modulate(0, t)
            groups(act, body)

        @block.sync
        def _(sp):
            for b in range(3):
                sp.sem_inc(conv_stored[b], 16)
            for b in range(2):
                sp.sem_inc(qkT_stored[b], 16)
                sp.sem_inc(tok_stored[b], TOK_DMAS * 16)
            for k in range(DC):
                w_rows = IN["w_in"][0, k * P:(k + 1) * P, :]
                sp.dma_start(w[:, k, AK0:], w_rows[:, AK0:]).then_inc(s["w_loaded"], 16)
                for v in range(A_KV):
                    sp.dma_start(w[:, k, 0:AK0].rearrange("p (g v d) -> p g v d", g=A_GROUP, v=A_KV)[:, :, v],
                                 w_rows[:, 0:AK0].rearrange("p (v g d) -> p v g d", v=A_KV, g=A_GROUP)[:, v]
                                 ).then_inc(s["w_loaded"], 16)

            def body(it, tiles, tokens, follows):
                tile0, chunk0, conv0 = it * GT, it * FEATS, it * CONV_CHUNKS
                at = bass.ds(it * GROUP, tokens)
                for f in range(CONV_CHUNKS):
                    sp.wait_ge(s["conv_act_done"], conv0 + (f + 4))
                    sp.dma_start(S["convT"][f, :, at], conv_act[:, f % 3, 0:tokens]
                                 ).then_inc(conv_stored[f % 3], 16)
                for q in range(QKT_N):
                    sp.wait_ge(s["feat_copied"], chunk0 + (CONV_CHUNKS + q + 4))
                    sp.dma_start(S["qkT"][q, :, at], qkT[:, q % 2, 0:tokens]).then_inc(qkT_stored[q % 2], 16)
                for t in range(tiles):
                    n = tile0 + t
                    rows_at = bass.ds(it * GROUP + t * P, P)
                    stage = tok[:, t % 2]
                    sp.wait_ge(s["tok_v"], n * 2 + 4)
                    sp.wait_ge(s["tok_z"], n * 2 + 4)
                    who = "s" if follows is None else "p"
                    ck, cv = (OUT[f"{who}_c_{a}"].rearrange("l b t h d -> (l b t) (h d)") for a in "kv")
                    out_at = slice(0, P) if follows is None else rows_at
                    for dst, src in ((S["av"][rows_at, :], stage[:, 0, 0:P]),
                                     (S["zba"][rows_at, :], stage[:, 1, 0:ZBA_W]),
                                     (S["cv"][rows_at, :], stage[:, 2, 256:512]),
                                     (ck[out_at, :], stage[:, 2, 0:256]),
                                     (cv[out_at, :], stage[:, 2, 256:512])):
                        sp.dma_start(dst, src).then_inc(tok_stored[t % 2], 16)
            groups(sp, body)
            sp.wait_ge(s["last_ready"], 1)
            sp.dma_start(OUT["p_b_conv"].rearrange("l b t c -> (l b t) c"), rows[0:HIST, :]
                         ).then_inc(s["rows_stored"], 16)
            sp.dma_start(OUT["s_b_conv"].rearrange("l b t c -> (l b t) c"), rows[HIST:NL, :]
                         ).then_inc(s["rows_stored"], 16)
            sp.wait_ge(s["rows_stored"], 32)
            for b in range(3):
                sp.wait_ge(conv_stored[b], 16 * (3 * (GROUPS + 1) + 1))
            for b in range(2):
                sp.wait_ge(qkT_stored[b], 16 * (QKT_N // 2 * (GROUPS + 1) + 1))
                sp.wait_ge(tok_stored[b], 16 * TOK_DMAS * (GROUPS * GT // 2 + (2 if b == 0 else 1)))

        @block.vector
        def _(dve):
            dve.sem_inc(s["tok_v"], 2)
            dve.wait_ge(s["taps_ps"], 1)
            dve.tensor_copy(taps[:].rearrange("p f t -> p (f t)"), ps_F[:, 0, 0:CONV_CHUNKS * B_CONV])
            dve.tensor_copy(histT[:].rearrange("p f t -> p (f t)"), ps_F[:, 1, 0:CONV_CHUNKS * HR])
            dve.memset(raw[:, :, 0:HIST], 0.0).then_inc(s["hist_ready"], 1)
            dve.wait_ge(s["lnrow_loaded"], 32)

            def norm(it, tiles):
                dve.wait_ge(s["x_loaded"], it * 16 + 16)
                layer_norm_stats(dve, x, stats, mean_var, tiles).then_inc(s["stats_done"], 1)
                dve.wait_ge(s["rstd_done"], it + 1)
                for t in range(tiles):
                    dve.tensor_scalar(x[:, t], x[:, t], mean_var[:, t, 0:1], rstd[:, t:t + 1],
                                      ALU.subtract, ALU.mult)
                dve.drain()
                for t in range(tiles):
                    dve.tensor_tensor(x[:, t], x[:, t], ln_g[:], ALU.mult)
                dve.drain()
                for t in range(tiles):
                    last = dve.tensor_tensor(x[:, t], x[:, t], ln_b[:], ALU.add)
                last.then_inc(s["x0_ready"], 1)

            def body(it, tiles, tokens, follows):
                tile0, chunk0, conv0 = it * GT, it * FEATS, it * CONV_CHUNKS
                if follows is None:
                    dve.wait_ge(s["hT_ps"], tile0 + 1)
                    for k in range(DC):
                        h = hT[:, k, 0:P].rearrange("p (b t) -> p b t", b=DEC_B)
                        by_seq = lambda j: K["modT"][:, j, k, 1:].unsqueeze(2).to_broadcast([P, DEC_B, DEC_T])
                        dve.tensor_tensor(h, ps_T[:, k, :].rearrange("p (b t) -> p b t", b=DEC_B),
                                          by_seq(1), ALU.mult)
                    dve.drain()
                    for k in range(DC):
                        h = hT[:, k, 0:P].rearrange("p (b t) -> p b t", b=DEC_B)
                        by_seq = lambda j: K["modT"][:, j, k, 1:].unsqueeze(2).to_broadcast([P, DEC_B, DEC_T])
                        last = dve.tensor_tensor(h, h, by_seq(0), ALU.add)
                    last.then_inc(s["hT_ready"], 1)
                for f in range(CONV_CHUNKS):
                    dve.wait_ge(s["feat_copied"], chunk0 + (f + 4))
                    dve.wait_ge(s["conv_act_done"], conv0 + (f + 1))
                    for i in range(B_CONV):
                        if follows is None:
                            src = raw[:, f, 0:DEC_B * (HIST + DEC_T)].rearrange(
                                "p (b t) -> p b t", b=DEC_B)[:, :, i:i + DEC_T]
                            dst = conv[:, f % 3, 0:tokens].rearrange("p (b t) -> p b t", b=DEC_B)
                        else:
                            src, dst = raw[:, f, i:i + GROUP], conv[:, f % 3, :]
                        if i == 0:
                            last = dve.tensor_scalar(dst, src, taps[:, f, 0:1], None, ALU.mult)
                        else:
                            dve.drain()
                            last = dve.scalar_tensor_tensor(dst, src, taps[:, f, i:i + 1], dst,
                                                            ALU.mult, ALU.add)
                    last.then_inc(s["conv_done"], 1)
                if follows == "prompt":
                    dve.tensor_copy(raw[:, :, 0:HIST], raw[:, :, GROUP:GROUP + HIST]
                                    ).then_inc(s["hist_ready"], 1)
                elif follows == "sample":
                    dve.tensor_copy(last_raw[:, :, 0:HIST], raw[:, :, GROUP:GROUP + HIST]
                                    ).then_inc(s["last_kept"], 1)
                    dve.drain()
                    for b in range(DEC_B):
                        o = b * (HIST + DEC_T)
                        last = dve.tensor_copy(raw[:, :, o:o + HIST], histT[:, :, b * HIST:(b + 1) * HIST])
                    last.then_inc(s["hist_ready"], 1)
                else:
                    for b in range(DEC_B):
                        o = (b + 1) * (HIST + DEC_T)
                        last = dve.tensor_copy(last_raw[:, :, HIST + b * HIST:HIST + (b + 1) * HIST],
                                               raw[:, :, o - HIST:o])
                    last.then_inc(s["last_kept"], 1)
                if follows is not None:
                    norm(it + 1, GT if follows == "prompt" else 1)
                for t in range(tiles):
                    dve.wait_ge(tok_stored[t % 2], it * (GT // 2 * TOK_DMAS * 16)
                                + ((t // 2 + 1) * TOK_DMAS * 16))
                    for j in (0, 2):
                        dve.wait_ge(s["tok_done"], (tile0 + t) * 3 + (j + 1))
                        width = TOK_PIECES[j][1]
                        dve.tensor_copy(tok[:, t % 2, j, 0:width], ps_K[:, j, 0:width]
                                        ).then_inc(s["tok_v"], 1)

            norm(0, GT)
            groups(dve, body)
            dve.wait_ge(s["last_ps"], 1)
            last = dve.tensor_copy(rows[0:NL, 0:1024], ps_F[0:NL, 0:2, :].rearrange("p a b -> p (a b)"))
            last = dve.tensor_copy(rows[0:NL, 1024:CONV_CH], ps_F[0:NL, 2, 0:CONV_CH - 1024])
            last.then_inc(s["last_ready"], 1)


def rstd_of(pool, rstd, variance, eps, minus_half):
    pool.tensor_tensor(rstd, variance, eps, ALU.add)
    pool.drain()
    return pool.tensor_tensor(rstd, rstd, minus_half, ALU.pow)


def stage_mix_out(nc, K, IN, S):
    TILES = TOKENS // P
    W_SLOTS = 4
    with ExitStack() as ctx:
        ctx.callback(nc.all_engine_barrier)
        sb = lambda name, shape: ctx.enter_context(nc.sbuf_tensor(name, shape, F32))
        ps = lambda name, shape: ctx.enter_context(nc.psum_tensor(name, shape, F32))
        rounded = lambda name, shape: ctx.enter_context(nc.sbuf_tensor(name, shape, F32R))
        w_chunk = sb("w_out_chunk", [P, W_SLOTS, D])
        w_high, w_low = rounded("w_out_high", [P, DC, D]), rounded("w_out_low", [P, DC, D])
        mixT = sb("mixT_tile", [P, 2, DC, P])
        mix_high, mix_low = (rounded(f"mixT_{part}", [P, 2, DC, P]) for part in ("high", "low"))
        x = sb("x_tile", [P, 2, D])
        y = sb("gated_mix", [P, 2, D])
        hT = sb("h2T_tile", [P, 2, DC, P])
        hT_low = sb("h2T_tile_low", [P, 2, DC, P])
        hT_high = rounded("h2T_tile_high", [P, 2, DC, P])
        ln_g, ln_b = sb("ln1_g_rows", [P, D]), sb("ln1_b_rows", [P, D])
        stats = sb("ln1_stats", [P, 1, 2, 6])
        mean_var = sb("ln1_mean_var", [P, 1, 2])
        rstd = sb("ln1_rstd", [P, 1])
        minus_half, eps = sb("ln1_minus_half", [P, 1]), sb("ln1_eps", [P, 1])
        ps_O = ps("ps_mix_out", [P, 2, D])
        ps_T = ps("ps_h2T", [P, 2, DC, P])
        s = signals(nc, ctx, "mix_out", "high_ready low_ready w_high_ready w_split mix_high_ready mix_split lnrow_loaded out_done out_copied stats_done rstd_done x1_ready "
                             "hT_ps hT_ready hT_sample_ready")
        mix_loaded, x_loaded, x1_stored, hT_stored, low_stored = (
            [signal(nc, ctx, "mix_out", f"{n}{b}") for b in range(2)]
            for n in ("mix_loaded", "x0_loaded", "x1_stored", "h2T_stored", "h2T_low_stored"))
        w_loaded = [signal(nc, ctx, "mix_out", f"w_out_loaded{k}") for k in range(DC)]
        block = ctx.enter_context(nc.Block())

        def tiles(engine, body):
            body(0, 0, 0, False)
            body(1, 1, 0, False)
            with engine.Fori(0, TILES // 2 - 2) as i:
                for b in range(2):
                    body(i * 2 + (2 + b), b, i + 1, False)
            for n in range(TILES - 3, TILES):
                body(n, n % 2, n // 2, n == TILES - 1)

        def first(n):
            return isinstance(n, int) and n == 0

        def two_ahead(n):
            return not isinstance(n, int) or n + 2 < TILES

        @block.sync
        def _(sp):
            def load_mix(n, slot):
                sp.dma_start(mixT[:, slot], S["mixT"][:, :, bass.ds(n * P, P)].rearrange("k p t -> p k t")
                             ).then_inc(mix_loaded[slot], 16)

            def store_low(n, slot):
                sp.wait_ge(s["low_ready"], n + 3)
                sp.dma_start(S["h2T_low"][:, :, bass.ds(n * P, P)].rearrange("k p t -> p k t"), hT_low[:, slot]
                             ).then_inc(low_stored[slot], 16)

            load_mix(0, 0)
            load_mix(1, 1)

            def body(n, slot, uses, sample):
                if two_ahead(n):
                    sp.wait_ge(s["mix_split"], n + 3)
                    load_mix(n + 2, slot)
                if not first(n):
                    store_low(n - 1, 1 - slot)
            tiles(sp, body)
            store_low(TILES - 1, 0)
            sp.wait_ge(low_stored[0], 16 * (TILES // 2 + 2))
            sp.wait_ge(low_stored[1], 16 * (TILES // 2 + 1))

        @block.gpsimd
        def _(pool):
            pool.sem_inc(s["low_ready"], 2)
            for b in range(2):
                pool.sem_inc(low_stored[b], 16)
            pool.memset(minus_half[:], -0.5)
            pool.memset(eps[:], LN_EPS)
            pool.drain()
            for k in range(DC):
                at = k % W_SLOTS
                if k >= W_SLOTS:
                    pool.wait_ge(s["w_split"], k - W_SLOTS + 1)
                if k < A_GROUP:
                    for v in range(A_KV):
                        r0 = (v * A_GROUP + k) * HD
                        pool.dma_start(w_chunk[v * HD:(v + 1) * HD, at, :], IN["w_out"][0, r0:r0 + HD, :]
                                     ).then_inc(w_loaded[k], 16)
                else:
                    pool.dma_start(w_chunk[:, at, :], IN["w_out"][0, k * P:(k + 1) * P, :]
                                 ).then_inc(w_loaded[k], 16)
            pool.dma_start(ln_g[:], row_broadcast(IN["ln1_g"])).then_inc(s["lnrow_loaded"], 16)
            pool.dma_start(ln_b[:], row_broadcast(IN["ln1_b"])).then_inc(s["lnrow_loaded"], 16)

            def low_of_h(n, slot, uses):
                pool.wait_ge(s["high_ready"], n + 1)
                pool.wait_ge(low_stored[slot], uses * 16 + 16)
                flat = lambda h: h[:, slot].rearrange("p k t -> p (k t)")
                pool.tensor_tensor(flat(hT_low), flat(hT), flat(hT_high).bitcast(F32), ALU.subtract
                                   ).then_inc(s["low_ready"], 1)

            def body(n, slot, uses, sample):
                pool.wait_ge(s["stats_done"], n + 1)
                rstd_of(pool, rstd[:], mean_var[:, :, 1], eps[:], minus_half[:]).then_inc(s["rstd_done"], 1)
                if not first(n):
                    low_of_h(n - 1, 1 - slot, uses + (slot - 1))
                pool.wait_ge(s["x1_ready"], n + 1)
                pool.dma_start(S["x1"][bass.ds(n * P, P), :], x[:, slot]).then_inc(x1_stored[slot], 16)
            tiles(pool, body)
            low_of_h(TILES - 1, 0, TILES // 2)
            pool.wait_ge(x1_stored[0], 16 * (TILES // 2 + 1))
            pool.wait_ge(x1_stored[1], 16 * (TILES // 2))

        @block.tensor
        def _(pe):
            pe.sem_inc(s["out_done"], 2)
            pe.sem_inc(s["hT_ps"], 2)

            def project(n, slot, first=False):
                pe.wait_ge(s["mix_split"], n + 3)
                pe.wait_ge(s["out_copied"], n + 1)
                for half in range(2):
                    cols = slice(half * 512, half * 512 + 512)
                    for k in range(DC):
                        if first and half == 0:
                            pe.wait_ge(s["w_split"], k + 1)
                        for part, (mix, w) in enumerate(((mix_high, w_high), (mix_high, w_low), (mix_low, w_high))):
                            last = pe.matmul(ps_O[:, slot, cols], mix[:, slot, k, :], w[:, k, cols],
                                             start=(k == 0 and part == 0), stop=(k == DC - 1 and part == 2))
                last.then_inc(s["out_done"], 1)

            def turn(n, slot):
                pe.wait_ge(s["x1_ready"], n + 1)
                pe.wait_ge(s["hT_ready"], n + 1)
                for k in range(DC):
                    last = pe.transpose(ps_T[:, slot, k, :], x[:, slot, k * P:(k + 1) * P], K["ident"][:])
                last.then_inc(s["hT_ps"], 1)

            project(0, 0, first=True)
            with pe.Fori(0, TILES // 2) as i:
                project(i * 2 + 1, 1)
                turn(i * 2, 0)
                project(i * 2 + 2, 0)
                turn(i * 2 + 1, 1)
            turn(TILES - 1, 0)

        @block.scalar
        def _(act):
            act.sem_inc(s["hT_ready"], 2)
            for b in range(2):
                act.sem_inc(hT_stored[b], 16)
            flat = lambda buffer, slot: buffer[:, slot].rearrange("p k t -> p (k t)")

            def load_x(n, slot):
                act.dma_start(x[:, slot], S["x0"][bass.ds(n * P, P), :]).then_inc(x_loaded[slot], 16)

            load_x(0, 0)
            load_x(1, 1)

            def round_mix(n, slot, uses):
                act.wait_ge(mix_loaded[slot], uses * 16 + 16)
                act.wait_ge(s["out_done"], n + 1)
                act.activation(flat(mix_high, slot), flat(mixT, slot), ACT.Identity).then_inc(s["mix_high_ready"], 1)

            for k in range(DC):
                act.wait_ge(w_loaded[k], 32 if k < A_GROUP else 16)
                act.activation(w_high[:, k, :], w_chunk[:, k % W_SLOTS, :], ACT.Identity
                               ).then_inc(s["w_high_ready"], 1)
                if k < 2:
                    round_mix(k, k, 0)

            def body(n, slot, uses, sample):
                if two_ahead(n):
                    round_mix(n + 2, slot, uses + 1)
                if not sample:
                    act.wait_ge(s["hT_ps"], n + 3)
                    act.wait_ge(hT_stored[slot], uses * 16 + 16)
                    act.wait_ge(s["low_ready"], n + 1)
                    for k in range(DC):
                        last = act.activation(hT[:, slot, k, :], ps_T[:, slot, k, :], ACT.Identity,
                                              bias=K["modT"][:, 2, k, 0:1], scale=K["modT"][:, 3, k, 0:1])
                    last.then_inc(s["hT_ready"], 1)
                if two_ahead(n):
                    act.wait_ge(x1_stored[slot], uses * 16 + 16)
                    load_x(n + 2, slot)
                if sample:
                    act.wait_ge(s["hT_sample_ready"], 1)
                else:
                    act.wait_ge(s["hT_ready"], n + 3)
                act.activation(flat(hT_high, slot), flat(hT, slot), ACT.Identity).then_inc(s["high_ready"], 1)
                at = bass.ds(n * P, P)
                act.dma_start(S["h2T"][:, :, at].rearrange("k p t -> p k t"), hT[:, slot]
                              ).then_inc(hT_stored[slot], 16)
            tiles(act, body)
            act.wait_ge(hT_stored[0], 16 * (TILES // 2 + 2))
            act.wait_ge(hT_stored[1], 16 * (TILES // 2 + 1))

        @block.vector
        def _(dve):
            dve.sem_inc(s["out_copied"], 2)
            dve.sem_inc(s["mix_split"], 2)
            flat = lambda buffer, slot: buffer[:, slot].rearrange("p k t -> p (k t)")

            def low_of_mix(n, slot):
                dve.wait_ge(s["mix_high_ready"], n + 1)
                dve.tensor_tensor(flat(mix_low, slot), flat(mixT, slot), flat(mix_high, slot).bitcast(F32),
                                  ALU.subtract).then_inc(s["mix_split"], 1)

            for k in range(DC):
                dve.wait_ge(s["w_high_ready"], k + 1)
                dve.tensor_tensor(w_low[:, k, :], w_chunk[:, k % W_SLOTS, :], w_high[:, k, :].bitcast(F32),
                                  ALU.subtract).then_inc(s["w_split"], 1)
                if k < 2:
                    low_of_mix(k, k)
            dve.wait_ge(s["lnrow_loaded"], 32)

            def body(n, slot, uses, sample):
                dve.wait_ge(s["out_done"], n + 3)
                dve.tensor_tensor(y[:, slot], ps_O[:, slot], K["gates"][:, 0, int(sample)], ALU.mult
                                  ).then_inc(s["out_copied"], 1)
                dve.drain()
                dve.wait_ge(x_loaded[slot], uses * 16 + 16)
                dve.scalar_tensor_tensor(x[:, slot], x[:, slot], ALPHA, y[:, slot], ALU.mult, ALU.add)
                dve.drain()
                layer_norm_stats(dve, x[:, slot:slot + 1, :], stats, mean_var, 1).then_inc(s["stats_done"], 1)
                dve.wait_ge(s["rstd_done"], n + 1)
                dve.tensor_scalar(x[:, slot], x[:, slot], mean_var[:, 0, 0:1], rstd[:, 0:1],
                                  ALU.subtract, ALU.mult)
                dve.drain()
                dve.tensor_tensor(x[:, slot], x[:, slot], ln_g[:], ALU.mult)
                dve.drain()
                dve.tensor_tensor(x[:, slot], x[:, slot], ln_b[:], ALU.add).then_inc(s["x1_ready"], 1)
                if two_ahead(n):
                    low_of_mix(n + 2, slot)
                if sample:
                    dve.wait_ge(s["hT_ps"], n + 3)
                    dve.wait_ge(hT_stored[slot], uses * 16 + 16)
                    dve.wait_ge(s["low_ready"], n + 1)
                    modulate_samples(dve, hT[:, slot], ps_T[:, slot], K["modT"], 2
                                     ).then_inc(s["hT_sample_ready"], 1)
            tiles(dve, body)


def modulate_samples(dve, hT, ps_T, modT, kind):
    split = lambda a, k: a[:, k, 0:P].rearrange("p (b t) -> p b t", b=DEC_B)
    by_sequence = lambda j, k: modT[:, j, k, 1:].unsqueeze(2).to_broadcast([P, DEC_B, DEC_T])
    for k in range(DC):
        dve.tensor_tensor(split(hT, k), split(ps_T, k), by_sequence(kind + 1, k), ALU.mult)
    dve.drain()
    for k in range(DC):
        last = dve.tensor_tensor(split(hT, k), split(hT, k), by_sequence(kind, k), ALU.add)
    return last


def stage_ffn(nc, K, IN, OUT, S):
    HIST = FFN_CONV - 1
    HR = DEC_B * HIST
    NL = HIST + HR
    WD = 4
    with ExitStack() as ctx:
        ctx.callback(nc.all_engine_barrier)
        sb = lambda name, shape: ctx.enter_context(nc.sbuf_tensor(name, shape, F32))
        ps = lambda name, shape: ctx.enter_context(nc.psum_tensor(name, shape, F32))
        sb_r = lambda name, shape: ctx.enter_context(nc.sbuf_tensor(name, shape, F32R))
        wgu = sb("w_gate_up", [P, 2, DC, P])
        wgu_high, wgu_low = (sb_r(f"w_gate_up_{n}", [P, 2, 2, DC, P]) for n in ("high", "low"))
        wd = sb("w_down_ring", [P, WD, 512])
        hT_high, hT_low = (sb_r(f"h2T_group_{n}", [P, DC, GROUP + P]) for n in ("high", "low"))
        act_T = sb("hidden_T", [P, FC, GROUP + P])
        x = sb("x1_group", [P, GT + 1, D])
        raw = sb("gate_raw", [P, 2, HIST + GROUP])
        conv = sb("gate_conv", [P, 2, GROUP])
        y = conv
        raw_s = sb("gate_raw_samples", [P, 2, DEC_B, HIST + DEC_T])
        conv_s = sb("gate_conv_samples", [P, 2, P])
        taps = sb("ffn_taps", [P, FC, FFN_CONV])
        hist = sb("ffn_hist", [P, FC, HIST])
        hist_s = sb("ffn_hist_samples", [P, FC, HR])
        last_raw = sb("ffn_last_raw", [P, FC, NL])
        rows = act_T[:].rearrange("p c t -> p (c t)")[:, 0:D_FF]
        ln_g, ln_b = sb("ln2_g_rows", [P, D]), sb("ln2_b_rows", [P, D])
        stats = sb("ln2_stats", [P, GT + 1, 2, 6])
        mean_var = sb("ln2_mean_var", [P, GT + 1, 2])
        rstd = sb("ln2_rstd", [P, GT + 1])
        shift = sb("ln2_shift", [P, GT + 1])
        minus_half, eps = sb("ln2_minus_half", [P, GT + 1]), sb("ln2_eps", [P, GT + 1])
        ps_gu = ps("ps_gate_up", [P, 2, 2, 512])
        ps_D = ps("ps_down", [P, GT, 512])
        s = signals(nc, ctx, "ffn", "rows_loaded lnrow_loaded hT_loaded high_ready low_ready0 low_ready1 x_loaded y_stored gu_done raw_ready "
                             "conv_done silu_done hidden_ready wd_used down_done down_copied "
                             "stats_done rstd_done y_ready taps_ps taps_ready last_kept last_ps "
                             "last_copied rows_stored shift_ready scaled")
        gu_loaded = [signal(nc, ctx, "ffn", f"gu_loaded{b}") for b in range(2)]
        wd_loaded = [signal(nc, ctx, "ffn", f"wd_loaded{b}") for b in range(WD)]

        def down_bank(t):
            return ps_D[:, t] if t < GT else ps_gu[:, 0, 1]

        def groups(engine, body):
            with engine.Fori(0, GROUPS - 1) as i:
                body(i, GT, False)
            body(GROUPS - 1, GT + 1, True)

        def groups_after(engine, body):
            body(0, GT, False, False)
            with engine.Fori(0, GROUPS - 2) as i:
                body(i + 1, GT, False, True)
            body(GROUPS - 1, GT + 1, True, True)

        block = ctx.enter_context(nc.Block())

        @block.sync
        def _(sp):
            w_gu = [IN[n][0].rearrange("(k p) f -> p k f", p=P) for n in ("w_gate", "w_up")]

            def load_gu(it, c):
                at = c % FC * P
                for j in range(2):
                    if not (isinstance(it, int) and it + c == 0):
                        sp.wait_ge(s[f"low_ready{j}"], it * FC + c)
                    sp.dma_start(wgu[:, j], w_gu[j][:, :, at:at + P]).then_inc(gu_loaded[j], 16)

            def body(it, tiles, last):
                for c in range(2, FC if last else FC + 2):
                    load_gu(it, c)
                for j in range(2 * FC):
                    half, c = j // FC, j % FC
                    sp.wait_ge(s["wd_used"], it * (2 * FC) + (j + 1))
                    sp.dma_start(wd[:, j % WD], IN["w_down"][0, c * P:(c + 1) * P, half * 512:half * 512 + 512]
                                 ).then_inc(wd_loaded[j % WD], 16)
            load_gu(0, 0)
            load_gu(0, 1)
            groups(sp, body)
            sp.wait_ge(s["last_copied"], 2)
            sp.dma_start(OUT["p_ffn_conv"].rearrange("l b t c -> (l b t) c"), rows[0:HIST, :]
                         ).then_inc(s["rows_stored"], 16)
            sp.dma_start(OUT["s_ffn_conv"].rearrange("l b t c -> (l b t) c"), rows[HIST:NL, :]
                         ).then_inc(s["rows_stored"], 16)
            sp.wait_ge(s["rows_stored"], 32)

        @block.gpsimd
        def _(pool):
            pool.memset(minus_half[:], -0.5)
            pool.memset(eps[:], LN_EPS)
            pool.drain()
            pool.dma_start(rows[0:FFN_CONV, :], IN["ffn_conv_w"][0]).then_inc(s["rows_loaded"], 16)
            pool.dma_start(rows[32:32 + HR, :], IN["state_ffn_conv"].rearrange("l b t c -> (l b t) c")
                           ).then_inc(s["rows_loaded"], 16)
            pool.dma_start(ln_g[:], row_broadcast(IN["ln2_g"])).then_inc(s["lnrow_loaded"], 16)
            pool.dma_start(ln_b[:], row_broadcast(IN["ln2_b"])).then_inc(s["lnrow_loaded"], 16)

            def load_hT(it):
                first = isinstance(it, int) and it == 0
                for at, src_at, n in [(0, it * GROUP, GROUP)] + [(GROUP, SEQ, P)] * first:
                    for dst, name in ((hT_high, "h2T"), (hT_low, "h2T_low")):
                        src = S[name][:, :, bass.ds(src_at, n)].rearrange("k p t -> p k t")
                        pool.dma_start(dst[:, :, at:at + n], src).then_inc(s["hT_loaded"], 16)

            def low(it, c):
                flat = lambda w: w.rearrange("p k f -> p (k f)")
                pool.wait_ge(s["high_ready"], it * (2 * FC) + (2 * c + 2))
                pool.tensor_tensor(flat(wgu_low[:, c % 2, 1]), flat(wgu[:, 1]), flat(wgu_high[:, c % 2, 1]).bitcast(F32),
                                   ALU.subtract
                                   ).then_inc(s["low_ready1"], 1)

            def load_x(it, tiles):
                pool.dma_start(x[:, 0:tiles], S["x1"][bass.ds(it * GROUP, tiles * P), :].rearrange(
                    "(t p) d -> p t d", p=P)).then_inc(s["x_loaded"], 16)

            def rstds(it, tiles):
                pool.wait_ge(s["stats_done"], it + 1)
                rstd_of(pool, rstd[:, 0:tiles], mean_var[:, 0:tiles, 1], eps[:, 0:tiles],
                        minus_half[:, 0:tiles]).then_inc(s["rstd_done"], 1)

            def store_y(it):
                pool.wait_ge(s["y_ready"], it + 1)
                pool.dma_start(OUT["y_prompt"][0, bass.ds(it * GROUP, GROUP), :].rearrange("(t p) d -> p t d", p=P),
                               x[:, 0:GT]).then_inc(s["y_stored"], 16)
                pool.wait_ge(s["y_stored"], it * 16 + 16)

            def body(it, tiles, last, after):
                for c in range(2, FC if last else FC + 2):
                    low(it, c)
                    if c == 3 and after:
                        rstds(it - 1, GT)
                    if c == 9 and after:
                        store_y(it - 1)
                        load_x(it, tiles)
                if not last:
                    pool.wait_ge(s["gu_done"], it * FC + (FC + 2))
                    load_hT(it + 1)

            load_hT(0)
            load_x(0, GT)
            low(0, 0)
            low(0, 1)
            groups_after(pool, body)
            rstds(GROUPS - 1, GT + 1)
            for t in range(GT + 1):
                pool.wait_ge(s["y_ready"], GROUPS + t)
                dst = (OUT["y_prompt"][0, (GROUPS - 1) * GROUP + t * P:(GROUPS - 1) * GROUP + (t + 1) * P, :]
                       if t < GT else OUT["y_sample"].rearrange("b t d -> (b t) d"))
                pool.dma_start(dst, x[:, t]).then_inc(s["y_stored"], 16)
            pool.wait_ge(s["y_stored"], 16 * (GROUPS + GT))

        @block.tensor
        def _(pe):
            pe.sem_inc(s["gu_done"], 2)
            pe.sem_inc(s["wd_used"], WD)
            pe.wait_ge(s["rows_loaded"], 32)
            for c in range(FC):
                pe.transpose(ps_gu[:, 0, 0, c * FFN_CONV:(c + 1) * FFN_CONV], rows[0:FFN_CONV, c * P:(c + 1) * P],
                             K["ident"][0:FFN_CONV, 0:FFN_CONV])
                last = pe.transpose(ps_gu[:, 0, 1, c * HR:(c + 1) * HR], rows[32:32 + HR, c * P:(c + 1) * P],
                                    K["ident"][32:32 + HR, 32:32 + HR])
            last.then_inc(s["taps_ps"], 1)
            pe.wait_ge(s["taps_ready"], 1)

            def split_product(out, b, j, tokens):
                for k in range(DC):
                    w_high, h_high = wgu_high[:, b, j, k, :], hT_high[:, k, tokens]
                    w_low, h_low = wgu_low[:, b, j, k, :], hT_low[:, k, tokens]
                    pe.matmul(out, w_high, h_high, start=(k == 0), stop=False)
                    pe.matmul(out, w_high, h_low, start=False, stop=False)
                    last = pe.matmul(out, w_low, h_high, start=False, stop=(k == DC - 1))
                return last

            def body(it, tiles, last_group):
                pe.wait_ge(s["hT_loaded"], it * 32 + 64)
                for c in range(FC):
                    b = c % 2
                    pe.wait_ge(s["hidden_ready"], it * FC + (c + 1))
                    for j in range(2):
                        pe.wait_ge(s[f"low_ready{j}"], it * FC + (c + 1))
                        last = split_product(ps_gu[:, b, j], b, j, slice(0, GROUP))
                    if last_group:
                        if c == 0:
                            pe.wait_ge(s["down_copied"], it * (2 * GT) + GT)
                        for j in range(2):
                            last = split_product(ps_D[:, 2 * b + j, 0:P], b, j, slice(GROUP, GROUP + P))
                    last.then_inc(s["gu_done"], 1)
                if last_group:
                    pe.wait_ge(s["hidden_ready"], it * FC + (FC + 2))
                for j in range(2 * FC):
                    half, c = j // FC, j % FC
                    pe.wait_ge(wd_loaded[j % WD], it * (2 * FC // WD * 16) + (j // WD * 16 + 16))
                    pe.wait_ge(s["hidden_ready"], it * FC + (c + 3))
                    for t in range(tiles):
                        if c == 0 and (t < GT or half):
                            pe.wait_ge(s["down_copied"], it * (2 * GT) + (half * GT + t + 1))
                        last = pe.matmul(down_bank(t), act_T[:, c, t * P:(t + 1) * P], wd[:, j % WD],
                                         start=(c == 0), stop=(c == FC - 1))
                        if c == FC - 1 and t < tiles - 1:
                            last.then_inc(s["down_done"], 1)
                    last.then_inc(s["wd_used"], 1)
            groups(pe, body)
            pe.wait_ge(s["last_kept"], 1)
            for part in range(2):
                pe.wait_ge(s["down_copied"], GT + 2 * (GROUPS * GT + 1))
                for c in range(part * 16, min(FC, part * 16 + 16)):
                    q = c - part * 16
                    dst = (ps_D[0:NL, q // 4] if part == 0 else ps_gu[0:NL, 0, q // 4])
                    last = pe.transpose(dst[:, (q % 4) * P:(q % 4 + 1) * P], last_raw[:, c, :], K["ident"][:])
                last.then_inc(s["last_ps"], 1)

        @block.scalar
        def _(act):
            def high(it, c):
                for j in range(2):
                    act.wait_ge(gu_loaded[j], it * (FC * 16) + (c * 16 + 16))
                    act.activation(wgu_high[:, c % 2, j].rearrange("p k f -> p (k f)"),
                                   wgu[:, j].rearrange("p k f -> p (k f)"), ACT.Identity
                                   ).then_inc(s["high_ready"], 1)

            def body(it, tiles, last_group):
                for c in range(FC):
                    b = c % 2
                    act.wait_ge(s["gu_done"], it * FC + (c + 3))
                    if last_group:
                        act.activation(raw_s[:, b, :, HIST:], ps_D[:, 2 * b, 0:P].rearrange("p (b t) -> p b t", b=DEC_B),
                                       ACT.Identity)
                    act.activation(raw[:, b, HIST:], ps_gu[:, b, 0, :], ACT.Identity).then_inc(s["raw_ready"], 1)
                    act.wait_ge(s["conv_done"], it * FC + (c + 1))
                    if last_group:
                        act.activation(conv_s[:, b], conv_s[:, b], ACT.Silu)
                    act.activation(conv[:, b], conv[:, b], ACT.Silu).then_inc(s["silu_done"], 1)
                    if not last_group or c + 2 < FC:
                        high(it, c + 2)
            high(0, 0)
            high(0, 1)
            groups(act, body)
            act.wait_ge(s["last_ps"], 1)
            act.activation(rows[0:NL, 0:2048], ps_D[0:NL].rearrange("p a b -> p (a b)"), ACT.Identity
                           ).then_inc(s["last_copied"], 1)
            act.wait_ge(s["last_ps"], 2)
            act.activation(rows[0:NL, 2048:D_FF], ps_gu[0:NL, 0].rearrange("p a b -> p (a b)")[:, 0:D_FF - 2048],
                           ACT.Identity).then_inc(s["last_copied"], 1)
            act.wait_ge(s["shift_ready"], 1)
            for t in range(GT + 1):
                act.activation(x[:, t], x[:, t], ACT.Identity, bias=shift[:, t:t + 1], scale=rstd[:, t:t + 1]
                               ).then_inc(s["scaled"], 1)

        @block.vector
        def _(dve):
            dve.sem_inc(s["hidden_ready"], 2)
            dve.sem_inc(s["down_copied"], GT)
            dve.wait_ge(s["taps_ps"], 1)
            dve.tensor_copy(taps[:].rearrange("p c t -> p (c t)"), ps_gu[:, 0, 0, 0:FC * FFN_CONV])
            dve.tensor_copy(hist_s[:].rearrange("p c t -> p (c t)"), ps_gu[:, 0, 1, 0:FC * HR])
            dve.memset(hist[:], 0.0).then_inc(s["taps_ready"], 1)
            dve.drain()
            dve.wait_ge(s["lnrow_loaded"], 32)

            def low(it, c):
                flat = lambda w: w.rearrange("p k f -> p (k f)")
                dve.wait_ge(s["high_ready"], it * (2 * FC) + (2 * c + 1))
                dve.tensor_tensor(flat(wgu_low[:, c % 2, 0]), flat(wgu[:, 0]), flat(wgu_high[:, c % 2, 0]).bitcast(F32),
                                  ALU.subtract
                                  ).then_inc(s["low_ready0"], 1)

            def normalize(t):
                dve.tensor_scalar(x[:, t], x[:, t], mean_var[:, t, 0:1], rstd[:, t:t + 1], ALU.subtract, ALU.mult)
                dve.drain()
                dve.tensor_tensor(x[:, t], x[:, t], ln_g[:], ALU.mult)
                dve.drain()
                return dve.tensor_tensor(x[:, t], x[:, t], ln_b[:], ALU.add)

            def conv_3(dst, src, c):
                for i in range(FFN_CONV):
                    if i == 0:
                        last = dve.tensor_scalar(dst, src(i), taps[:, c, 0:1], None, ALU.mult)
                    else:
                        dve.drain()
                        last = dve.scalar_tensor_tensor(dst, src(i), taps[:, c, i:i + 1], dst, ALU.mult, ALU.add)
                return last

            def body(it, tiles, last_group, after):
                by_seq = lambda t: t.rearrange("p (b t) -> p b t", b=DEC_B)
                for c in range(FC):
                    b = c % 2
                    dve.tensor_copy(raw[:, b, 0:HIST], hist[:, c])
                    if last_group:
                        dve.tensor_copy(raw_s[:, b, :, 0:HIST], by_seq(hist_s[:, c]))
                    dve.drain()
                    dve.wait_ge(s["raw_ready"], it * FC + (c + 1))
                    if last_group:
                        conv_3(by_seq(conv_s[:, b]), lambda i: raw_s[:, b, :, i:i + DEC_T], c)
                    conv_3(conv[:, b], lambda i: raw[:, b, i:i + GROUP], c).then_inc(s["conv_done"], 1)
                    if last_group:
                        dve.tensor_copy(last_raw[:, c, 0:HIST], raw[:, b, GROUP:GROUP + HIST])
                        dve.tensor_copy(by_seq(last_raw[:, c, HIST:NL]), raw_s[:, b, :, DEC_T:DEC_T + HIST])
                    else:
                        dve.tensor_copy(hist[:, c], raw[:, b, GROUP:GROUP + HIST])
                    dve.wait_ge(s["silu_done"], it * FC + (c + 1))
                    if last_group:
                        dve.tensor_tensor(act_T[:, c, GROUP:], conv_s[:, b], ps_D[:, 2 * b + 1, 0:P], ALU.mult)
                    dve.tensor_tensor(act_T[:, c, 0:GROUP], conv[:, b], ps_gu[:, b, 1, :], ALU.mult
                                      ).then_inc(s["hidden_ready"], 1)
                    if not last_group or c + 2 < FC:
                        low(it, c + 2)
                    if after and c == 0:
                        layer_norm_stats(dve, x, stats, mean_var, GT).then_inc(s["stats_done"], 1)
                    if after and 1 <= c <= GT:
                        if c == 1:
                            dve.wait_ge(s["rstd_done"], it)
                        last = normalize(c - 1)
                        if c == GT:
                            last.then_inc(s["y_ready"], 1)
                if last_group:
                    dve.drain()
                    dve.sem_inc(s["last_kept"], 1)
                dve.wait_ge(s["x_loaded"], it * 16 + 16)
                for half in range(2):
                    cols = slice(half * 512, half * 512 + 512)
                    for t in range(tiles):
                        if t < tiles - 1:
                            dve.wait_ge(s["down_done"], it * (2 * GT - 2) + (half * (tiles - 1) + t + 1))
                        else:
                            dve.wait_ge(s["wd_used"], it * (2 * FC) + ((half + 1) * FC + WD))
                        dve.tensor_tensor(y[:, (half * tiles + t) % 2], down_bank(t), K["gates"][:, 1, t // GT, cols], ALU.mult
                                          ).then_inc(s["down_copied"], 1)
                        dve.drain()
                        dve.scalar_tensor_tensor(x[:, t, cols], x[:, t, cols], ALPHA, y[:, (half * tiles + t) % 2],
                                                 ALU.mult, ALU.add)
                dve.drain()
            low(0, 0)
            low(0, 1)
            groups_after(dve, body)
            layer_norm_stats(dve, x, stats, mean_var, GT + 1).then_inc(s["stats_done"], 1)
            dve.wait_ge(s["rstd_done"], GROUPS)
            dve.scalar_tensor_tensor(shift[:], mean_var[:, :, 0], -1.0, rstd[:], ALU.mult, ALU.mult
                                     ).then_inc(s["shift_ready"], 1)
            for t in range(GT + 1):
                dve.wait_ge(s["scaled"], t + 1)
                dve.tensor_tensor(x[:, t], x[:, t], ln_g[:], ALU.mult)
                dve.drain()
                dve.tensor_tensor(x[:, t], x[:, t], ln_b[:], ALU.add).then_inc(s["y_ready"], 1)


def stage_window(nc, K, M, IN, OUT, S):
    TILES = SEQ // P
    H, KEYS, SKEYS = A_HEADS, 2 * P, WINDOW + DEC_T
    SC = HD ** -0.5
    with ExitStack() as ctx:
        ctx.callback(nc.all_engine_barrier)
        sb = lambda name, shape: ctx.enter_context(nc.sbuf_tensor(name, shape, F32))
        ps = lambda name, shape: ctx.enter_context(nc.psum_tensor(name, shape, F32))
        qT = sb("aqT", [P, 4, A_GROUP, P])
        kT = sb("akT", [P, 4, P])
        v_rows = sb("av_rows", [P, 4, P])
        mask = sb("window_mask", [P, 2, KEYS])
        sc = sb("scores", [P, 2, H, KEYS])
        pT = sb("probsT", [P, A_KV, A_GROUP, 2, P])
        mix = sb("mixA", [P, 2, A_GROUP, P])
        sink = sb("sink_rows", [P, H])
        top, neg_top, sink_less = sb("top", [P, 2, H]), sb("neg_top", [P, 2, H]), sb("sink_less", [P, 2, H])
        sink_exp, den = sb("sink_exp", [P, 2, H]), sb("den", [P, 2, H])
        s_cache_k = sb("s_cache_k", [P, DEC_B, P])
        s_cache_v = sb("s_cache_v", [P, DEC_B, P])
        s_new_v = sb("s_new_v", [DEC_T, DEC_B, P])
        s_kT = sb("s_kT", [P, DEC_B, SKEYS])
        s_qT = sb("s_qT_masked", [P, A_GROUP, DEC_B, P])
        ak_rows = sb("ak_rows", [P, 2, P])
        ps_S = ps("ps_scores", [P, A_KV, 1024])
        ps_T = ps("ps_probsT", [P, 1024])
        ps_O = ps("ps_window_out", [P, A_KV, 512])
        s = signals(nc, ctx, "window", "sink_loaded blank_ready masks_ready scores_done scores_read bias_ready "
                             "exp_done p_ready pT_ps pT_copied_act pT_copied_dve out_done mix_copied "
                             "cache_loaded s_kT_ps s_kT_ready rows_ps rows_ready q_masked moved "
                             "s_tail_ps s_tail_copied s_vnew_loaded")
        loaded = [signal(nc, ctx, "window", f"qkv_loaded{j}") for j in range(4)]
        mix_stored = [signal(nc, ctx, "window", f"mixA_stored{b}") for b in range(2)]
        block = ctx.enter_context(nc.Block())

        def quads(engine, body):
            with engine.Fori(0, TILES // 4 - 1) as i:
                for j in range(4):
                    body(i * 4 + j, j, i, False)
            for j in range(4):
                body(TILES - 4 + j, j, TILES // 4 - 1, j == 3)

        def copy_probs(engine, pT, ps_T, v, width):
            copy = (lambda o, i: engine.activation(o, i, ACT.Identity)) if v == 0 else engine.tensor_copy
            split = ps_T[:, 0:A_GROUP * 2 * P].rearrange("p (g w t) -> p g w t", g=A_GROUP, w=2)
            if width == KEYS:
                return copy(pT[:, v].rearrange("p g w t -> p (g w t)"), ps_T[:, 0:A_GROUP * 2 * P])
            copy(pT[:, v, :, 0], split[:, :, 0])
            return copy(pT[0:width - P, v, :, 1], split[0:width - P, :, 1])

        @block.sync
        def _(sp):
            def load(n, j):
                at = bass.ds(n * P, P)
                sp.dma_start(qT[:, j], S["qkT"][QKT_AQ:QKT_AK, :, at].rearrange("g p t -> p g t")
                             ).then_inc(loaded[j], 16)
                sp.dma_start(kT[:, j], S["qkT"][QKT_AK, :, at]).then_inc(loaded[j], 16)
                sp.dma_start(v_rows[:, j], S["av"][at, :]).then_inc(loaded[j], 16)

            for b in range(2):
                sp.sem_inc(mix_stored[b], 16)

            def store(n, b):
                sp.wait_ge(s["mix_copied"], n * 2 + 4)
                sp.dma_start(S["mixT"][0:A_GROUP, :, bass.ds(n * P, P)].rearrange("g p t -> p g t"), mix[:, b]
                             ).then_inc(mix_stored[b], 16)

            for j in range(3):
                load(j, j)

            def body(n, j, i, last):
                sp.wait_ge(s["out_done"], n + 1)
                load(n + 3, (j + 3) % 4)
                store(n, j % 2)
            with sp.Fori(0, TILES // 4 - 1) as i:
                for j in range(4):
                    body(i * 4 + j, j, i, False)
            body(TILES - 4, 0, 0, False)
            sp.wait_ge(s["out_done"], TILES - 2)
            load(TILES, 0)
            for n in range(TILES - 3, TILES):
                store(n, n % 2)
            sp.dma_start(s_new_v[:], S["av"][SEQ:TOKENS, :].rearrange("(b t) d -> t b d", b=DEC_B)
                         ).then_inc(s["s_vnew_loaded"], 16)
            for c, (name, dst) in enumerate((("cache_a_k", s_cache_k), ("cache_a_v", s_cache_v))):
                sp.dma_start(dst[:], IN[name][0].rearrange("b w h d -> w b (h d)")).then_inc(s["cache_loaded"], 16)
            rows = lambda a: a.rearrange("l b w h d -> (l b) w (h d)")
            keep = WINDOW - DEC_T
            sp.dma_start(rows(OUT["p_a_v"])[0], S["av"][SEQ - WINDOW:SEQ, :]).then_inc(s["moved"], 16)
            sp.dma_start(rows(OUT["s_a_v"])[:, keep:, :], S["av"][SEQ:TOKENS, :].rearrange(
                "(b t) d -> b t d", b=DEC_B)).then_inc(s["moved"], 16)
            for a in ("k", "v"):
                sp.dma_start(rows(OUT[f"s_a_{a}"])[:, 0:keep, :], rows(IN[f"cache_a_{a}"])[:, DEC_T:, :]
                             ).then_inc(s["moved"], 16)
            sp.wait_ge(s["rows_ready"], 1)
            sp.dma_start(rows(OUT["p_a_k"])[0], ak_rows[:, 0]).then_inc(s["moved"], 16)
            for b in range(DEC_B):
                sp.dma_start(rows(OUT["s_a_k"])[b, keep:, :], ak_rows[b * DEC_T:(b + 1) * DEC_T, 1]
                             ).then_inc(s["moved"], 16)
            store(TILES, 0)
            sp.wait_ge(s["moved"], 16 * (5 + DEC_B))
            sp.wait_ge(mix_stored[0], 16 * (TILES // 2 + 2))
            sp.wait_ge(mix_stored[1], 16 * (TILES // 2 + 1))

        @block.gpsimd
        def _(pool):
            pool.dma_start(sink[:], row_broadcast(IN["a_sinks"])).then_inc(s["sink_loaded"], 16)
            pool.memset(kT[:, 3], 0.0)
            pool.memset(v_rows[:, 3], 0.0).then_inc(s["blank_ready"], 1)
            pool.memset(mask[:], 0.0)
            pool.memset(s_qT[:], 0.0)
            pool.drain()
            pool.memset(mask[64:P, 1, 0:64], NEG)
            pool.drain()
            pool.memset(mask[0:64, 1, P + 64:], NEG)
            pool.drain()
            pool.memset(mask[:, 0, 0:P], NEG)
            pool.drain()
            pool.memset(mask[0:64, 0, P + 64:], NEG).then_inc(s["masks_ready"], 1)
            pool.drain()
            build_delta_masks(pool, M)

        @block.tensor
        def _(pe):
            pe.wait_ge(s["blank_ready"], 1)

            def scores(n, j, uses):
                pe.wait_ge(loaded[j], uses * 48 + 48)
                pe.wait_ge(s["scores_read"], n + 1)
                for v in range(A_KV):
                    rows = slice(v * HD, (v + 1) * HD)
                    for g in range(A_GROUP):
                        for w, slot in ((0, (j + 3) % 4), (1, j)):
                            c0 = g * KEYS + w * P
                            last = pe.matmul(ps_S[:, v, c0:c0 + P], qT[rows, j, g, :], kT[rows, slot, :],
                                             start=True, stop=True)
                last.then_inc(s["scores_done"], 1)

            def probs_turned(n, b, width):
                for v in range(A_KV):
                    pe.wait_ge(s["p_ready"], n * 2 + (v + 1))
                    if v == 0:
                        pe.wait_ge(s["pT_copied_dve"], n + 1)
                    else:
                        pe.wait_ge(s["pT_copied_act"], n + 1)
                    for g in range(A_GROUP):
                        for w in range(2):
                            keys = min(P, width - w * P)
                            o = (g * 2 + w) * P
                            last = pe.transpose(ps_T[0:keys, o:o + P],
                                                sc[:, b, v * A_GROUP + g, w * P:w * P + keys], K["ident"][:])
                    last.then_inc(s["pT_ps"], 1)

            def out(n, j):
                pe.wait_ge(s["pT_copied_dve"], n + 2)
                pe.wait_ge(s["mix_copied"], n * 2 + 2)
                for v in range(A_KV):
                    for g in range(A_GROUP):
                        for w, slot in ((0, (j + 3) % 4), (1, j)):
                            last = pe.matmul(ps_O[:, v, g * P:(g + 1) * P], v_rows[:, slot, :],
                                             pT[:, v, g, w, :], start=(w == 0), stop=(w == 1))
                last.then_inc(s["out_done"], 1)

            scores(0, 0, 0)

            def body(n, j, i, last):
                if not last:
                    scores(n + 1, (j + 1) % 4, i + (1 if j == 3 else 0))
                probs_turned(n, j % 2, KEYS)
                out(n, j)
            quads(pe, body)

            pe.wait_ge(loaded[0], 48 * (TILES // 4 + 1))
            pe.wait_ge(s["pT_copied_dve"], TILES + 1)
            for a, slot in enumerate((3, 0)):
                last = pe.transpose(ps_T[:, a * P:(a + 1) * P], kT[:, slot, :], K["ident"][:])
            last.then_inc(s["rows_ps"], 1)
            pe.wait_ge(s["cache_loaded"], 32)
            pe.wait_ge(s["rows_ready"], 1)
            for b in range(DEC_B):
                last = pe.transpose(ps_T[:, b * P:(b + 1) * P], s_cache_k[:, b, :], K["ident"][:])
            last.then_inc(s["s_kT_ps"], 1)
            pe.wait_ge(s["s_kT_ready"], 1)
            pe.wait_ge(s["q_masked"], 1)
            pe.wait_ge(s["scores_read"], TILES + 1)
            for v in range(A_KV):
                rows = slice(v * HD, (v + 1) * HD)
                for g in range(A_GROUP):
                    for b in range(DEC_B):
                        last = pe.matmul(ps_S[:, v, g * KEYS:g * KEYS + SKEYS], s_qT[rows, g, b, :], s_kT[rows, b, :],
                                         start=(b == 0), stop=(b == DEC_B - 1))
            last.then_inc(s["scores_done"], 1)
            probs_turned(TILES, 0, SKEYS)
            pe.wait_ge(s["pT_copied_dve"], TILES + 2)
            pe.wait_ge(s["mix_copied"], TILES * 2 + 2)
            pe.wait_ge(s["s_vnew_loaded"], 16)
            for v in range(A_KV):
                for g in range(A_GROUP):
                    for b in range(DEC_B):
                        q = slice(b * DEC_T, (b + 1) * DEC_T)
                        o = ps_O[:, v, g * P + b * DEC_T:g * P + (b + 1) * DEC_T]
                        pe.matmul(o, s_cache_v[:, b, :], pT[:, v, g, 0, q], start=True, stop=False)
                        last = pe.matmul(o, s_new_v[:, b, :], pT[0:DEC_T, v, g, 1, q], start=False, stop=True)
            last.then_inc(s["out_done"], 1)

        @block.scalar
        def _(act):
            def exps(n, b, width):
                act.wait_ge(s["bias_ready"], n + 1)
                for h in range(H):
                    act.activation(sc[:, b, h, 0:width], sc[:, b, h, 0:width], ACT.Exp, bias=neg_top[:, b, h:h + 1],
                                   scale=SC, accum_out=den[:, b, h:h + 1])
                act.activation(sink_exp[:, b], sink_less[:, b], ACT.Exp).then_inc(s["exp_done"], 1)

            def body(n, b, uses, width, follows):
                act.wait_ge(s["pT_ps"], n * 2 + 1)
                copy_probs(act, pT, ps_T, 0, width).then_inc(s["pT_copied_act"], 1)
                if follows:
                    exps(n + 1, 1 - b, KEYS)
                act.wait_ge(s["out_done"], n + 1)
                act.wait_ge(mix_stored[b], uses * 16 + 16)
                act.activation(mix[0:HD, b].rearrange("p g t -> p (g t)"), ps_O[0:HD, 0, 0:A_GROUP * P],
                               ACT.Identity).then_inc(s["mix_copied"], 1)
            exps(0, 0, KEYS)
            quads(act, lambda n, j, i, last: body(n, j % 2, i * 2 + j // 2, KEYS, not last))
            exps(TILES, 0, SKEYS)
            body(TILES, 0, TILES // 2, SKEYS, False)

        @block.vector
        def _(dve):
            dve.sem_inc(s["scores_read"], 1)
            dve.sem_inc(s["pT_copied_dve"], 1)
            dve.sem_inc(s["mix_copied"], 2)
            dve.wait_ge(s["sink_loaded"], 16)
            dve.wait_ge(s["masks_ready"], 1)

            def shifted(n, b, width, which):
                dve.wait_ge(s["scores_done"], n + 1)
                for v in range(A_KV):
                    src = ps_S[:, v, 0:A_GROUP * KEYS].rearrange("p (g k) -> p g k", g=A_GROUP)[:, :, 0:width]
                    dst = sc[:, b, v * A_GROUP:(v + 1) * A_GROUP, 0:width]
                    if which is None:
                        last = dve.tensor_copy(dst, src)
                    else:
                        last = dve.tensor_tensor(dst, src, mask[:, which].unsqueeze(1).to_broadcast(
                            [P, A_GROUP, KEYS]), ALU.add)
                last.then_inc(s["scores_read"], 1)
                dve.drain()
                dve.tensor_reduce(top[:, b], sc[:, b, :, 0:width], AX.X, ALU.max)
                dve.drain()
                dve.scalar_tensor_tensor(top[:, b], top[:, b], SC, sink[:], ALU.mult, ALU.max)
                dve.drain()
                dve.tensor_scalar(neg_top[:, b], top[:, b], -1.0, None, ALU.mult)
                dve.tensor_tensor(sink_less[:, b], sink[:], top[:, b], ALU.subtract).then_inc(s["bias_ready"], 1)

            def normalised(n, b, width):
                dve.wait_ge(s["exp_done"], n + 1)
                dve.tensor_tensor(den[:, b], den[:, b], sink_exp[:, b], ALU.add)
                dve.drain()
                dve.reciprocal(den[:, b], den[:, b])
                dve.drain()
                for v in range(A_KV):
                    for g in range(A_GROUP):
                        h = v * A_GROUP + g
                        last = dve.tensor_scalar(sc[:, b, h, 0:width], sc[:, b, h, 0:width], den[:, b, h:h + 1], None,
                                                 ALU.mult)
                    last.then_inc(s["p_ready"], 1)

            def copied(n, width):
                dve.wait_ge(s["pT_ps"], n * 2 + 2)
                copy_probs(dve, pT, ps_T, 1, width).then_inc(s["pT_copied_dve"], 1)

            def out_copied(n, b, uses):
                dve.wait_ge(s["out_done"], n + 1)
                dve.wait_ge(mix_stored[b], uses * 16 + 16)
                dve.tensor_copy(mix[HD:P, b].rearrange("p g t -> p (g t)"), ps_O[HD:P, 1, 0:A_GROUP * P]
                                ).then_inc(s["mix_copied"], 1)

            shifted(0, 0, KEYS, 0)

            def body(n, j, i, last):
                copied(n, KEYS)
                if not last:
                    shifted(n + 1, (j + 1) % 2, KEYS, 1)
                    normalised(n + 1, (j + 1) % 2, KEYS)
                out_copied(n, j % 2, i * 2 + j // 2)
            normalised(0, 0, KEYS)
            quads(dve, body)
            dve.wait_ge(s["rows_ps"], 1)
            dve.tensor_copy(ak_rows[:].rearrange("p a t -> p (a t)"), ps_T[:, 0:2 * P]).then_inc(s["rows_ready"], 1)
            dve.wait_ge(loaded[0], 48 * (TILES // 4 + 1))
            for b in range(DEC_B):
                q = slice(b * DEC_T, (b + 1) * DEC_T)
                last = dve.tensor_copy(s_qT[:, :, b, q], qT[:, 0, :, q])
            last.then_inc(s["q_masked"], 1)
            dve.tensor_copy(s_kT[:, :, WINDOW:], kT[:, 0, :].rearrange("p (b t) -> p b t", b=DEC_B))
            dve.wait_ge(s["s_kT_ps"], 1)
            dve.tensor_copy(s_kT[:, :, 0:WINDOW], ps_T[:].rearrange("p (b k) -> p b k", b=DEC_B)
                            ).then_inc(s["s_kT_ready"], 1)
            shifted(TILES, 0, SKEYS, None)
            normalised(TILES, 0, SKEYS)
            copied(TILES, SKEYS)
            out_copied(TILES, 0, TILES // 2)


def softplus_part(act, z, e):
    act.activation(e, z, ACT.Abs)
    act.drain()
    act.activation(e, e, ACT.Exp, scale=-1.0)
    act.drain()
    return act.activation(e, e, ACT.Ln, bias=1.0)


def stage_stick(nc, K, IN, S):
    H = C_HEADS
    with ExitStack() as ctx:
        ctx.callback(nc.all_engine_barrier)
        sb = lambda name, shape: ctx.enter_context(nc.sbuf_tensor(name, shape, F32))
        ps = lambda name, shape: ctx.enter_context(nc.psum_tensor(name, shape, F32))
        qT = sb("cqT", [P, 2, 2, GROUP])
        kT = sb("ckT_block", [P, 2, 2, P])
        v_rows = sb("cv_block", [P, 2, H * HD])
        e = sb("stick_e", [P, H, GROUP])
        sp_ = sb("stick_softplus", [P, H, GROUP])
        a = sb("stick_weight", [P, H, GROUP])
        mix = sb("mixC", [P, 2, GROUP])
        ps_z = ps("ps_z", [P, 2, GROUP])
        ps_C = ps("ps_later", [P, H, GROUP])
        ps_O = ps("ps_stick_out", [P, 2, GROUP])
        s = signals(nc, ctx, "stick", "q_loaded q_ready z_done chain_done sp_done T_done u_done exp_done "
                             "a_masked item_done o_done o_copied mix_stored")
        loaded = [signal(nc, ctx, "stick", f"ckv_loaded{b}") for b in range(2)]
        block = ctx.enter_context(nc.Block())

        first_beta = [sum(4 * q + 4 for q in range(Q)) for Q in range(GROUPS + 1)]

        def blocks(engine, body):
            for Q in range(GROUPS):
                b0 = first_beta[Q]
                for j in (3, 2, 1, 0):
                    nxt = ((4 - j) % 2, max(j - 1, 0) * P)
                    if Q == 0 and j == 0:
                        nxt = None
                    body(Q, b0 + 3 - j, (3 - j) % 2, 4 * Q + j, j * P, True, nxt, j == 3)
                pairs = 2 * Q
                if pairs > 1:
                    with engine.Fori(0, pairs - 1) as i:
                        for r in range(2):
                            body(Q, i * 2 + (b0 + 4 + r), r, i * -2 + (4 * Q - 1 - r), 0, False, (1 - r, 0), False)
                if pairs:
                    i = pairs - 1
                    for r in range(2):
                        body(Q, b0 + 4 + 2 * i + r, r, 1 - r, 0, False, (1, 0) if r == 0 else None, False)

        @block.sync
        def _(sp):
            def body(Q, beta, slot, kb, c0, diag, follows, first):
                if first:
                    if Q >= 2:
                        sp.wait_ge(s["o_done"], Q - 1)
                    sp.dma_start(qT[:, Q % 2], S["qkT"][QKT_CQ:QKT_CK, :, Q * GROUP:(Q + 1) * GROUP].rearrange(
                        "a p t -> p a t")).then_inc(s["q_loaded"], 16)
                sp.wait_ge(s["item_done"], beta * H + H)
                at = bass.ds(kb * P, P)
                sp.dma_start(kT[:, slot], S["qkT"][QKT_CK:QKT_N, :, at].rearrange("a p t -> p a t")
                             ).then_inc(loaded[slot], 16)
                sp.dma_start(v_rows[:, slot], S["cv"][at, :]).then_inc(loaded[slot], 16)
            blocks(sp, body)

        @block.tensor
        def _(pe):
            pe.sem_inc(s["item_done"], 2 * H)

            def z(Q, beta, slot, c0, h):
                rows = slice(h % 2 * HD, h % 2 * HD + HD)
                if h == 0:
                    pe.wait_ge(loaded[slot], (beta - slot) * 16 + 32)
                pe.wait_ge(s["sp_done"], beta * H + (h + 1))
                pe.matmul(ps_z[:, h % 2, c0:], kT[rows, slot, h // 2, :], qT[rows, Q % 2, h // 2, c0:],
                          start=True, stop=True).then_inc(s["z_done"], 1)

            def rest_and_pv(Q, beta, slot, c0, h, diag, first, last):
                if not last:
                    pe.wait_ge(s["u_done"], beta * H + (h + 1))
                    pe.matmul(ps_C[:, h, c0:], K["upto"][:], sp_[:, h, c0:], start=False, stop=True,
                              skip_group_check=True)
                if diag:
                    pe.wait_ge(s["a_masked"], Q * 4 * H + (beta - first_beta[Q]) * H + h + 1)
                else:
                    pe.wait_ge(s["exp_done"], beta * H + (h + 1))
                    pe.wait_ge(s["a_masked"], (Q + 1) * 4 * H)
                if first and Q:
                    pe.wait_ge(s["o_copied"], Q)
                rows = slice(h % 2 * HD, h % 2 * HD + HD)
                pe.matmul(ps_O[rows, h // 2, c0:], v_rows[:, slot, h * HD:(h + 1) * HD], a[:, h, c0:],
                          start=first, stop=last, skip_group_check=True).then_inc(s["item_done"], 1)

            def body(Q, beta, slot, kb, c0, diag, follows, first):
                if first:
                    pe.wait_ge(s["q_ready"], Q + 1)
                    z(Q, beta, slot, c0, 0)
                    z(Q, beta, slot, c0, 1)
                for h in range(H):
                    pe.wait_ge(s["sp_done"], beta * H + (h + 3))
                    pe.matmul(ps_C[:, h, c0:], K["later"][:], sp_[:, h, c0:], start=first, stop=True,
                              skip_group_check=True).then_inc(s["T_done"], 1)
                    if h + 2 < H:
                        z(Q, beta, slot, c0, h + 2)
                    elif follows is not None:
                        z(Q, beta + 1, follows[0], follows[1], h - 2)
                    if h > 0:
                        rest_and_pv(Q, beta, slot, c0, h - 1, diag, first, follows is None)
                    elif not first:
                        was_diag = diag or (isinstance(beta, int) and beta == first_beta[Q] + 4)
                        rest_and_pv(Q, beta - 1, 1 - slot, c0 + P if diag else 0, H - 1,
                                    was_diag, diag and beta == first_beta[Q] + 1, False)
                if follows is None:
                    rest_and_pv(Q, beta, slot, c0, H - 1, diag, first, True)
                    pe.drain()
                    pe.sem_inc(s["o_done"], 1)
            blocks(pe, body)

        @block.scalar
        def _(act):
            act.preload_act_table_set(LOG_EXP_TABLES)
            act.sem_inc(s["mix_stored"], 16)

            def chain(beta, c0, h):
                act.wait_ge(s["z_done"], beta * H + (h + 1))
                softplus_part(act, ps_z[:, h % 2, c0:], e[:, h, c0:]).then_inc(s["chain_done"], 1)

            def body(Q, beta, slot, kb, c0, diag, follows, first):
                if first:
                    chain(beta, c0, 0)
                    chain(beta, c0, 1)
                for h in range(H):
                    if h + 2 < H:
                        chain(beta, c0, h + 2)
                    elif follows is not None:
                        chain(beta + 1, follows[1], h - 2)
                    act.wait_ge(s["u_done"], beta * H + (h + 1))
                    act.activation(a[:, h, c0:], a[:, h, c0:], ACT.Exp).then_inc(s["exp_done"], 1)
                if follows is None:
                    act.wait_ge(s["o_done"], Q + 1)
                    act.wait_ge(s["mix_stored"], 16 * (Q + 1))
                    act.activation(mix[:].rearrange("p a t -> p (a t)"), ps_O[:].rearrange("p a t -> p (a t)"),
                                   ACT.Identity).then_inc(s["o_copied"], 1)
                    act.wait_ge(s["o_copied"], Q + 1)
                    act.dma_start(S["mixT"][6:8, :, Q * GROUP:(Q + 1) * GROUP].rearrange("a p t -> p a t"), mix[:]
                                  ).then_inc(s["mix_stored"], 16)
            blocks(act, body)
            act.wait_ge(s["mix_stored"], 16 * (GROUPS + 1))

        @block.gpsimd
        def _(pool):
            def body(Q, beta, slot, kb, c0, diag, follows, first):
                if diag:
                    for h in range(H):
                        pool.wait_ge(s["exp_done"], beta * H + (h + 1))
                        pool.tensor_tensor(a[:, h, c0:c0 + P], a[:, h, c0:c0 + P], K["before"][:], ALU.mult
                                           ).then_inc(s["a_masked"], 1)
            for Q in range(GROUPS):
                for j in (3, 2, 1, 0):
                    body(Q, first_beta[Q] + 3 - j, 0, 0, j * P, True, None, False)

        @block.vector
        def _(dve):
            dve.sem_inc(s["sp_done"], 2)

            def softplus_and_sigmoid(beta, c0, h, diag):
                dve.wait_ge(s["chain_done"], beta * H + (h + 1))
                last = dve.scalar_tensor_tensor(sp_[:, h, c0:], ps_z[:, h % 2, c0:], 0.0, e[:, h, c0:],
                                                ALU.max, ALU.add)
                if diag:
                    dve.drain()
                    dve.tensor_tensor(sp_[:, h, c0:c0 + P], sp_[:, h, c0:c0 + P], K["before"][:], ALU.mult)
                dve.scalar_tensor_tensor(a[:, h, c0:], ps_z[:, h % 2, c0:], 0.0, e[:, h, c0:],
                                         ALU.min, ALU.subtract).then_inc(s["sp_done"], 1)

            def body(Q, beta, slot, kb, c0, diag, follows, first):
                if first:
                    dve.wait_ge(s["q_loaded"], 16 * (Q + 1))
                    q = qT[:, Q % 2].rearrange("p a t -> p (a t)")
                    dve.tensor_scalar(q, q, HD ** -0.5, None, ALU.mult).then_inc(s["q_ready"], 1)
                    softplus_and_sigmoid(beta, c0, 0, True)
                    softplus_and_sigmoid(beta, c0, 1, True)
                for h in range(H):
                    dve.wait_ge(s["T_done"], beta * H + (h + 1))
                    dve.tensor_tensor(a[:, h, c0:], a[:, h, c0:], ps_C[:, h, c0:], ALU.subtract
                                      ).then_inc(s["u_done"], 1)
                    if h + 2 < H:
                        softplus_and_sigmoid(beta, c0, h + 2, diag)
                    elif follows is not None:
                        softplus_and_sigmoid(beta + 1, follows[1], h - 2, diag and c0 > 0)
            blocks(dve, body)


def stage_stick_samples(nc, K, IN, S):
    H, PAIRS = C_HEADS, 2
    BLOCKS = PAST // P
    COLS = DEC_B * H * DEC_T
    with ExitStack() as ctx:
        ctx.callback(nc.all_engine_barrier)
        sb = lambda name, shape: ctx.enter_context(nc.sbuf_tensor(name, shape, F32))
        ps = lambda name, shape: ctx.enter_context(nc.psum_tensor(name, shape, F32))
        q_new = sb("s_cqT", [P, PAIRS, P])
        k_new = sb("s_ckT", [P, PAIRS, P])
        v_new = sb("s_cv_new", [DEC_T, DEC_B, H * HD])
        q_diag = sb("s_cq_diag", [P, DEC_B, PAIRS, 2 * DEC_T])
        k_rows = sb("s_ck_block", [P, 2, DEC_B, H * HD])
        v_rows = sb("s_cv_block", [P, 2, DEC_B, H * HD])
        kT = sb("s_ckT_block", [P, 2, DEC_B, PAIRS, P])
        e = sb("s_stick_e", [P, COLS])
        sp_ = sb("s_stick_softplus", [P, 2, COLS])
        a = sb("s_stick_weight", [P, 2, COLS])
        mix = sb("s_mixC", [P, PAIRS, P])
        ps_K = ps("ps_s_kT", [P, DEC_B, PAIRS, P])
        ps_z = ps("ps_s_z", [P, COLS])
        ps_C = ps("ps_s_later", [P, COLS])
        ps_O = ps("ps_s_stick_out", [P, COLS])
        s = signals(nc, ctx, "stick_samples", "new_loaded q_ready zeroed kT_ps kT_ready_act kT_ready_dve z_done chain_done "
                             "sp_done T_done u_done exp_done a_masked pv_done o_copied mix_stored")
        k_loaded = [signal(nc, ctx, "stick_samples", f"s_ck_loaded{b}") for b in range(2)]
        v_loaded = [signal(nc, ctx, "stick_samples", f"s_cv_loaded{b}") for b in range(2)]
        block = ctx.enter_context(nc.Block())

        def cached(engine, body):
            with engine.Fori(0, BLOCKS // 2 - 1) as i:
                for r in range(2):
                    body(i * 2 + (1 + r), r, i, False)
            for r in range(2):
                body(BLOCKS - 1 + r, r, BLOCKS // 2 - 1, r == 1)

        @block.sync
        def _(sp):
            for dst, src in ((q_new, S["qkT"][QKT_CQ:QKT_CK, :, SEQ:TOKENS].rearrange("a p t -> p a t")),
                             (k_new, S["qkT"][QKT_CK:QKT_N, :, SEQ:TOKENS].rearrange("a p t -> p a t")),
                             (v_new, S["cv"][SEQ:TOKENS, :].rearrange("(b t) d -> t b d", b=DEC_B))):
                sp.dma_start(dst[:], src).then_inc(s["new_loaded"], 16)

            def body(n, slot, uses, last):
                at = bass.ds(n * -P + PAST, P)
                src = lambda name: IN[name][0][:, at].rearrange("b k h d -> k b (h d)")
                sp.wait_ge(s["kT_ps"], n)
                sp.dma_start(k_rows[:, slot], src("cache_c_k")).then_inc(k_loaded[slot], 16)
                sp.wait_ge(s["pv_done"], n)
                sp.dma_start(v_rows[:, slot], src("cache_c_v")).then_inc(v_loaded[slot], 16)
            cached(sp, body)
            sp.wait_ge(s["o_copied"], 1)
            sp.dma_start(S["mixT"][6:8, :, SEQ:TOKENS].rearrange("a p t -> p a t"), mix[:]
                         ).then_inc(s["mix_stored"], 16)
            sp.wait_ge(s["mix_stored"], 16)

        @block.tensor
        def _(pe):
            pe.sem_inc(s["kT_ps"], 2)
            pe.sem_inc(s["pv_done"], 1)

            def turn(n, slot, uses):
                pe.wait_ge(k_loaded[slot], uses * 16 + 16)
                pe.wait_ge(s["kT_ready_act"], n)
                pe.wait_ge(s["kT_ready_dve"], n)
                for b in range(DEC_B):
                    for p in range(PAIRS):
                        last = pe.transpose(ps_K[:, b, p, :], k_rows[:, slot, b, p * P:(p + 1) * P], K["ident"][:])
                last.then_inc(s["kT_ps"], 1)

            def z(n, slot):
                pe.wait_ge(s["kT_ready_act"], n + 1)
                pe.wait_ge(s["kT_ready_dve"], n + 1)
                pe.wait_ge(s["sp_done"], n)
                for b in range(DEC_B):
                    for p in range(PAIRS):
                        c0 = (b * PAIRS + p) * 2 * DEC_T
                        last = pe.matmul(ps_z[:, c0:c0 + 2 * DEC_T], kT[:, slot, b, p, :], q_diag[:, b, p, :],
                                         start=True, stop=True)
                last.then_inc(s["z_done"], 1)

            def pv(slot, first, last_block):
                for b in range(DEC_B):
                    for p in range(PAIRS):
                        c0 = (b * PAIRS + p) * 2 * DEC_T
                        v = (v_new[:, b, p * P:(p + 1) * P] if first else v_rows[:, slot, b, p * P:(p + 1) * P])
                        w = a[0:DEC_T if first else P, slot, c0:c0 + 2 * DEC_T]
                        last = pe.matmul(ps_O[:, c0:c0 + 2 * DEC_T], v, w, start=(first and c0 == 0),
                                         stop=last_block, skip_group_check=True)
                last.then_inc(s["pv_done"], 1)

            pe.wait_ge(s["new_loaded"], 48)
            pe.wait_ge(s["q_ready"], 1)
            for b in range(DEC_B):
                for p in range(PAIRS):
                    c0 = (b * PAIRS + p) * 2 * DEC_T
                    last = pe.matmul(ps_z[0:DEC_T, c0:c0 + 2 * DEC_T], k_new[:, p, b * DEC_T:(b + 1) * DEC_T],
                                     q_diag[:, b, p, :], start=True, stop=True)
            last.then_inc(s["z_done"], 1)
            turn(1, 0, 0)
            pe.wait_ge(s["sp_done"], 1)
            pe.matmul(ps_C[:], K["later"][:], sp_[:, 1], start=True, stop=True, skip_group_check=True
                      ).then_inc(s["T_done"], 1)
            z(1, 0)
            turn(2, 1, 0)
            pe.wait_ge(s["u_done"], 1)
            pe.matmul(ps_C[:], K["upto"][:], sp_[:, 1], start=False, stop=True, skip_group_check=True)
            pe.wait_ge(s["a_masked"], 1)
            pv(1, True, False)

            def body(n, slot, uses, last):
                pe.wait_ge(s["sp_done"], n + 1)
                pe.matmul(ps_C[:], K["later"][:], sp_[:, slot], start=False, stop=True, skip_group_check=True
                          ).then_inc(s["T_done"], 1)
                if not last:
                    z(n + 1, 1 - slot)
                    if not (isinstance(n, int) and n == BLOCKS - 1):
                        turn(n + 2, slot, uses + 1)
                    pe.wait_ge(s["u_done"], n + 1)
                    pe.matmul(ps_C[:], K["upto"][:], sp_[:, slot], start=False, stop=True, skip_group_check=True)
                pe.wait_ge(s["exp_done"], n + 1)
                pe.wait_ge(v_loaded[slot], uses * 16 + 16)
                pv(slot, False, last)
            cached(pe, body)

        halves = {"act": slice(0, DEC_B // 2), "dve": slice(DEC_B // 2, DEC_B)}

        @block.scalar
        def _(act):
            act.preload_act_table_set(LOG_EXP_TABLES)
            act.sem_inc(s["kT_ready_act"], 1)

            def copy_kT(n, slot):
                act.wait_ge(s["kT_ps"], n + 2)
                act.activation(kT[:, slot, halves["act"]].rearrange("p b a k -> p (b a k)"),
                               ps_K[:, halves["act"]].rearrange("p b a k -> p (b a k)"), ACT.Identity
                               ).then_inc(s["kT_ready_act"], 1)

            def chain(n, rows):
                act.wait_ge(s["z_done"], n + 1)
                softplus_part(act, ps_z[0:rows], e[0:rows]).then_inc(s["chain_done"], 1)

            chain(0, DEC_T)
            copy_kT(1, 0)
            chain(1, P)
            act.wait_ge(s["u_done"], 1)
            act.activation(a[0:DEC_T, 1], a[0:DEC_T, 1], ACT.Exp).then_inc(s["exp_done"], 1)
            copy_kT(2, 1)

            def body(n, slot, uses, last):
                if not last:
                    chain(n + 1, P)
                act.wait_ge(s["u_done"], n + 1)
                act.activation(a[:, slot], a[:, slot], ACT.Exp).then_inc(s["exp_done"], 1)
                if not last and not (isinstance(n, int) and n == BLOCKS - 1):
                    copy_kT(n + 2, slot)
            cached(act, body)

        @block.gpsimd
        def _(pool):
            pool.memset(q_diag[:], 0.0)
            pool.memset(sp_[:, 1], 0.0).then_inc(s["zeroed"], 1)
            pool.wait_ge(s["exp_done"], 1)
            weights = a[0:DEC_T, 1].rearrange("p (c i) -> p c i", i=DEC_T)
            pool.tensor_tensor(weights, weights, K["before"][0:DEC_T, 0:DEC_T].unsqueeze(1).to_broadcast(
                [DEC_T, COLS // DEC_T, DEC_T]), ALU.mult).then_inc(s["a_masked"], 1)

        @block.vector
        def _(dve):
            dve.sem_inc(s["kT_ready_dve"], 1)
            dve.wait_ge(s["new_loaded"], 48)
            dve.wait_ge(s["zeroed"], 1)
            for h2 in range(2):
                rows = slice(h2 * HD, (h2 + 1) * HD)
                for p in range(PAIRS):
                    last = dve.tensor_scalar(q_diag[rows, :, p, h2 * DEC_T:(h2 + 1) * DEC_T],
                                             q_new[rows, p, :].rearrange("p (b t) -> p b t", b=DEC_B),
                                             HD ** -0.5, None, ALU.mult)
            last.then_inc(s["q_ready"], 1)

            def copy_kT(n, slot):
                dve.wait_ge(s["kT_ps"], n + 2)
                dve.tensor_copy(kT[:, slot, halves["dve"]].rearrange("p b a k -> p (b a k)"),
                                ps_K[:, halves["dve"]].rearrange("p b a k -> p (b a k)")
                                ).then_inc(s["kT_ready_dve"], 1)

            def softplus_and_sigmoid(n, slot, rows, masked):
                dve.wait_ge(s["chain_done"], n + 1)
                if not masked:
                    dve.wait_ge(s["pv_done"], n)
                dve.scalar_tensor_tensor(sp_[0:rows, slot], ps_z[0:rows], 0.0, e[0:rows], ALU.max, ALU.add)
                if masked:
                    dve.drain()
                    cols = sp_[0:rows, slot].rearrange("p (c i) -> p c i", i=DEC_T)
                    dve.tensor_tensor(cols, cols, K["before"][0:DEC_T, 0:DEC_T].unsqueeze(1).to_broadcast(
                        [DEC_T, COLS // DEC_T, DEC_T]), ALU.mult)
                dve.scalar_tensor_tensor(a[0:rows, slot], ps_z[0:rows], 0.0, e[0:rows], ALU.min, ALU.subtract
                                         ).then_inc(s["sp_done"], 1)

            def less_later(n, slot, rows):
                dve.wait_ge(s["T_done"], n + 1)
                dve.tensor_tensor(a[0:rows, slot], a[0:rows, slot], ps_C[0:rows], ALU.subtract).then_inc(s["u_done"], 1)

            softplus_and_sigmoid(0, 1, DEC_T, True)
            copy_kT(1, 0)
            less_later(0, 1, DEC_T)
            copy_kT(2, 1)
            softplus_and_sigmoid(1, 0, P, False)

            def body(n, slot, uses, last):
                less_later(n, slot, P)
                if not last:
                    if not (isinstance(n, int) and n == BLOCKS - 1):
                        copy_kT(n + 2, slot)
                    softplus_and_sigmoid(n + 1, 1 - slot, P, False)
            cached(dve, body)
            dve.wait_ge(s["pv_done"], BLOCKS + 2)
            for h2 in range(2):
                rows = slice(h2 * HD, (h2 + 1) * HD)
                src = ps_O[rows].rearrange("p (b a h t) -> p a b h t", b=DEC_B, a=PAIRS, h=2)
                for p in range(PAIRS):
                    last = dve.tensor_copy(mix[rows, p, :].rearrange("p (b t) -> p b t", b=DEC_B),
                                           src[:, p, :, h2, :])
            last.then_inc(s["o_copied"], 1)


def same_block(pool, view, first, size, fill):
    n, inner = view.shape[1], view.shape[2]
    pool.affine_select(out=view, in_=view, compare_op=ALU.is_ge, fill=fill, base=-first,
                       pattern=[[-size, n], [0, inner]], channel_multiplier=1)
    pool.drain()
    pool.affine_select(out=view, in_=view, compare_op=ALU.is_ge, fill=fill, base=first + size - 1,
                       pattern=[[size, n], [0, inner]], channel_multiplier=-1)
    pool.drain()


DELTA_LEVELS = 6
DELTA_MASKS = {"ident": [P, HD], "expo_mask": [P, 2, 2, HD], "level": [P, DELTA_LEVELS, HD], "level_1T": [P, HD],
               "run_sum": [P, 2, P], "seq_sum": [P, 2, P], "in_seq": [P, 2, DEC_B]}


def delta_masks(nc, ctx):
    return {n: ctx.enter_context(nc.sbuf_tensor(f"delta_{n}", s, F32)) for n, s in DELTA_MASKS.items()}


def build_delta_masks(pool, M):
    C, LEVELS = HD, DELTA_LEVELS
    ident, expo_mask, level, level_1T, run_sum, seq_sum, in_seq = (M[n] for n in DELTA_MASKS)
    for t in (ident, level, in_seq, run_sum, seq_sum):
        pool.memset(t[:], 1.0)
    for t in (expo_mask, level_1T):
        pool.memset(t[:], 0.0)
    pool.drain()
    for c in range(2):
        r = slice(c * C, (c + 1) * C)
        pool.affine_select(out=ident[r], in_=ident[r], compare_op=ALU.is_equal, fill=0.0, base=0,
                           pattern=[[-1, C]], channel_multiplier=1)
        pool.drain()
        for sample in range(2):
            for kind in range(2):
                m = expo_mask[r, sample, kind, :]
                pool.affine_select(out=m, in_=m, compare_op=ALU.is_ge, fill=NEG, base=-kind,
                                   pattern=[[1, C]], channel_multiplier=-1)
                pool.drain()
                if sample:
                    same_block(pool, m.rearrange("p (b t) -> p b t", t=DEC_T), 0, DEC_T, NEG)
        for l in range(LEVELS):
            b = 1 << l
            m = level[r, l, :].rearrange("p (n a t) -> p n a t", a=2, t=b)
            pool.memset(m[:, :, 1, :], 0.0)
            same_block(pool, m[:, :, 0, :], 0, 2 * b, 0.0)
            pool.affine_select(out=m[:, :, 0, :], in_=m[:, :, 0, :], compare_op=ALU.is_ge, fill=0.0,
                               base=-b, pattern=[[-2 * b, C // (2 * b)], [0, b]], channel_multiplier=1)
            pool.drain()
        m = level_1T[r].rearrange("p (n a) -> p n a", a=2)[:, :, 1]
        pool.affine_select(out=m, in_=m, compare_op=ALU.not_equal, fill=1.0, base=0,
                           pattern=[[-2, C // 2]], channel_multiplier=1)
        pool.drain()
    for sample, size in ((0, C), (1, DEC_T)):
        m = in_seq[:, sample, 0:P // size].unsqueeze(2)
        same_block(pool, m, 0, size, 0.0)
        for t in (run_sum, seq_sum):
            same_block(pool, t[:, sample].rearrange("p (b t) -> p b t", t=size), 0, size, 0.0)
        pool.affine_select(out=run_sum[:, sample], in_=run_sum[:, sample], compare_op=ALU.is_ge,
                           fill=0.0, base=0, pattern=[[1, P]], channel_multiplier=-1)
    pool.drain()


def stage_delta(nc, K, M, IN, OUT, S):
    TILES = SEQ // P
    H, J, C = B_HEADS, B_HEADS // 2, HD
    HH = H // 2
    W = H * HD
    LEVELS = DELTA_LEVELS
    S_LEVELS = 4
    GATE = {0: slice(0, H), 1: slice(H, 2 * H)}
    BETA, KBE, KD, QG = range(4)
    with ExitStack() as ctx:
        ctx.callback(nc.all_engine_barrier)
        sb = lambda name, shape: ctx.enter_context(nc.sbuf_tensor(name, shape, F32))
        ps = lambda name, shape: ctx.enter_context(nc.psum_tensor(name, shape, F32))
        chT = sb("d_convT", [P, 2, CONV_CHUNKS, P])
        zba = sb("d_zba", [P, 2, ZBA_W])
        squares = sb("d_squares", [P, H, P])
        soft_in, soft_e, soft = (sb(f"d_soft_{n}", [P, 2 * H]) for n in ("in", "e", "out"))
        logs = sb("d_norm_logs", [P, 2 * H])
        g, g_seq = sb("d_g", [P, H]), sb("d_g_by_seq", [P, 2, DEC_B, J])
        sums = sb("d_sums", [P, 2 * H + DEC_B * J])
        minus_gc = sb("d_minus_gc", [P, H])
        fac_log, fac = sb("d_factor_logs", [P, 4, H]), sb("d_factors", [P, 2, 4, H])
        decay = sb("d_decay", [P, 2, DEC_B, J])
        diag = sb("d_log_diag", [P, H, 2, C])
        wgt = sb("d_weights", [P, H, 2, C])
        mats = sb("d_matrices", [P, 2, H, 2, C])
        X = sb("d_inverse", [P, H, 2, C])
        Y = sb("d_LX", [P, H, C])
        v_beta, k_beta, k_decay = (sb(f"d_{n}", [P, 2, W]) for n in ("v_beta", "k_beta", "k_decay"))
        wT = sb("d_wT", [P, J, P])
        v_new = sb("d_v_new", [P, W])
        state, faded = sb("d_state", [P, J, P]), sb("d_state_faded", [P, J, P])
        out, out_sq = sb("d_out", [P, W]), sb("d_out_sq", [P, W])
        out_ss, out_r = sb("d_out_ss", [P, H]), sb("d_out_r", [P, H])
        gate = sb("d_gate", [P, 2, W])
        qT = sb("d_qT", [P, 2, J, P])
        zero = sb("d_zero", [P, H])
        mix = sb("d_mix", [P, J, P])
        s_state, s_faded = sb("d_s_state", [P, DEC_B, J, P]), sb("d_s_faded", [P, DEC_B, J, P])
        s_wT, s_qT = sb("d_s_wT", [P, DEC_B, J, P]), sb("d_s_qT", [P, DEC_B, J, P])
        s_k_decay = sb("d_s_k_decay", [P, DEC_B, W])
        ident, expo_mask, level, level_1T, run_sum, seq_sum, in_seq = (M[n] for n in DELTA_MASKS)
        eps = sb("d_eps", [P, 1])
        a_log, dt_bias, norm_w = sb("d_a_log", [P, H]), sb("d_dt_bias", [P, H]), sb("d_norm_w", [P, HD])
        ps_kv = ps("ps_d_kv", [P, 2, 512])
        ps_A = ps("ps_d_qk", [P, 2, 512])
        ps_Z = ps("ps_d_Z", [P, 2, 512])
        ps_Y = ps("ps_d_Y", [P, 2, 512])
        ps_s = ps_A[:, 1, HH * 2 * C:]
        SS, GC, SEQ_SUM = 0, 12, 24
        s = signals(nc, ctx, "delta", "masks_ready blank_ready pe_passed rows_loaded a_log_exp squares_ready soft_in_ready soft_ready "
                             "kv_done qk_done ss_done logs_ready g_ready sums_done fac_log_ready fac_ready "
                             "diag_ready G_done0 G_done1 expo_ready0 expo_ready1 wgt_ready0 wgt_ready1 "
                             "mats_ready0 mats_ready1 X_ready0 X_ready1 Y_done0 Y_done1 "
                             "Y_ready0 Y_ready1 Z_done0 Z_done1 kv_ready wT_done wT_ready v_done "
                             "v_ready state_done state_ready out_done out_ss_ready out_r_ready gate_ready "
                             "out_ready outT_done qT_ready mix_ready s_state_loaded s_operands s_k_decay_ready "
                             "state_stored")
        loaded = [signal(nc, ctx, "delta", f"d_loaded{b}") for b in range(2)]
        mix_stored = signal(nc, ctx, "delta", "d_mix_stored")
        block = ctx.enter_context(nc.Block())
        halves = [slice(0, HH), slice(HH, H)]
        by_head = lambda t: t.rearrange("p (h d) -> p h d", d=HD)

        def tiles(engine, body):
            body(0, 0, 0, "prompt")
            with engine.Fori(0, TILES // 2 - 1) as i:
                body(i * 2 + 1, 1, i, "prompt")
                body(i * 2 + 2, 0, i + 1, "prompt")
            body(TILES - 1, 1, TILES // 2 - 1, "sample")
            body(TILES, 0, TILES // 2, None)

        def ahead(prepare, n, slot, uses, follows):
            if follows is not None:
                prepare(n + 1, 1 - slot, uses + slot, follows == "sample")

        def flat(t):
            return t.rearrange("p h a c -> p (h a c)")

        def at(h):
            return h % 2 * J + h // 2

        @block.gpsimd
        def _(pool):
            for row, src in ((a_log, "b_a_log"), (dt_bias, "b_dt_bias"), (norm_w, "b_norm_w")):
                pool.dma_start(row[:], row_broadcast(IN[src])).then_inc(s["rows_loaded"], 16)
            for t in (zero, state):
                pool.memset(t[:], 0.0)
            pool.memset(eps[:], RMS_EPS)
            pool.drain()
            pool.sem_inc(s["masks_ready"], 1)
            pool.wait_ge(s["rows_loaded"], 48)

            def prepare(n, slot, uses, sample):
                pool.wait_ge(loaded[slot], uses * 32 + 32)
                pool.wait_ge(s["ss_done"], n + 1)
                pool.tensor_tensor(squares[:].rearrange("p f t -> p (f t)"),
                                   chT[:, slot, 0:H].rearrange("p f t -> p (f t)"),
                                   chT[:, slot, 0:H].rearrange("p f t -> p (f t)"), ALU.mult
                                   ).then_inc(s["squares_ready"], 1)
                pool.wait_ge(s["g_ready"], n + 1)
                pool.tensor_tensor(soft_in[:, GATE[0]], zero[:], zba[:, slot, W:W + H], ALU.subtract)
                pool.tensor_tensor(soft_in[:, GATE[1]], zba[:, slot, W + H:], dt_bias[:], ALU.add
                                   ).then_inc(s["soft_in_ready"], 1)
                pool.wait_ge(s["out_ready"], n + 1)
                pool.wait_ge(s["out_done"], n + 1)
                pool.tensor_tensor(by_head(gate[:, slot]), by_head(zba[:, slot, 0:W]),
                                   norm_w[:].unsqueeze(1).to_broadcast([P, H, HD]), ALU.mult
                                   ).then_inc(s["gate_ready"], 1)
                if not sample:
                    pool.tensor_copy(qT[:, slot].rearrange("p j t -> p (j t)"),
                                     chT[:, slot, 0:J].rearrange("p j t -> p (j t)")).then_inc(s["qT_ready"], 1)
                else:
                    for b in range(DEC_B):
                        t = slice(b * DEC_T, (b + 1) * DEC_T)
                        pool.tensor_copy(s_qT[:, b, :, t], chT[:, slot, 0:J, t])
                    pool.drain()
                    pool.sem_inc(s["qT_ready"], 1)
            pool.sem_inc(s["ss_done"], 1)
            pool.sem_inc(s["g_ready"], 1)
            pool.sem_inc(s["out_done"], 2)
            pool.sem_inc(s["out_ready"], 2)
            prepare(0, 0, 0, False)
            tiles(pool, lambda *tile: ahead(prepare, *tile))

        @block.sync
        def _(sp):
            def load(n, slot):
                rows = bass.ds(n * P, P)
                sp.dma_start(chT[:, slot], S["convT"][:, :, rows].rearrange("f p t -> p f t")
                             ).then_inc(loaded[slot], 16)
                sp.dma_start(zba[:, slot], S["zba"][rows, :]).then_inc(loaded[slot], 16)

            sp.sem_inc(mix_stored, 16)
            load(0, 0)
            load(1, 1)
            sp.wait_ge(s["blank_ready"], 1)
            for hh in range(2):
                r = slice(hh * HD, (hh + 1) * HD)
                src = IN["state_b_ssm"][0].rearrange("b (j a) k v -> a k (b j) v", a=2)[hh]
                sp.dma_start(s_state[r].rearrange("p b j v -> p (b j) v")[:, :, r], src
                             ).then_inc(s["s_state_loaded"], 16)


            def body(n, slot, uses, follows):
                if follows is not None and not (isinstance(n, int) and n == TILES - 1):
                    sp.wait_ge(s["qk_done"], n + 1)
                    sp.wait_ge(s["qT_ready"], n + 1)
                    load(n + 2, slot)
                sp.wait_ge(s["mix_ready"], n + 3)
                sp.dma_start(S["mixT"][A_GROUP:A_GROUP + J, :, bass.ds(n * P, P)].rearrange("j p t -> p j t"),
                             mix[:]).then_inc(mix_stored, 16)
            tiles(sp, body)
            sp.wait_ge(s["state_ready"], 1 + 2 * TILES + DEC_B)
            for hh in range(2):
                r = slice(hh * HD, (hh + 1) * HD)
                dst = OUT["p_b_ssm"][0, 0].rearrange("(j a) k v -> a k j v", a=2)[hh]
                sp.dma_start(dst, state[r, :, r]).then_inc(s["state_stored"], 16)
                dst = OUT["s_b_ssm"][0].rearrange("b (j a) k v -> a k (b j) v", a=2)[hh]
                sp.dma_start(dst, s_state[r].rearrange("p b j v -> p (b j) v")[:, :, r]
                             ).then_inc(s["state_stored"], 16)
            sp.wait_ge(s["state_stored"], 64)
            sp.wait_ge(mix_stored, 16 * (TILES + 2))

        @block.tensor
        def _(pe):
            def wait(name, value):
                pe.wait_ge(s[name], value)
                pe.sem_inc(s["pe_passed"], 1)

            def quadrants(outs, lhs, rhs, half):
                for c in range(2):
                    for j in range(J):
                        r = slice(c * C, (c + 1) * C)
                        i = half * J + j
                        last = pe.matmul(outs(r, j), lhs(r, i), rhs(r, i), start=True, stop=True)
                return last

            def norms(n, slot, uses, sample):
                pe.wait_ge(s["squares_ready"], n + 1)
                for f in range(H):
                    last = pe.matmul(ps_s[:, SS + 2 * f:SS + 2 * f + 2], squares[:, f, :], in_seq[:, 0, 0:2],
                                     start=True, stop=True)
                last.then_inc(s["ss_done"], 1)

            def sums_and_kv(n, slot, uses, sample):
                pe.wait_ge(loaded[slot], uses * 32 + 32)
                pe.wait_ge(s["out_ss_ready"], n + 1)
                for f in range(2):
                    for j in range(J):
                        last = pe.transpose(ps_kv[:, f, j * P:(j + 1) * P], chT[:, slot, (f + 1) * J + j, :],
                                            K["ident"][:])
                last.then_inc(s["kv_done"], 1)
                kind, seqs = int(sample), DEC_B if sample else 2
                pe.wait_ge(s["g_ready"], n + 2)
                pe.wait_ge(s["logs_ready"], n + 1)
                pe.matmul(ps_s[:, GC:GC + H], run_sum[:, kind, :], g[:], start=True, stop=True)
                pe.matmul(ps_s[:, GC + H:GC + 2 * H], seq_sum[:, kind, :], g[:], start=True, stop=True)
                for hh in range(2):
                    r = slice(hh * HD, (hh + 1) * HD)
                    last = pe.matmul(ps_s[r, SEQ_SUM:SEQ_SUM + seqs * J], K["ones"][:, r],
                                     g_seq[:, hh, 0:seqs].rearrange("p b j -> p (b j)"), start=True, stop=True)
                last.then_inc(s["sums_done"], 1)

            def products(n, slot, uses, sample):
                pe.wait_ge(s["mix_ready"], n + 1)
                wait("fac_log_ready", n + 1)
                for h in range(H):
                    r = slice(h % 2 * HD, h % 2 * HD + HD)
                    for c in range(2):
                        cols = slice(c * C, (c + 1) * C)
                        o = h // 2 * 2 * C
                        last = pe.matmul(ps_A[cols, h % 2, o:o + 2 * C].rearrange("p (a t) -> p a t", a=2),
                                         chT[r, slot, J + h // 2, cols], chT[r, slot, h // 2:2 * J:J, cols],
                                         start=True, stop=True)
                last.then_inc(s["qk_done"], 1)
                pe.wait_ge(s["diag_ready"], n + 1)
                pe.wait_ge(s["kv_ready"], n + 1)
                for half in range(2):
                    pe.matmul(ps_kv[:, half, 0:HH * 2 * C], seq_sum[:, 0, :], flat(diag[:, halves[half]]),
                              start=True, stop=True).then_inc(s[f"G_done{half}"], 1)

            def turn_L(n, slot, uses, sample):
                for half in range(2):
                    wait(f"mats_ready{half}", n + 1)
                    if half == 0:
                        wait("mats_ready1", n + 1)
                    quadrants(lambda r, j: ps_A[r, half, j * C:(j + 1) * C],
                              lambda r, i: mats[r, slot, i, 1, :], lambda r, i: K["ident"][r, r], half
                              ).then_inc(s[f"Y_done{half}"], 1)

            def turn_out(n):
                pe.wait_ge(s["out_ready"], n + 3)
                for j in range(J):
                    last = pe.transpose(ps_A[:, 0, j * P:(j + 1) * P], out[:, j * P:(j + 1) * P], K["ident"][:])
                last.then_inc(s["outT_done"], 1)

            def body(n, slot, uses, follows):
                sample = follows is None
                tile = (n, slot, uses, follows)
                levels = S_LEVELS if sample else LEVELS
                X_at, Y_at = n * LEVELS, n * (LEVELS - 1)
                for l in range(1, levels):
                    for half in range(2):
                        wait(f"X_ready{half}", X_at + l)
                        quadrants(lambda r, j: ps_Y[r, half, j * C:(j + 1) * C],
                                  lambda r, i: mats[r, slot, i, 1, :], lambda r, i: X[r, i, 0, :], half
                                  ).then_inc(s[f"Y_done{half}"], 1)
                    for half in range(2):
                        wait(f"Y_ready{half}", Y_at + l)
                        if l < levels - 1:
                            quadrants(lambda r, j: ps_Z[r, half, j * 2 * C:j * 2 * C + C],
                                      lambda r, i: X[r, i, 1, :], lambda r, i: Y[r, i, :], half)
                        quadrants(lambda r, j: ps_Z[r, half, j * 2 * C + C:(j + 1) * 2 * C],
                                  lambda r, i: Y[r, i, :], lambda r, i: X[r, i, 1, :], half
                                  ).then_inc(s[f"Z_done{half}"], 1)
                    if l == 1:
                        ahead(norms, *tile)
                    if l == 2:
                        ahead(sums_and_kv, *tile)
                    if l == 3 and not (isinstance(n, int) and n == 0):
                        turn_out(n - 1)
                    if l == 4:
                        ahead(products, *tile)
                for half in range(2):
                    wait(f"X_ready{half}", X_at + levels)
                wait("kv_ready", n + 1)
                for h in range(H):
                    rows = slice(h % 2 * HD, h % 2 * HD + HD)
                    for c in range(2):
                        r = slice(c * C, (c + 1) * C)
                        last = pe.matmul(ps_Y[rows, c, h // 2 * C:(h // 2 + 1) * C],
                                         k_beta[r, slot, h * HD:(h + 1) * HD], X[r, at(h), 1, :],
                                         start=True, stop=True)
                last.then_inc(s["wT_done"], 1)
                for h in range(H):
                    for c in range(2):
                        r = slice(c * C, (c + 1) * C)
                        pe.matmul(ps_Z[r, 0, h * HD:(h + 1) * HD], X[r, at(h), 1, :],
                                  v_beta[r, slot, h * HD:(h + 1) * HD],
                                  start=(h == 0), stop=False, skip_group_check=True)
                if follows is not None:
                    for half in range(2):
                        wait(f"expo_ready{half}", n + 2)

                def intra(c):
                    r = slice(c * C, (c + 1) * C)
                    for h in range(H):
                        last = pe.matmul(ps_kv[r, 1, h * HD:(h + 1) * HD], mats[r, slot, at(h), 0, :],
                                         v_new[r, h * HD:(h + 1) * HD], start=True, stop=True)
                    return last

                pe.wait_ge(s["wT_ready"], n + 1)
                pe.wait_ge(s["qT_ready"], n + 1)
                if not sample:
                    for c in range(2):
                        r = slice(c * C, (c + 1) * C)
                        pe.wait_ge(s["state_ready"], n * 2 + (c + 1))
                        for j in range(J):
                            last = pe.matmul(ps_Z[r, 0, j * P:(j + 1) * P], wT[:, j, r], state[:, j, :],
                                             start=False, stop=True, skip_group_check=True)
                        last.then_inc(s["v_done"], 1)
                        for j in range(J):
                            pe.matmul(ps_kv[r, 0, j * P:(j + 1) * P], qT[:, slot, j, r], state[:, j, :],
                                      start=True, stop=True)
                        wait("v_ready", n * 2 + (c + 1))
                        for j in range(J):
                            last = pe.matmul(ps_Z[:, 1, j * P:(j + 1) * P], k_decay[r, slot, j * P:(j + 1) * P],
                                             v_new[r, j * P:(j + 1) * P], start=True, stop=True)
                        last.then_inc(s["state_done"], 1)
                        if c == 1:
                            ahead(turn_L, *tile)
                        last = intra(c)
                    last.then_inc(s["out_done"], 1)
                else:
                    pe.wait_ge(s["s_state_loaded"], 32)
                    for b in range(DEC_B):
                        for j in range(J):
                            last = pe.matmul(ps_Z[:, 0, j * P:(j + 1) * P], s_wT[:, b, j, :], s_state[:, b, j, :],
                                             start=False, stop=(b == DEC_B - 1), skip_group_check=True)
                    last.then_inc(s["v_done"], 2)
                    for j in range(J):
                        for b in range(DEC_B):
                            pe.matmul(ps_kv[:, 0, j * P:(j + 1) * P], s_qT[:, b, j, :], s_state[:, b, j, :],
                                      start=(b == 0), stop=(b == DEC_B - 1))
                    pe.wait_ge(s["v_ready"], n * 2 + 2)
                    intra(0)
                    intra(1).then_inc(s["out_done"], 1)
                    pe.wait_ge(s["s_k_decay_ready"], 1)
                    for b in range(DEC_B):
                        if b >= 2:
                            pe.wait_ge(s["state_ready"], 1 + 2 * TILES + b - 1)
                        for j in range(J):
                            last = pe.matmul((ps_Z[:, 1] if b % 2 else ps_Y[:, 0])[:, j * P:(j + 1) * P],
                                             s_k_decay[:, b, j * P:(j + 1) * P], v_new[:, j * P:(j + 1) * P],
                                             start=True, stop=True)
                        last.then_inc(s["state_done"], 1)
                    turn_out(n)

            first = (0, 0, 0, False)
            norms(*first)
            sums_and_kv(*first)
            products(*first)
            turn_L(*first)
            tiles(pe, body)

        @block.scalar
        def _(act):
            act.preload_act_table_set(LOG_EXP_TABLES)
            act.sem_inc(s["out_ss_ready"], 2)
            act.sem_inc(s["mix_ready"], 2)

            def softplus(n, slot, uses, sample):
                act.wait_ge(s["soft_in_ready"], n + 1)
                softplus_part(act, soft_in[:], soft_e[:]).then_inc(s["soft_ready"], 1)

            def norm_logs(n, slot, uses, sample):
                act.wait_ge(s["ss_done"], n + 2)
                act.activation(logs[:], ps_s[:, SS:SS + 2 * H], ACT.Ln, bias=eps[:, 0:1]).then_inc(s["logs_ready"], 1)

            def factors(n, slot, uses, sample):
                act.wait_ge(s["fac_log_ready"], n + 1)
                act.activation(decay[:, slot].rearrange("p b j -> p (b j)"), sums[:, 2 * H:], ACT.Exp)
                act.activation(fac[:, slot].rearrange("p k h -> p (k h)"), fac_log[:].rearrange("p k h -> p (k h)"),
                               ACT.Exp).then_inc(s["fac_ready"], 1)

            def weights(n, half):
                act.wait_ge(s[f"expo_ready{half}"], n + 1)
                for j in range(J):
                    w = wgt[:, half * J + j].rearrange("p a c -> p (a c)")
                    h = 2 * j + half
                    last = act.activation(w, w, ACT.Exp, bias=minus_gc[:, h:h + 1])
                last.then_inc(s[f"wgt_ready{half}"], 1)

            def norm_out(n):
                act.wait_ge(s["out_ss_ready"], n + 3)
                act.activation(out_r[:], out_ss[:], ACT.Ln, bias=eps[:, 0:1], scale=1.0 / HD)
                act.drain()
                act.activation(out_r[:], out_r[:], ACT.Exp, scale=-0.5).then_inc(s["out_r_ready"], 1)

            def copy_mix(n):
                act.wait_ge(s["outT_done"], n + 1)
                act.wait_ge(mix_stored, n * 16 + 16)
                act.activation(mix[:].rearrange("p j t -> p (j t)"), ps_A[:, 0, 0:W], ACT.Identity
                               ).then_inc(s["mix_ready"], 1)

            def body(n, slot, uses, follows):
                tile = (n, slot, uses, follows)
                first = isinstance(n, int) and n == 0
                ahead(softplus, *tile)
                ahead(norm_logs, *tile)
                if not first:
                    norm_out(n - 1)
                ahead(factors, *tile)
                if not first:
                    copy_mix(n - 1)
                act.wait_ge(s["wT_done"], n + 1)
                if follows is None:
                    for b in range(DEC_B):
                        t = slice(b * DEC_T, (b + 1) * DEC_T)
                        c, b_t = b // 4, slice(b % 4 * DEC_T, (b % 4 + 1) * DEC_T)
                        last = act.activation(s_wT[:, b, :, t], ps_Y[:, c, 0:J * C].rearrange(
                            "p (j t) -> p j t", j=J)[:, :, b_t], ACT.Identity)
                else:
                    last = act.activation(wT[:].rearrange("p j (c t) -> p c j t", c=2),
                                          ps_Y[:, :, 0:J * C].rearrange("p c (j t) -> p c j t", j=J), ACT.Identity)
                last.then_inc(s["wT_ready"], 1)
                for c in range(2):
                    r = slice(c * C, (c + 1) * C)
                    if follows is not None:
                        weights(n + 1, c)
                    act.wait_ge(s["v_done"], n * 2 + (c + 1))
                    act.activation(v_new[r], ps_Z[r, 0, 0:W], ACT.Identity).then_inc(s["v_ready"], 1)
            act.wait_ge(s["masks_ready"], 1)
            act.wait_ge(s["rows_loaded"], 48)
            act.activation(a_log[:], a_log[:], ACT.Exp).then_inc(s["a_log_exp"], 1)
            first = (0, 0, 0, False)
            softplus(*first)
            norm_logs(*first)
            factors(*first)
            weights(0, 0)
            weights(0, 1)
            tiles(act, body)
            norm_out(TILES)
            copy_mix(TILES)

        @block.vector
        def _(dve):
            for t in (s_state, s_wT, s_qT):
                last = dve.memset(t[:], 0.0)
            last.then_inc(s["blank_ready"], 1)
            dve.wait_ge(s["rows_loaded"], 48)
            dve.wait_ge(s["masks_ready"], 1)
            dve.memset(sums[:], 0.0).then_inc(s["state_ready"], 1)

            def wide(col, d=C):
                return col.unsqueeze(2).to_broadcast([P, col.shape[1], d])

            def decays(n, slot, uses, sample):
                kind, seqs = int(sample), DEC_B if sample else 2
                dve.wait_ge(s["soft_ready"], n + 1)
                dve.scalar_tensor_tensor(soft[:], soft_in[:], 0.0, soft_e[:], ALU.max, ALU.add)
                dve.drain()
                dve.tensor_tensor(g[:], soft[:, GATE[1]], a_log[:], ALU.mult)
                dve.drain()
                for hh in range(2):
                    last = dve.tensor_tensor(g_seq[:, hh, 0:seqs],
                                             g[:].rearrange("p (j a) -> p a j", a=2)[:, hh].unsqueeze(1).to_broadcast(
                                                 [P, seqs, J]),
                                             in_seq[:, kind, 0:seqs].unsqueeze(2).to_broadcast([P, seqs, J]), ALU.mult)
                last.then_inc(s["g_ready"], 1)

            def factor_logs(n, slot, uses, sample):
                seqs = DEC_B if sample else 2
                dve.wait_ge(s["logs_ready"], n + 1)
                dve.tensor_scalar(logs[:, GATE[0]], logs[:, GATE[0]], -0.5, float(-0.5 * np.log(HD)), ALU.mult, ALU.add)
                dve.tensor_scalar(logs[:, GATE[1]], logs[:, GATE[1]], -0.5, None, ALU.mult)
                dve.tensor_scalar(fac_log[:, BETA], soft[:, GATE[0]], -1.0, None, ALU.mult)
                dve.wait_ge(s["sums_done"], n + 1)
                dve.tensor_copy(sums[:, 0:2 * H + seqs * J], ps_s[:, GC:GC + 2 * H + seqs * J])
                dve.drain()
                gc, whole = sums[:, GATE[0]], sums[:, GATE[1]]
                dve.tensor_tensor(fac_log[:, QG], gc, logs[:, GATE[0]], ALU.add)
                dve.tensor_tensor(fac_log[:, KBE], gc, logs[:, GATE[1]], ALU.add)
                dve.tensor_tensor(minus_gc[:], logs[:, GATE[1]], gc, ALU.subtract)
                dve.drain()
                dve.tensor_tensor(fac_log[:, KBE], fac_log[:, KBE], fac_log[:, BETA], ALU.add)
                dve.tensor_tensor(fac_log[:, KD], minus_gc[:], whole, ALU.add).then_inc(s["fac_log_ready"], 1)
                dve.drain()
                for half in range(2):
                    for a, f in enumerate((QG, KBE)):
                        row = fac_log[:, f].rearrange("p (j a) -> p a j", a=2)[:, half]
                        last = dve.tensor_tensor(diag[:, halves[half], a, :],
                                                 ident[:].unsqueeze(1).to_broadcast([P, HH, C]), wide(row), ALU.mult)
                last.then_inc(s["diag_ready"], 1)

            def scale_kv(n, slot, uses, sample):
                dve.wait_ge(s["fac_ready"], n + 1)
                dve.wait_ge(s["kv_done"], n + 1)
                k_rows, v_rows = (by_head(ps_kv[:, f, 0:W]) for f in range(2))
                factor = lambda f: wide(fac[:, slot, f], HD)
                dve.tensor_tensor(by_head(v_beta[:, slot]), v_rows, factor(BETA), ALU.mult)
                dve.scalar_tensor_tensor(by_head(k_beta[:, slot]), k_rows, -1.0, factor(KBE), ALU.mult, ALU.mult)
                dve.tensor_tensor(by_head(k_decay[:, slot]), k_rows, factor(KD), ALU.mult
                                  ).then_inc(s["kv_ready"], 1)
                if sample:
                    dve.drain()
                    for b in range(DEC_B):
                        last = dve.tensor_scalar(s_k_decay[:, b], k_decay[:, slot], in_seq[:, 1, b:b + 1], None, ALU.mult)
                    last.then_inc(s["s_k_decay_ready"], 1)

            def exponents(n, slot, uses, sample):
                for half in range(2):
                    dve.wait_ge(s[f"G_done{half}"], n + 1)
                    dve.tensor_tensor(wgt[:, halves[half]].rearrange("p h a c -> p h (a c)"),
                                      ps_kv[:, half, 0:HH * 2 * C].rearrange("p (h x) -> p h x", h=HH),
                                      expo_mask[:, int(sample)].rearrange("p a c -> p (a c)").unsqueeze(1).to_broadcast(
                                          [P, HH, 2 * C]), ALU.add).then_inc(s[f"expo_ready{half}"], 1)

            def matrices(n, slot, uses, sample):
                for half in range(2):
                    dve.wait_ge(s[f"wgt_ready{half}"], n + 1)
                    dve.wait_ge(s["qk_done"], n + 1)
                    dve.tensor_tensor(flat(mats[:, slot, halves[half]]), flat(wgt[:, halves[half]]),
                                      ps_A[:, half, 0:HH * 2 * C], ALU.mult).then_inc(s[f"mats_ready{half}"], 1)

            def first_inverse(n, slot, uses, sample):
                for half in range(2):
                    hs = halves[half]
                    rows_h = lambda m: m.unsqueeze(1).to_broadcast([P, HH, C])
                    dve.wait_ge(s[f"Y_done{half}"], n * LEVELS + 1)
                    dve.scalar_tensor_tensor(X[:, hs, 1, :], mats[:, slot, hs, 1, :], -1.0, rows_h(level_1T[:]),
                                             ALU.mult, ALU.mult)
                    dve.scalar_tensor_tensor(X[:, hs, 0, :], ps_A[:, half, 0:HH * C].rearrange("p (h c) -> p h c", h=HH),
                                             -1.0, rows_h(level[:, 0]), ALU.mult, ALU.mult)
                    dve.drain()
                    x = X[:, hs].rearrange("p h a c -> p (h a) c")
                    dve.tensor_tensor(x, x, ident[:].unsqueeze(1).to_broadcast([P, 2 * HH, C]), ALU.add
                                      ).then_inc(s[f"X_ready{half}"], 1)

            def output(n, slot):
                dve.wait_ge(s["out_done"], n + 3)
                dve.tensor_tensor(by_head(out[:]), by_head(ps_kv[:, 0, 0:W]), wide(fac[:, slot, QG], HD), ALU.mult)
                dve.drain()
                dve.tensor_tensor(out[:], out[:], ps_kv[:, 1, 0:W], ALU.add)
                dve.drain()
                dve.tensor_tensor(out_sq[:], out[:], out[:], ALU.mult)
                dve.drain()
                dve.tensor_reduce(out_ss[:], by_head(out_sq[:]), AX.X, ALU.add).then_inc(s["out_ss_ready"], 1)

            def gated_output(n, slot):
                dve.wait_ge(s["gate_ready"], n + 1)
                dve.tensor_tensor(out[:], out[:], gate[:, slot], ALU.mult)
                dve.drain()
                dve.wait_ge(s["out_r_ready"], n + 1)
                dve.tensor_tensor(by_head(out[:]), by_head(out[:]), wide(out_r[:], HD), ALU.mult
                                  ).then_inc(s["out_ready"], 1)

            def fade(s_new, s_old, factor):
                dve.tensor_tensor(s_new.rearrange("p b j v -> p (b j) v"), s_old.rearrange("p b j v -> p (b j) v"),
                                  factor.unsqueeze(2).to_broadcast([P, factor.shape[1], P]), ALU.mult)

            def body(n, slot, uses, follows):
                tile = (n, slot, uses, follows)
                sample = follows is None
                first = isinstance(n, int) and n == 0
                levels = S_LEVELS if sample else LEVELS
                for l in range(1, levels):
                    for half in range(2):
                        dve.wait_ge(s[f"Y_done{half}"], n * LEVELS + (l + 1))
                        dve.tensor_tensor(Y[:, halves[half]], ps_Y[:, half, 0:HH * C].rearrange("p (h c) -> p h c", h=HH),
                                          level[:, l].unsqueeze(1).to_broadcast([P, HH, C]), ALU.mult
                                          ).then_inc(s[f"Y_ready{half}"], 1)
                    for half in range(2):
                        dve.wait_ge(s[f"Z_done{half}"], n * (LEVELS - 1) + l)
                        if l < levels - 1:
                            x = flat(X[:, halves[half]])
                            z = ps_Z[:, half, 0:HH * 2 * C]
                        else:
                            x = X[:, halves[half], 1, :]
                            z = ps_Z[:, half, 0:HH * 2 * C].rearrange("p (h a c) -> p h a c", h=HH, a=2)[:, :, 1, :]
                        dve.tensor_tensor(x, x, z, ALU.subtract).then_inc(s[f"X_ready{half}"], 1)
                    if l == 1:
                        ahead(decays, *tile)
                        if not first:
                            output(n - 1, 1 - slot)
                    if l == 2:
                        ahead(factor_logs, *tile)
                        if not first:
                            gated_output(n - 1, 1 - slot)
                    if l == 3:
                        ahead(scale_kv, *tile)
                if not sample:
                    ahead(exponents, *tile)
                    for c in range(2):
                        fade(faded[:].unsqueeze(1), state[:].unsqueeze(1), decay[:, slot, c])
                        dve.drain()
                        dve.wait_ge(s["state_done"], n * 2 + (c + 1))
                        for hh in range(2):
                            r = slice(hh * HD, (hh + 1) * HD)
                            last = dve.tensor_tensor(state[r, :, r], faded[r, :, r],
                                                     ps_Z[r, 1, 0:W].rearrange("p (j v) -> p j v", j=J)[:, :, r], ALU.add)
                        last.then_inc(s["state_ready"], 1)
                        if c == 0:
                            ahead(matrices, *tile)
                        dve.drain()
                    ahead(first_inverse, *tile)
                else:
                    dve.wait_ge(s["s_state_loaded"], 32)
                    fade(s_faded[:], s_state[:], decay[:, slot].rearrange("p b j -> p (b j)"))
                    dve.drain()
                    output(n, slot)
                    gated_output(n, slot)
                    for b in range(DEC_B):
                        dve.wait_ge(s["state_done"], 2 * TILES + b + 1)
                        for hh in range(2):
                            r = slice(hh * HD, (hh + 1) * HD)
                            last = dve.tensor_tensor(s_state[r, b, :, r], s_faded[r, b, :, r],
                                                     (ps_Z[r, 1] if b % 2 else ps_Y[r, 0])[:, 0:W].rearrange(
                                                         "p (j v) -> p j v", j=J)[:, :, r], ALU.add)
                        last.then_inc(s["state_ready"], 1)
            dve.wait_ge(s["a_log_exp"], 1)
            dve.tensor_scalar(a_log[:], a_log[:], -1.0, None, ALU.mult)
            dve.drain()
            start = (0, 0, 0, False)
            decays(*start)
            factor_logs(*start)
            scale_kv(*start)
            exponents(*start)
            matrices(*start)
            first_inverse(*start)
            tiles(dve, body)


def scratch(nc, kind="Internal"):
    shapes = {"x0": [TOKENS, D], "convT": [CONV_CHUNKS, P, TOKENS], "qkT": [QKT_N, P, TOKENS],
              "av": [TOKENS, P], "zba": [TOKENS, ZBA_W], "cv": [TOKENS, C_HEADS * HD],
              "mixT": [DC, P, TOKENS], "x1": [TOKENS, D], "h2T": [DC, P, TOKENS], "h2T_low": [DC, P, TOKENS]}
    return {n: nc.dram_tensor(f"scratch_{n}", s, F32, kind=kind).ap() for n, s in shapes.items()}


def constants(nc, ctx):
    shapes = {"ident": [P, P], "ones": [P, P], "later": [P, P], "upto": [P, P], "before": [P, P],
              "sel": [N_COND, 2, P], "modT": [P, 4, DC, N_COND], "gates": [P, 2, 2, D]}
    return {n: ctx.enter_context(nc.sbuf_tensor(f"const_{n}", s, F32)) for n, s in shapes.items()}


def program(nc, IN, OUT, S):
    with ExitStack() as ctx:
        K = constants(nc, ctx)
        build_constants(nc, K)
        stage_modulation(nc, K, IN)
        stage_projection(nc, K, IN, OUT, S)
        with ExitStack() as masks:
            M = delta_masks(nc, masks)
            stage_window(nc, K, M, IN, OUT, S)
            stage_delta(nc, K, M, IN, OUT, S)
        stage_stick(nc, K, IN, S)
        stage_stick_samples(nc, K, IN, S)
        stage_mix_out(nc, K, IN, S)
        stage_ffn(nc, K, IN, OUT, S)


def output_shapes():
    shapes = {"y_prompt": (1, SEQ, D), "y_sample": (DEC_B, DEC_T, D)}
    for who, b, t in (("p", 1, SEQ), ("s", DEC_B, DEC_T)):
        shapes |= {f"{who}_a_k": (1, b, WINDOW, A_KV, HD), f"{who}_a_v": (1, b, WINDOW, A_KV, HD),
                   f"{who}_b_conv": (1, b, B_CONV - 1, CONV_CH), f"{who}_b_ssm": (1, b, B_HEADS, HD, HD),
                   f"{who}_c_k": (1, b, t, C_HEADS, HD), f"{who}_c_v": (1, b, t, C_HEADS, HD),
                   f"{who}_ffn_conv": (1, b, FFN_CONV - 1, D_FF)}
    return shapes


def kernel(**inputs):
    import concourse.bacc as bacc
    from concourse.bass_utils import run_bass_kernel_spmd

    nc = bacc.Bacc("TRN2", target_bir_lowering=False, num_devices=1)
    arrays, ins = {}, {}
    for name, value in inputs.items():
        a = np.ascontiguousarray(value)
        if a.ndim == 1:
            a = a.reshape(1, -1)
        arrays[f"in_{name}"] = a
        ins[name] = nc.dram_tensor(f"in_{name}", a.shape, F32, kind="ExternalInput").ap()
    outs = {name: nc.dram_tensor(f"out_{name}", shape, F32, kind="ExternalOutput").ap()
            for name, shape in output_shapes().items()}
    program(nc, ins, outs, scratch(nc))
    r = run_bass_kernel_spmd(nc, [arrays], core_ids=[0])
    return tuple(r.results[0][f"out_{name}"] for name in outs)
```
